# Optimizing a Trainium2 kernel written in Bass

```python
import jax, jax.numpy as jnp
from jax import lax
import numpy as np

D_MODEL = 1024
BATCH = 1
SEQ = 256
DEPTH = 1
DEC_BATCH = 1
DEC_SEQ = 256
PAST_LEN = 128

A_HEADS = 8
A_KV_HEADS = 2
A_GROUP = A_HEADS // A_KV_HEADS
A_HEAD_DIM = 64
A_WIDTH = A_HEADS * A_HEAD_DIM
A_KV_WIDTH = A_KV_HEADS * A_HEAD_DIM
WINDOW = 128
BLOCK = 128
ROPE_DIM = A_HEAD_DIM // 4
ROPE_THETA = 500000.0

M_HEADS = 4
M_HEAD_DIM = 128
M_WIDTH = M_HEADS * M_HEAD_DIM
M_CHUNK = 128
CONV_W = 3

OFF_AQ = 0
OFF_AK = OFF_AQ + A_WIDTH
OFF_AV = OFF_AK + A_KV_WIDTH
OFF_MQ = OFF_AV + A_KV_WIDTH
OFF_MK = OFF_MQ + M_WIDTH
OFF_MV = OFF_MK + M_WIDTH
OFF_MO = OFF_MV + M_WIDTH
OFF_MG = OFF_MO + M_WIDTH
OFF_BG = OFF_MG + 4 * M_HEADS
IN_TOTAL = OFF_BG + 2 * D_MODEL

N_GROUPS = 4
EXPERTS_PER_GROUP = 4
N_EXPERTS = N_GROUPS * EXPERTS_PER_GROUP
TOP_K = 2
D_EXPERT = 512

EPS = 1e-6
NEG_BIG = -1e30
F32 = jnp.float32

kernel_name = "hybrid_bidir_swa_mlstm_hmoe_encoder"

def rms_norm(x, g):
    xf = x.astype(F32)
    y = xf * lax.rsqrt(jnp.mean(xf * xf, axis=-1, keepdims=True) + EPS)
    return (y * g.astype(F32)).astype(x.dtype)

def partial_rope(x, pos):
    half = ROPE_DIM // 2
    inv_freq = 1.0 / (ROPE_THETA ** (jnp.arange(half, dtype=F32) * 2.0 / ROPE_DIM))
    ang = pos[:, None] * inv_freq[None, :]
    cos = jnp.cos(ang)[None, :, None, :]
    sin = jnp.sin(ang)[None, :, None, :]
    xr = x[..., :ROPE_DIM].astype(F32)
    x1, x2 = xr[..., :half], xr[..., half:]
    rot = jnp.concatenate([x1 * cos - x2 * sin, x2 * cos + x1 * sin], axis=-1).astype(x.dtype)
    return jnp.concatenate([rot, x[..., ROPE_DIM:]], axis=-1)

def windowed_gqa(q, k, v, sink):
    B, S = q.shape[0], q.shape[1]
    nb = S // BLOCK
    qb = q.reshape(B, nb, BLOCK, A_KV_HEADS, A_GROUP, A_HEAD_DIM)

    def band(t):
        tp = jnp.pad(t, ((0, 0), (BLOCK, BLOCK), (0, 0), (0, 0)))
        tb = tp.reshape(B, nb + 2, BLOCK, A_KV_HEADS, A_HEAD_DIM)
        return jnp.concatenate([tb[:, :-2], tb[:, 1:-1], tb[:, 2:]], axis=2)

    kb, vb = band(k), band(v)
    s = jnp.einsum('bnqhgd,bnkhd->bnhgqk', qb, kb).astype(F32) * (A_HEAD_DIM ** -0.5)
    blk = jnp.arange(nb)[:, None]
    qpos = blk * BLOCK + jnp.arange(BLOCK)[None, :]
    kpos = (blk - 1) * BLOCK + jnp.arange(3 * BLOCK)[None, :]
    rel = kpos[:, None, :] - qpos[:, :, None]
    valid = (jnp.abs(rel) <= WINDOW) & (kpos[:, None, :] >= 0) & (kpos[:, None, :] < S)
    s = jnp.where(valid[None, :, None, None], s, NEG_BIG)
    sk = sink.astype(F32).reshape(1, 1, A_KV_HEADS, A_GROUP, 1, 1)
    m = jnp.maximum(jnp.max(s, axis=-1, keepdims=True), sk)
    p = jnp.exp(s - m)
    p = p / (jnp.sum(p, axis=-1, keepdims=True) + jnp.exp(sk - m))
    o = jnp.einsum('bnhgqk,bnkhd->bnqhgd', p.astype(v.dtype), vb)
    return o.reshape(B, S, A_WIDTH)

def centred_dwconv(u, w):
    S = u.shape[1]
    pad = CONV_W // 2
    up = jnp.pad(u, ((0, 0), (pad, pad), (0, 0)))
    out = up[:, 0:S] * w[0]
    for j in range(1, CONV_W):
        out = out + up[:, j:j + S] * w[j]
    return out

def mlstm_direction(q, k, v, i_pre, logf):
    B, H, S, dh = q.shape
    nc = S // M_CHUNK

    def to_chunks(t):
        return jnp.moveaxis(t.reshape(B, H, nc, M_CHUNK, *t.shape[3:]), 2, 0)

    xs = tuple(to_chunks(t) for t in (q, k, v, i_pre, logf))
    lower = jnp.tril(jnp.ones((M_CHUNK, M_CHUNK), dtype=bool))

    def step(carry, inp):
        C, n, m = carry
        qc, kc, vc, ic, fc = inp
        b = jnp.cumsum(fc, axis=-1)
        log_w = jnp.where(lower, b[..., :, None] - b[..., None, :] + ic[..., None, :], -jnp.inf)
        log_inter = b + m[..., None]
        m_t = jnp.maximum(log_inter, jnp.max(log_w, axis=-1))
        w_inter = jnp.exp(log_inter - m_t)
        a = jnp.einsum('bhtd,bhsd->bhts', qc, kc) * jnp.exp(log_w - m_t[..., None])
        num = w_inter[..., None] * jnp.einsum('bhtd,bhed->bhte', qc, C) + jnp.einsum('bhts,bhse->bhte', a, vc)
        den = w_inter * jnp.einsum('bhtd,bhd->bht', qc, n) + jnp.sum(a, axis=-1)
        h = num / jnp.maximum(jnp.abs(den), jnp.exp(-m_t))[..., None]
        b_last = b[..., -1]
        log_g = b_last[..., None] - b + ic
        m_new = jnp.maximum(b_last + m, jnp.max(log_g, axis=-1))
        decay = jnp.exp(b_last + m - m_new)
        wk = jnp.exp(log_g - m_new[..., None])
        C_new = decay[..., None, None] * C + jnp.einsum('bhse,bhsd->bhed', wk[..., None] * vc, kc)
        n_new = decay[..., None] * n + jnp.einsum('bhs,bhsd->bhd', wk, kc)
        return (C_new, n_new, m_new), h

    init = (jnp.zeros((B, H, dh, dh), F32), jnp.zeros((B, H, dh), F32), jnp.zeros((B, H), F32))
    _, hs = lax.scan(step, init, xs)
    return jnp.moveaxis(hs, 0, 2).reshape(B, H, S, dh)

def hier_moe(h, rg_w, rg_b, re_w, re_b, w_gate, w_up, w_down):
    B, S, D = h.shape
    t = h.reshape(-1, D)
    g_logits = (t @ rg_w).astype(F32) + rg_b.astype(F32)
    g_prob = jax.nn.softmax(g_logits, axis=-1)
    grp = jnp.argmax(g_logits, axis=-1)
    p_grp = jnp.take_along_axis(g_prob, grp[:, None], axis=-1)
    e_logits = ((t @ re_w).astype(F32) + re_b.astype(F32)).reshape(-1, N_GROUPS, EXPERTS_PER_GROUP)
    e_in_grp = jnp.take_along_axis(e_logits, grp[:, None, None], axis=1)[:, 0]
    top_v, top_i = lax.top_k(e_in_grp, TOP_K)
    top_w = jax.nn.softmax(top_v, axis=-1) * p_grp
    eid = grp[:, None] * EXPERTS_PER_GROUP + top_i
    dense_w = jnp.sum(jax.nn.one_hot(eid, N_EXPERTS, dtype=F32) * top_w[..., None], axis=1).astype(t.dtype)
    out = jnp.zeros_like(t)
    for e in range(N_EXPERTS):
        he = jax.nn.silu(t @ w_gate[e]) * (t @ w_up[e])
        out = out + dense_w[:, e:e + 1] * (he @ w_down[e])
    return out.reshape(B, S, D)

def encoder_layer(x, c, ada_w, ada_b, norm1_g, w_in, conv_w, m_gate_b, attn_sink, head_norm_g,
                  w_up_attn, w_up_mlstm, w_out, norm2_g, rg_w, rg_b, re_w, re_b, w_gate, w_up, w_down):
    B, S, _ = x.shape
    mod = jax.nn.silu(c) @ ada_w + ada_b
    sh1, sc1, g1, sh2, sc2, g2 = jnp.split(mod[:, None, :], 6, axis=-1)

    h = rms_norm(x, norm1_g) * (1 + sc1) + sh1
    proj = h @ w_in
    pos = jnp.arange(S, dtype=F32)

    q = partial_rope(proj[..., OFF_AQ:OFF_AK].reshape(B, S, A_HEADS, A_HEAD_DIM), pos)
    k = partial_rope(proj[..., OFF_AK:OFF_AV].reshape(B, S, A_KV_HEADS, A_HEAD_DIM), pos)
    v = proj[..., OFF_AV:OFF_MQ].reshape(B, S, A_KV_HEADS, A_HEAD_DIM)
    attn = windowed_gqa(q, k, v, attn_sink)

    qk = jax.nn.silu(centred_dwconv(proj[..., OFF_MQ:OFF_MV], conv_w))

    def heads(t):
        return t.reshape(B, S, M_HEADS, M_HEAD_DIM).transpose(0, 2, 1, 3).astype(F32)

    mq = heads(qk[..., :M_WIDTH])
    mk = heads(qk[..., M_WIDTH:]) * (M_HEAD_DIM ** -0.5)
    mv = heads(proj[..., OFF_MV:OFF_MO])
    o_gate = jax.nn.sigmoid(proj[..., OFF_MO:OFF_MG])
    gates = (proj[..., OFF_MG:OFF_BG].astype(F32) + m_gate_b.astype(F32)).transpose(0, 2, 1)
    i_fw, f_fw, i_bw, f_bw = jnp.split(gates, 4, axis=1)
    h_fw = mlstm_direction(mq, mk, mv, i_fw, jax.nn.log_sigmoid(f_fw))
    fl = lambda t: jnp.flip(t, axis=2)
    h_bw = fl(mlstm_direction(fl(mq), fl(mk), fl(mv), fl(i_bw), fl(jax.nn.log_sigmoid(f_bw))))
    hm = (h_fw + h_bw).transpose(0, 2, 1, 3)
    hm = rms_norm(hm, head_norm_g.reshape(M_HEADS, M_HEAD_DIM)).reshape(B, S, M_WIDTH).astype(x.dtype)
    mlstm_out = o_gate * hm

    bg = jax.nn.sigmoid(proj[..., OFF_BG:])
    merged = bg[..., :D_MODEL] * (attn @ w_up_attn) + bg[..., D_MODEL:] * (mlstm_out @ w_up_mlstm)
    x = x + g1 * (merged @ w_out)

    h2 = rms_norm(x, norm2_g) * (1 + sc2) + sh2
    x = x + g2 * hier_moe(h2, rg_w, rg_b, re_w, re_b, w_gate, w_up, w_down)
    return x

def setup_inputs(seed: int = 0) -> dict:
    key = jax.random.key(seed)
    ks = jax.random.split(key, 32)
    D = D_MODEL

    def nrm(k, shape, scale):
        return jax.random.normal(k, shape, F32) * scale

    gate_b = jnp.concatenate([
        nrm(ks[9], (DEPTH, M_HEADS), 0.1),
        3.0 + 3.0 * jax.random.uniform(ks[10], (DEPTH, M_HEADS), F32),
        nrm(ks[11], (DEPTH, M_HEADS), 0.1),
        3.0 + 3.0 * jax.random.uniform(ks[12], (DEPTH, M_HEADS), F32),
    ], axis=-1)
    return {
        'x_prompt': nrm(ks[0], (BATCH, SEQ, D), 1.0),
        'x_sample': nrm(ks[1], (DEC_BATCH, DEC_SEQ, D), 1.0),
        'c_prompt': nrm(ks[2], (BATCH, D), 1.0),
        'c_sample': nrm(ks[3], (DEC_BATCH, D), 1.0),
        'ada_w': nrm(ks[4], (DEPTH, D, 6 * D), 0.5 * D ** -0.5),
        'ada_b': nrm(ks[5], (DEPTH, 6 * D), 0.02),
        'norm1_g': 1.0 + nrm(ks[6], (DEPTH, D), 0.02),
        'w_in': nrm(ks[7], (DEPTH, D, IN_TOTAL), D ** -0.5),
        'conv_w': nrm(ks[8], (DEPTH, CONV_W, 2 * M_WIDTH), CONV_W ** -0.5),
        'm_gate_b': gate_b,
        'attn_sink': nrm(ks[13], (DEPTH, A_HEADS), 0.5),
        'head_norm_g': 1.0 + nrm(ks[14], (DEPTH, M_WIDTH), 0.02),
        'w_up_attn': nrm(ks[15], (DEPTH, A_WIDTH, D), A_WIDTH ** -0.5),
        'w_up_mlstm': nrm(ks[16], (DEPTH, M_WIDTH, D), M_WIDTH ** -0.5),
        'w_out': nrm(ks[17], (DEPTH, D, D), D ** -0.5),
        'norm2_g': 1.0 + nrm(ks[18], (DEPTH, D), 0.02),
        'rg_w': nrm(ks[19], (DEPTH, D, N_GROUPS), D ** -0.5),
        'rg_b': nrm(ks[20], (DEPTH, N_GROUPS), 0.01),
        're_w': nrm(ks[21], (DEPTH, D, N_EXPERTS), D ** -0.5),
        're_b': nrm(ks[22], (DEPTH, N_EXPERTS), 0.01),
        'w_gate': nrm(ks[23], (DEPTH, N_EXPERTS, D, D_EXPERT), D ** -0.5),
        'w_up': nrm(ks[24], (DEPTH, N_EXPERTS, D, D_EXPERT), D ** -0.5),
        'w_down': nrm(ks[25], (DEPTH, N_EXPERTS, D_EXPERT, D), D_EXPERT ** -0.5),
        'final_norm_g': 1.0 + nrm(ks[26], (D,), 0.02),
    }

def reference(x_prompt, x_sample, c_prompt, c_sample, ada_w, ada_b, norm1_g, w_in, conv_w, m_gate_b,
              attn_sink, head_norm_g, w_up_attn, w_up_mlstm, w_out, norm2_g, rg_w, rg_b, re_w, re_b,
              w_gate, w_up, w_down, final_norm_g):
    layer_params = (ada_w, ada_b, norm1_g, w_in, conv_w, m_gate_b, attn_sink, head_norm_g,
                    w_up_attn, w_up_mlstm, w_out, norm2_g, rg_w, rg_b, re_w, re_b, w_gate, w_up, w_down)

    def trunk(x, c):
        for l in range(DEPTH):
            x = encoder_layer(x, c, *[p[l] for p in layer_params])
        return rms_norm(x, final_norm_g)

    y_prompt = trunk(x_prompt, c_prompt)
    y_sample = trunk(x_sample, c_sample)
    return (y_prompt, y_sample)


_drawn_inputs = setup_inputs


def setup_inputs(seed=0):
    import zlib

    import numpy as np

    out = dict(_drawn_inputs(seed))
    spreads = {}
    factors = {'ada_b': 3.159,
     'norm1_g': 7.478,
     'attn_sink': 8.0,
     'head_norm_g': 8.0,
     'norm2_g': 6.038,
     'rg_b': 53.536,
     're_b': 8.0,
     'final_norm_g': 7.662}
    for name, (base, spread) in spreads.items():
        noise = np.random.default_rng([zlib.crc32(name.encode()), seed]).standard_normal(out[name].shape)
        drawn = base * np.exp(spread * noise) if base else spread * noise
        out[name] = __import__('jax').numpy.asarray(drawn.astype(out[name].dtype))
    for name, factor in factors.items():
        out[name] = (out[name] * factor).astype(out[name].dtype)
    return out
```

```python
from contextlib import ExitStack

import numpy as np
import concourse.bass as bass
from concourse import mybir

F32 = mybir.dt.float32
I32 = mybir.dt.int32
U32 = mybir.dt.uint32
ALU = mybir.AluOpType
ACT = mybir.ActivationFunctionType
AX = mybir.AxisListType

P = 128
D = 1024
KD = D // P
REQS, SEQ = 2, 256
TOK = REQS * SEQ
TT = TOK // P
TPR = SEQ // P
COLS = 512

A_HEADS, A_KV, A_HD = 8, 2, 64
PAIRS = A_HEADS // A_KV
ROPE_DIM, ROPE_THETA = 16, 500000.0
M_HEADS, M_HD = 4, 128
KM = M_HEADS
VW = M_HD + 1

OFF_AQ, OFF_AK, OFF_MQ, OFF_MK = 0, 512, 768, 1280
OFF_MV, OFF_MO, OFF_MG, OFF_BG = 1792, 2304, 2816, 2832

N_GRP, PER_GRP = 4, 4
N_EXP = N_GRP * PER_GRP
D_EXP = 512
KF = D_EXP // P
MOE_TILES = (2 * TOK + N_EXP * (P - 1)) // P
EPS = 1e-6
BIG = 1e30

FRONT_SLOTS = 3
SCRATCH = 4096

EARLY = {"ident": (0, 128), "maskL": (128, 256), "maskU": (384, 256), "cos": (640, 256),
         "sin": (896, 256), "perm": (1152, 128)}
EARLY_W = 1280
LATE = {"tri": (0, 128), "ones": (128, 128), "iota": (256, 128), "iota4": (384, 4), "tokid": (388, 4)}
LATE_W = 392

BLOCKS = (["ada0", "ada1", "ada2", "ada3", "kvg", "aq", "mq", "mk", "mv", "mo"]
          + ["bg0", "bg1", "bg2", "bg3", "ada4", "ada5", "upa", "upm", "ada6", "ada7", "ada8", "ada9"]
          + ["wo0", "wo1", "ada10", "ada11"])


def list_groups():
    g = [("cT", "v"), ("gainT", "v"), ("ada0", "v"), ("ada1", "v"), ("modT0", "v"), ("ada2", "v"),
         ("modT1", "v"), ("ada3", "v"), ("modT2", "v"), ("modT3", "v")]
    g += [(f"xT{k}", "vs"[k % 2]) for k in range(KD)]
    g += [("gates", "v"), ("raw0", "s"), ("av", "s")]
    for n in range(1, 5):
        g += [(f"raw{n}", "s"), (f"swap{n - 1}", "v")]
    g += [("conv0", "v"), ("swap4", "v")] + [(f"conv{c}", "v") for c in range(1, 8)]
    g += [(f"mv{t}", "s") for t in range(TT)] + [("gateT", "s")] + [(f"mo{t}", "s") for t in range(TT)]
    for b in range(TT):
        bg = [(f"bg{4 * b + n}", "s") for n in range(4)]
        g += [(f"score{b}.{j}", "v") for j in range(PAIRS)]
        g += [(f"mrow{2 * b}", "v"), (f"qk{2 * b}", "v"), bg[0], bg[1]]
        g += [(f"pT{b}.{n}", "vs"[n % 2]) for n in range(4)]
        g += [(f"num{2 * b}.0", "v"), (f"num{2 * b}.1", "v")]
        g += [(f"mrow{2 * b + 1}", "v"), (f"qk{2 * b + 1}", "v"), bg[2], (f"pv{b}", "v")]
        g += [(f"num{2 * b + 1}.0", "v"), (f"num{2 * b + 1}.1", "v"), bg[3], (f"oT{b}", "s")]
    g += ada_groups(4, "s")
    g += [(f"mT{t}", "s") for t in range(TT)]
    g += [(f"upa{j}", "v") for j in range(KD)] + [(f"upm{j}", "v") for j in range(KD)]
    g += ada_groups(6, "s") + ada_groups(8, "v")
    g += [(f"wo{t}.{h}", "v") for h in range(2) for t in range(TT)]
    for t in range(TT):
        g += [(f"h2T{t}.0", "s"), (f"h2T{t}.1", "s"), (f"logit{t}", "v")]
    g += ada_groups(10, "s")
    g += [("rank", "v"), ("ids", "v")]
    return g


def ada_groups(b, empties):
    return ([(f"ada{b}", "v"), (f"ada{b + 1}", "v")]
            + [(f"spread{b + n}.{r}", empties) for n in range(2) for r in range(REQS)])


GROUPS = list_groups()
INDEX = {name: n for n, (name, _) in enumerate(GROUPS)}
BANKS = 8


def emptied_count(name):
    n = INDEX[name]
    return sum(1 for _, e in GROUPS[:n + 1] if e == GROUPS[n][1])


LAST_USE = {"kvg": "av", "aq": "raw4", "mq": "conv3", "mk": "conv7", "mv": "mv3", "mo": "mo3",
            "bg0": "bg3", "bg1": "bg7", "bg2": "bg11", "bg3": "bg15", "upa": "upa7", "upm": "upm7",
            "wo0": "wo3.0", "wo1": "wo3.1"}
LAST_USE.update({f"ada{b}": f"ada{b}" for b in range(12)})


def hybrid_layer(nc, x_prompt, x_sample, c_prompt, c_sample, ada_w, ada_b, norm1_g, w_in, conv_w,
                 m_gate_b, attn_sink, head_norm_g, w_up_attn, w_up_mlstm, w_out, norm2_g, rg_w,
                 rg_b, re_w, re_b, w_gate, w_up, w_down, final_norm_g, early_consts, late_consts,
                 y_prompt, y_sample):
    ctx = ExitStack()
    with ctx:
        def sb(name, shape, dt=F32):
            return ctx.enter_context(nc.sbuf_tensor(name, shape, dt))

        def sem(name):
            return ctx.enter_context(nc.semaphore(name))

        x_in = [x_prompt, x_sample]
        y_out = [y_prompt, y_sample]

        front_ring = sb("front_ring", [P, FRONT_SLOTS, 4096])
        slot3 = sb("slot3", [P, 4096])
        slots45 = sb("slots45", [P, 2, 4096])
        xbuf = sb("xbuf", [P, TT, D])
        hT = sb("hT", [P, KD, TOK])
        g1b = sb("g1b", [P, REQS, D])
        rot_v = sb("rot_v", [P, 3072])
        mqk = sb("mqk", [P, 8, TOK])
        mvb = sb("mvb", [P, TT, M_HEADS, VW])
        og = sb("og", [P, TT, COLS])
        pTb = sb("pTb", [P, 16, P])
        hm = sb("hm", [P, TT, COLS])
        oT = sb("oT", [P, KM, TOK])
        tmp = sb("tmp", [P, COLS])
        modrow = sb("modrow", [REQS, 2, COLS])
        early = sb("early", [P, EARLY_W])
        hng = sb("hng", [P, COLS])
        cT = sb("cT", [P, KD, REQS])
        gainT = sb("gainT", [P, 32])
        modT = sb("modT", [P, 4, 4, REQS])
        scale1 = sb("scale1", [P, KD, REQS])
        small = sb("small", [P, 64])
        sink = sb("sink", [P, A_HEADS])
        nsink = sb("nsink", [P, A_HEADS])
        stat = sb("stat", [P, 2, 8, A_HEADS])
        gateT = sb("gateT", [P, 2, 2, TT, M_HEADS])
        mstat = sb("mstat", [P, 2, 2, 2])
        gbias = sb("gbias", [M_HEADS, 4])
        router_w = sb("router_w", [P, KD, 20])
        router_b = sb("router_b", [P, 20])
        eps = sb("eps", [P, 1])

        psum = ctx.enter_context(nc.psum_tensor("psum", [P, BANKS, COLS], F32))
        h2_rows = nc.dram_tensor("h2_rows", [TOK, D], F32, kind="Internal").ap()
        y_rows = nc.dram_tensor("y_rows", [MOE_TILES * P, D], F32, kind="Internal").ap()

        ebuf = g1b[:, :, :].rearrange("p r d -> p (r d)")[:, 0:1536].rearrange(
            "p (b d n) -> p b d n", b=2, d=2)
        crow = hm[0:REQS, 0:2, :].rearrange("p a b -> p (a b)")
        biasrow = slot3[0:REQS, 3328:3840]
        gains = slot3[0:32, 3840:3968]
        def const(name):
            a, w = EARLY[name]
            return early[:, a:a + w]

        ident, perm = const("ident"), const("perm")
        rows = slot3[0:M_HEADS, 0:2048].rearrange("p (g t) -> p g t", g=4)
        rows_x = slot3[0:M_HEADS, 2048:3072].rearrange("p (g t) -> p g t", g=2)
        ones_row = slot3[0:M_HEADS, 3072:3328]
        bgate = slots45[:, :, :].rearrange("p s (c t) -> p (s c) t", t=TOK)
        probs = xbuf[:, :, :].rearrange("p (b a) n -> p b (a n)", b=2).rearrange(
            "p b (h k) -> p b h k", h=A_HEADS)
        rot = rot_v[:, 0:2560].rearrange("p (c t) -> p c t", c=5)
        av = rot_v[:, 2560:3072].rearrange("p (t f) -> p t f", t=TT)
        mT = rot_v[:, 0:2048].rearrange("p (k t) -> p k t", k=KM)
        pTflat = pTb[:, :, :].rearrange("p a b -> p (a b)")
        raw = [pTflat[:, n * 512:(n + 1) * 512] for n in range(2)]
        acc = [pTflat[:, 1024 + n * 512:1536 + n * 512] for n in range(2)]
        mqkf = mqk[:, :, :].rearrange("p a b -> p (a b)")
        scale2 = mqkf[:, 0:2048].rearrange("p (r d) -> p r d", r=REQS)
        shift2 = mqkf[:, 2048:4096].rearrange("p (r d) -> p r d", r=REQS)
        g2b = og[:, :, :].rearrange("p a b -> p (a b)").rearrange("p (r d) -> p r d", r=REQS)
        mvf = mvb[:, :, :, :].rearrange("p a b c -> p (a b c)")
        gain2 = mvf[:, 0:D]
        late = mvf[:, D:D + LATE_W]
        lc = {n: late[:, a:a + w] for n, (a, w) in LATE.items()}
        route = mvf[:, D + LATE_W:D + LATE_W + 640]
        h2 = pTflat.rearrange("p (b d) -> p b d", b=2)
        hmf = hm[:, :, :].rearrange("p a b -> p (a b)")
        h2T = hmf.rearrange("p (b k t) -> p b k t", b=2, k=KD)
        hTf = hT[:, :, :].rearrange("p a b -> p (a b)")
        xs = hTf[:, 0:2048].rearrange("p (b d) -> p b d", b=2)
        ybuf = hTf[:, 2048:4096].rearrange("p (b d) -> p b d", b=2)
        xsT = rot_v[:, 0:1024].rearrange("p (k t) -> p k t", k=KD)
        sg = rot_v[:, 1024:2048].rearrange("p (b f) -> p b f", b=2)
        oTf = oT[:, :, :].rearrange("p a b -> p (a b)")
        he = oTf[:, 0:1024].rearrange("p (b f) -> p b f", b=2)
        heT = oTf[:, 1024:1536].rearrange("p (k t) -> p k t", k=KF)
        fgain = g1b[:, 0, :]
        junk = g1b[:, 1, :]
        sqjunk = hTf[:, 0:1024]
        pair = [mqkf[:, n * D:(n + 1) * D] for n in range(4)]
        ids = sb("ids", [P, 24], U32)
        pos = sb("pos", [P, TT, 2], U32)
        topw = sb("topw", [P, TT, 2])
        tile_expert = sb("tile_expert", [1, 24], I32)

        hot_place = [pTflat[:, n * P:(n + 1) * P] for n in range(2 * TT)]
        hot_tile = [route[:, 256 + n * 24:280 + n * 24] for n in range(2 * TT)]

        moe_slot = [slot3[:, :], slots45[:, 0, :], front_ring[:, 1, :], slots45[:, 1, :],
                    front_ring[:, 2, :], front_ring[:, 0, :]]

        landed = [sem(f"landed{i}") for i in range(FRONT_SLOTS)]
        moe_landed = [sem(f"moe_landed{i}") for i in range(6)]
        x_landed = sem("x_landed")
        x_again = sem("x_again")
        small_landed = sem("small_landed")
        early_landed = sem("early_landed")
        late_landed = sem("late_landed")
        router_landed = sem("router_landed")
        fgain_landed = sem("fgain_landed")
        bias_landed = sem("bias_landed")
        psum_full = sem("psum_full")
        dve_emptied = sem("dve_emptied")
        act_emptied = sem("act_emptied")
        dve_chain = sem("dve_chain")
        act_chain = sem("act_chain")
        pool_chain = sem("pool_chain")
        c_ready = sem("c_ready")
        xsq_ready = sem("xsq_ready")
        xn_ready = sem("xn_ready")
        gpad_ready = sem("gpad_ready")
        conv_done = sem("conv_done")
        forget_abs = sem("forget_abs")
        forget_ln = sem("forget_ln")
        rows_ready = sem("rows_ready")
        ones_ready = sem("ones_ready")
        negmax_ready = sem("negmax_ready")
        probs_ready = sem("probs_ready")
        decay_ready = sem("decay_ready")
        hm_sq = sem("hm_sq")
        hm_root = sem("hm_root")
        hm_ready = sem("hm_ready")
        x1_root = sem("x1_root")
        h2_ready = sem("h2_ready")
        h2_stored = [sem(f"h2_stored{i}") for i in range(2)]
        gate_sum = sem("gate_sum")
        gate_exp = sem("gate_exp")
        onehots_ready = sem("onehots_ready")
        hot_slots_ready = sem("hot_slots_ready")
        tiles_ready = sem("tiles_ready")
        xs_landed = [sem(f"xs_landed{i}") for i in range(2)]
        xT_full = sem("xT_full")
        xT_act = sem("xT_act")
        xT_dve = sem("xT_dve")
        gate_full = sem("gate_full")
        up_full = sem("up_full")
        silu_done = sem("silu_done")
        he_ready = sem("he_ready")
        heT_full = sem("heT_full")
        heT_emptied = sem("heT_emptied")
        down_full = sem("down_full")
        y_act = sem("y_act")
        y_dve = sem("y_dve")
        y_stored = [sem(f"y_stored{i}") for i in range(2)]
        pair_landed = [sem(f"pair_landed{i}") for i in range(4)]
        x2_ready = sem("x2_ready")
        x2_root = sem("x2_root")
        y_ready = sem("y_ready")
        out_stored = sem("out_stored")

        per_block = {"kvg": 2, "aq": A_HEADS}
        slot_count, block_landed = [0] * FRONT_SLOTS, []
        for n, name in enumerate(BLOCKS):
            slot_count[n % FRONT_SLOTS] += 16 * per_block.get(name, 1)
            block_landed.append(slot_count[n % FRONT_SLOTS])

        def block_of(name):
            n = BLOCKS.index(name)
            return front_ring[:, n % FRONT_SLOTS, :]

        def wait_block(eng, name):
            n = BLOCKS.index(name)
            eng.wait_ge(landed[n % FRONT_SLOTS], block_landed[n])

        def bank(name, width=COLS):
            return psum[:, INDEX[name] % BANKS, 0:width]

        def wait_full(eng, name):
            eng.wait_ge(psum_full, INDEX[name] + 1)

        def wait_emptied(eng, name):
            eng.wait_ge(dve_emptied if GROUPS[INDEX[name]][1] == "v" else act_emptied,
                        emptied_count(name))

        def wait_bank(eng, name):
            if INDEX[name] >= BANKS:
                wait_emptied(eng, GROUPS[INDEX[name] - BANKS][0])

        def row_bcast(ap, n=P):
            return ap.rearrange("(a n) -> a n", a=1).to_broadcast([n, ap.shape[0]])

        block = ctx.enter_context(nc.Block())

        @block.sync
        def _(sp):
            for r in range(REQS):
                sp.dma_start(xbuf[:, 2 * r:2 * r + 2, :],
                             x_in[r][0].rearrange("(t p) d -> p t d", p=P)).then_inc(x_landed, 16)
            src = {"kvg": w_in[0, :, OFF_AK:OFF_AK + 256], "aq": w_in[0, :, OFF_AQ:OFF_AQ + COLS],
                   "mq": w_in[0, :, OFF_MQ:OFF_MQ + COLS], "mk": w_in[0, :, OFF_MK:OFF_MK + COLS],
                   "mv": w_in[0, :, OFF_MV:OFF_MV + COLS], "mo": w_in[0, :, OFF_MO:OFF_MO + COLS]}
            for b in range(4):
                src[f"bg{b}"] = w_in[0, :, OFF_BG + b * COLS:OFF_BG + (b + 1) * COLS]
            for b in range(12):
                src[f"ada{b}"] = ada_w[0, :, b * COLS:(b + 1) * COLS]
            for h in range(2):
                src[f"wo{h}"] = w_out[0, :, h * COLS:(h + 1) * COLS]
            for n, name in enumerate(BLOCKS):
                if n >= FRONT_SLOTS:
                    wait_full(sp, LAST_USE[BLOCKS[n - FRONT_SLOTS]])
                slot, done = front_ring[:, n % FRONT_SLOTS, :], landed[n % FRONT_SLOTS]
                if name in ("upa", "upm"):
                    w = w_up_attn if name == "upa" else w_up_mlstm
                    sp.dma_start(slot.rearrange("p (k n) -> p k n", k=KM),
                                 w[0].rearrange("(k p) n -> p k n", p=P)).then_inc(done, 16)
                    continue
                dst = slot.rearrange("p (k n) -> p k n", k=KD)
                if name == "aq":
                    for h in range(A_HEADS):
                        to = (h % PAIRS) * P + (h // PAIRS) * A_HD
                        sp.dma_start(dst[:, :, to:to + A_HD],
                                     src[name][:, h * A_HD:(h + 1) * A_HD].rearrange("(k p) n -> p k n", p=P)
                                     ).then_inc(done, 16)
                    continue
                cols = src[name].shape[1]
                sp.dma_start(dst[:, :, 0:cols],
                             src[name].rearrange("(k p) n -> p k n", p=P)).then_inc(done, 16)
                if name == "kvg":
                    sp.dma_start(dst[:, :, 256:272],
                                 w_in[0, :, OFF_MG:OFF_MG + 16].rearrange("(k p) n -> p k n", p=P)
                                 ).then_inc(done, 16)

            def expert(s):
                return sp.value_load(tile_expert[0:1, bass.ds(s, 1)], min_val=0, max_val=N_EXP - 1)

            def load_in(e, q, which):
                w = (w_gate, w_up)[which]
                sp.dma_start(moe_slot[3 * q + which],
                             w[0, bass.ds(e, 1)].rearrange("e (p k) n -> (e p) (k n)", k=KD)
                             ).then_inc(moe_landed[3 * q + which], 16)

            def load_down(e, q):
                sp.dma_start(moe_slot[3 * q + 2],
                             w_down[0, bass.ds(e, 1)].rearrange("e (p k) n -> (e p) (k n)", k=KF)
                             ).then_inc(moe_landed[3 * q + 2], 16)

            sp.wait_ge(tiles_ready, 1)
            before = expert(0)
            load_in(before, 0, 0)
            wait_full(sp, "wo3.1")
            load_in(before, 0, 1)
            e = expert(1)
            load_in(e, 1, 0)
            wait_full(sp, "ada11")
            load_in(e, 1, 1)
            load_down(before, 1)

            def tile_loads(s, q, first=False):
                e, before = expert(s), expert(s - 1)
                sp.wait_ge(gate_full, s - 1)
                load_in(e, q, 0)
                sp.wait_ge(up_full, s - 1)
                load_in(e, q, 1)
                if not first:
                    sp.wait_ge(down_full, s - 2)
                load_down(before, q)

            tile_loads(2, 0, first=True)
            with sp.Fori(3, MOE_TILES, 2) as s:
                tile_loads(s, 1)
                tile_loads(s + 1, 0)
            last = MOE_TILES - 1
            e = expert(last)
            sp.wait_ge(down_full, last - 1)
            load_down(e, (last + 1) % 2)

        @block.tensor
        def _(pe):
            def chunks(name):
                return block_of(name).rearrange("p (k n) -> p k n", k=KD)

            def product(name, out, lhs, rhs, count, finish=True):
                for k in range(count):
                    mm = pe.matmul(out, lhs(k), rhs(k), start=(k == 0), stop=(k == count - 1))
                if finish:
                    mm.then_inc(psum_full, 1)

            def columns_out(name, block_name, col):
                wait_bank(pe, name)
                w = chunks(block_name)
                product(name, bank(name), lambda k: w[:, k, col:col + P], lambda k: hT[:, k, :], KD)

            def tokens_out(name, block_name, t, cols=COLS):
                wait_bank(pe, name)
                w = chunks(block_name)
                product(name, bank(name, cols), lambda k: hT[:, k, t * P:(t + 1) * P],
                        lambda k: w[:, k, 0:cols], KD)

            def transposes(name, srcs, idn=None):
                wait_bank(pe, name)
                out = bank(name).rearrange("p (n t) -> p n t", t=P)
                for n, s in enumerate(srcs):
                    mm = pe.transpose(out[:, n, :], s, ident)
                mm.then_inc(psum_full, 1)

            def ada(b):
                name = f"ada{b}"
                wait_block(pe, name)
                wait_bank(pe, name)
                w = chunks(name)
                product(name, bank(name)[0:REQS, :], lambda k: cT[:, k, :], lambda k: w[:, k, :], KD)

            def mod_turn(b):
                name = f"modT{b}"
                wait_bank(pe, name)
                wait_emptied(pe, f"ada{b}")
                for c in range(4):
                    mm = pe.transpose(bank(name)[:, c * REQS:(c + 1) * REQS],
                                      modrow[:, b % 2, c * P:(c + 1) * P], ident[0:REQS, 0:REQS])
                mm.then_inc(psum_full, 1)

            def ada_pair(b):
                ada(b)
                ada(b + 1)
                for n in range(2):
                    wait_emptied(pe, f"ada{b + n}")
                    for r in range(REQS):
                        name = f"spread{b + n}.{r}"
                        wait_bank(pe, name)
                        pe.matmul(bank(name), ident[0:REQS, r:r + 1].to_broadcast([REQS, P]),
                                  modrow[:, (b + n) % 2, :], start=True, stop=True).then_inc(psum_full, 1)

            pe.wait_ge(early_landed, 16)
            pe.wait_ge(c_ready, 1)
            for k in range(KD):
                mm = pe.transpose(bank("cT")[:, k * REQS:(k + 1) * REQS], crow[:, k * P:(k + 1) * P],
                                  ident[0:REQS, 0:REQS])
            mm.then_inc(psum_full, 1)
            pe.wait_ge(small_landed, 16 * 9)
            pe.transpose(bank("gainT")[:, 0:32], gains, ident[0:32, 0:32]).then_inc(psum_full, 1)
            wait_emptied(pe, "cT")
            ada(0)
            ada(1)
            mod_turn(0)
            ada(2)
            mod_turn(1)
            ada(3)
            mod_turn(2)
            mod_turn(3)
            pe.wait_ge(xn_ready, TT)
            for k in range(KD):
                transposes(f"xT{k}", [xbuf[:, t, k * P:(k + 1) * P] for t in range(TT)])
            wait_block(pe, "kvg")
            pe.wait_ge(gpad_ready, 1)
            wait_emptied(pe, f"xT{KD - 2}")
            wait_emptied(pe, f"xT{KD - 1}")
            columns_out("gates", "kvg", 384)
            columns_out("raw0", "kvg", 0)
            wait_bank(pe, "av")
            w = chunks("kvg")
            for t in range(TT):
                product("av", bank("av")[:, t * P:(t + 1) * P], lambda k: hT[:, k, t * P:(t + 1) * P],
                        lambda k: w[:, k, 128:256], KD, finish=(t == TT - 1))

            def swap(n):
                wait_bank(pe, f"swap{n}")
                wait_emptied(pe, f"raw{n}")
                pe.matmul(bank(f"swap{n}"), perm, raw[n % 2], start=True, stop=True).then_inc(psum_full, 1)

            wait_block(pe, "aq")
            for n in range(1, 5):
                name = f"raw{n}"
                wait_bank(pe, name)
                w = chunks("aq")
                product(name, bank(name), lambda k: w[:, k, (n - 1) * P:n * P], lambda k: hT[:, k, :], KD)
                swap(n - 1)
            wait_block(pe, "mq")
            columns_out("conv0", "mq", 0)
            swap(4)
            for c in range(1, 8):
                if c == 4:
                    wait_block(pe, "mk")
                columns_out(f"conv{c}", "mq" if c < 4 else "mk", (c % 4) * P)
            wait_block(pe, "mv")
            for t in range(TT):
                tokens_out(f"mv{t}", "mv", t)
            pe.wait_ge(rows_ready, 1)
            wait_bank(pe, "gateT")
            for kind in range(2):
                for d in range(2):
                    for t in range(TT):
                        c = ((kind * 2 + d) * TT + t) * M_HEADS
                        src = rows if kind == 0 else rows_x
                        mm = pe.transpose(bank("gateT")[:, c:c + M_HEADS], src[:, d, t * P:(t + 1) * P],
                                          ident[0:M_HEADS, 0:M_HEADS])
            mm.then_inc(psum_full, 1)
            wait_block(pe, "mo")
            for t in range(TT):
                tokens_out(f"mo{t}", "mo", t)

            def branch_gate(c):
                if c % 4 == 0:
                    wait_block(pe, f"bg{c // 4}")
                columns_out(f"bg{c}", f"bg{c // 4}", (c % 4) * P)

            def scores(b):
                r = b // TPR
                if b == 0:
                    wait_emptied(pe, "swap4")
                for n in range(A_HEADS // 2):
                    name = f"score{b}.{n}"
                    wait_bank(pe, name)
                    for h in (2 * n, 2 * n + 1):
                        at, j = h // PAIRS * A_HD, h % PAIRS
                        mm = pe.matmul(bank(name)[:, (h % 2) * SEQ:(h % 2 + 1) * SEQ],
                                       rot[at:at + A_HD, 1 + j, b * P:(b + 1) * P],
                                       rot[at:at + A_HD, 0, r * SEQ:(r + 1) * SEQ],
                                       start=True, stop=True)
                    mm.then_inc(psum_full, 1)

            def mlstm_scores(u):
                r, h = u // M_HEADS, u % M_HEADS
                name = f"mrow{u}"
                wait_bank(pe, name)
                for d in range(2):
                    mm = pe.matmul(bank(name)[:, d * SEQ:(d + 1) * SEQ],
                                   ident[0:M_HEADS, h:h + 1].to_broadcast([M_HEADS, P]),
                                   rows[:, 2 + d, r * SEQ:(r + 1) * SEQ], start=True, stop=True)
                mm.then_inc(psum_full, 1)
                if u == 0:
                    pe.wait_ge(conv_done, 8)
                name = f"qk{u}"
                wait_bank(pe, name)
                for s in range(TPR):
                    mm = pe.matmul(bank(name)[:, s * SEQ:(s + 1) * SEQ],
                                   mqk[:, 4 + h, r * SEQ + s * P:r * SEQ + (s + 1) * P],
                                   mqk[:, h, r * SEQ:(r + 1) * SEQ], start=True, stop=True)
                mm.then_inc(psum_full, 1)

            def mlstm_values(u):
                r, h = u // M_HEADS, u % M_HEADS
                wait_emptied(pe, f"qk{u}")
                if u == 0:
                    wait_emptied(pe, "mv3")
                    pe.wait_ge(ones_ready, 1)
                e = ebuf[:, u % 2]
                v = [mvb[:, r * TPR + s, h, :] for s in range(TPR)]
                plan = [[(0, [(0, 0)]), (1, [(128, 0), (256, 1)])],
                        [(0, [(0, 1), (256, 0)]), (1, [(128, 1)])]]
                for d in range(2):
                    name = f"num{u}.{d}"
                    wait_bank(pe, name)
                    for t, parts in plan[d]:
                        for n, (col, s) in enumerate(parts):
                            mm = pe.matmul(bank(name)[:, t * VW:(t + 1) * VW], e[:, d, col:col + P],
                                           v[s], start=(n == 0), stop=(n == len(parts) - 1))
                    mm.then_inc(psum_full, 1)

            def turn_probs(b):
                pe.wait_ge(probs_ready, b + 1)
                for n in range(4):
                    transposes(f"pT{b}.{n}", [probs[:, b % 2, 2 * n + i // 2, (i % 2) * P:(i % 2 + 1) * P]
                                              for i in range(4)])

            def attend(b):
                r = b // TPR
                wait_emptied(pe, f"pT{b}.2")
                wait_emptied(pe, f"pT{b}.3")
                if b == 0:
                    wait_emptied(pe, "av")
                wait_bank(pe, f"pv{b}")
                for h in range(A_HEADS):
                    for s in range(TPR):
                        kv = h // PAIRS
                        mm = pe.matmul(bank(f"pv{b}")[:, h * 64:(h + 1) * 64], pTb[:, 2 * h + s, :],
                                       av[:, r * TPR + s, kv * 64:(kv + 1) * 64],
                                       start=(s == 0), stop=(s == 1))
                mm.then_inc(psum_full, 1)

            for b in range(TT):
                scores(b)
                mlstm_scores(2 * b)
                branch_gate(4 * b)
                branch_gate(4 * b + 1)
                turn_probs(b)
                mlstm_values(2 * b)
                mlstm_scores(2 * b + 1)
                branch_gate(4 * b + 2)
                attend(b)
                mlstm_values(2 * b + 1)
                branch_gate(4 * b + 3)
                wait_emptied(pe, f"pv{b}")
                o = probs[:, b % 2].rearrange("p h k -> p (h k)")
                transposes(f"oT{b}", [o[:, k * P:(k + 1) * P] for k in range(KM)])

            ada_pair(4)
            for t in range(TT):
                pe.wait_ge(hm_ready, t + 1)
                transposes(f"mT{t}", [hm[:, t, k * P:(k + 1) * P] for k in range(KM)])
            for name, src, need in (("upa", oT, "oT3"), ("upm", mT, "mT3")):
                wait_block(pe, name)
                wait_emptied(pe, need)
                w = block_of(name).rearrange("p (k n) -> p k n", k=KM)
                for j in range(KD):
                    wait_bank(pe, f"{name}{j}")
                    product(name, bank(f"{name}{j}"), lambda k: w[:, k, j * P:(j + 1) * P],
                            lambda k: src[:, k, :], KM)
            ada_pair(6)
            ada_pair(8)
            wait_emptied(pe, "upm7")
            for h in range(2):
                wait_block(pe, f"wo{h}")
                w = chunks(f"wo{h}")
                for t in range(TT):
                    name = f"wo{t}.{h}"
                    wait_bank(pe, name)
                    product(name, bank(name), lambda k: bgate[:, k, t * P:(t + 1) * P],
                            lambda k: w[:, k, :], KD)
            pe.wait_ge(router_landed, 16 * 2)
            for t in range(TT):
                pe.wait_ge(h2_ready, t + 1)
                for h in range(2):
                    transposes(f"h2T{t}.{h}", [h2[:, t % 2, (4 * h + n) * P:(4 * h + n + 1) * P]
                                               for n in range(4)])
                name = f"logit{t}"
                wait_bank(pe, name)
                wait_emptied(pe, f"h2T{t}.1")
                product(name, bank(name, 20), lambda k: h2T[:, t % 2, k, :],
                        lambda k: router_w[:, k, :], KD)
            ada_pair(10)

            pe.wait_ge(onehots_ready, 1)
            pe.wait_ge(late_landed, 16 * 2)
            name = "rank"
            wait_bank(pe, name)
            chosen = route[:, 128:192].rearrange("p (t e) -> p t e", t=TT)
            for t in range(TT + 1):
                out = bank(name)[:, t * N_EXP:(t + 1) * N_EXP]
                for b in range(min(t, TT)):
                    mm = pe.matmul(out, lc["ones"], chosen[:, b, :], start=(b == 0),
                                   stop=(t == TT and b == TT - 1))
                if t < TT:
                    mm = pe.matmul(out, lc["tri"], chosen[:, t, :], start=(t == 0), stop=True)
            mm.then_inc(psum_full, 1)
            name = "ids"
            wait_bank(pe, name)
            for n in range(2 * TT):
                pe.wait_ge(hot_slots_ready, n + 1)
                mm = pe.matmul(bank(name)[:, 0:24], hot_place[n], hot_tile[n], start=(n == 0),
                               stop=(n == 2 * TT - 1))
            mm.then_inc(psum_full, 1)

            bank_gate, bank_up, bank_heT = psum[:, 0, :], psum[:, 1, :], psum[:, 2, :]
            wait_emptied(pe, "ids")
            wait_emptied(pe, "rank")
            wait_emptied(pe, "spread11.1")

            def weights(q, part, k):
                return moe_slot[3 * q + part].rearrange("p (k n) -> p k n", k=k)

            def turn_x(s, q, nth):
                pe.wait_ge(xs_landed[q], 16 * nth)
                v = xs[:, q, :].rearrange("t (p k) -> t k p", k=KD)
                for k in range(KD):
                    mm = pe.transpose(psum[:, 3 + k // 4, (k % 4) * P:(k % 4 + 1) * P], v[:, k, :], ident)
                mm.then_inc(xT_full, 1)

            def expand(s, q, nth, part):
                w = weights(q, part, KD)
                out, done = (bank_gate, gate_full) if part == 0 else (bank_up, up_full)
                pe.wait_ge(moe_landed[3 * q + part], 16 * nth)
                for k in range(KD):
                    mm = pe.matmul(out, xsT[:, k, :], w[:, k, :], start=(k == 0), stop=(k == KD - 1))
                mm.then_inc(done, 1)

            def turn_he(q):
                v = he[:, q, :].rearrange("t (p k) -> t k p", k=KF)
                for k in range(KF):
                    mm = pe.transpose(bank_heT[:, k * P:(k + 1) * P], v[:, k, :], ident)
                mm.then_inc(heT_full, 1)

            def contract(q, nth):
                w = weights(q, 2, KF)
                pe.wait_ge(moe_landed[3 * q + 2], 16 * nth)
                for h in range(2):
                    for k in range(KF):
                        mm = pe.matmul(psum[:, 5 + h, :], heT[:, k, :], w[:, k, h * COLS:(h + 1) * COLS],
                                       start=(k == 0), stop=(k == KF - 1))
                mm.then_inc(down_full, 1)

            turn_x(0, 0, 1)
            pe.wait_ge(xT_act, 1)
            pe.wait_ge(xT_dve, 1)
            expand(0, 0, 1, 0)
            expand(0, 0, 1, 1)

            def tile_step(s, q, fills, fills_down, first=False):
                turn_x(s, q, fills)
                pe.wait_ge(he_ready, s)
                turn_he(1 - q)
                pe.wait_ge(xT_act, s + 1)
                pe.wait_ge(xT_dve, s + 1)
                pe.wait_ge(silu_done, s)
                expand(s, q, fills, 0)
                expand(s, q, fills, 1)
                pe.wait_ge(heT_emptied, s)
                if not first:
                    pe.wait_ge(y_act, s - 1)
                    pe.wait_ge(y_dve, s - 1)
                contract(q, fills_down)

            tile_step(1, 1, 1, 1, first=True)
            tile_step(2, 0, 2, 1)
            with pe.Fori(1, (MOE_TILES - 1) // 2) as i:
                tile_step(i * 2 + 1, 1, i + 1, i + 1)
                tile_step(i * 2 + 2, 0, i + 2, i + 1)
            last = MOE_TILES - 1
            pe.wait_ge(he_ready, last + 1)
            turn_he(last % 2)
            pe.wait_ge(heT_emptied, last + 1)
            pe.wait_ge(y_act, last)
            pe.wait_ge(y_dve, last)
            contract((last + 1) % 2, (last + 1) // 2 + (last + 1) % 2)

        @block.scalar
        def _(act):
            steps = [0]

            def link(ins):
                steps[0] += 1
                ins.then_inc(act_chain, 1)
                act.wait_ge(act_chain, steps[0])

            act.dma_start(crow[0:1, :], c_prompt).then_inc(small_landed, 16)
            act.dma_start(crow[1:2, :], c_sample).then_inc(small_landed, 16)
            act.dma_start(early[:, :], early_consts).then_inc(early_landed, 16)
            act.dma_start(gains[0:KD, :], norm1_g.rearrange("a (k p) -> (a k) p", p=P)).then_inc(small_landed, 16)
            act.dma_start(gains[KD:32, :], conv_w[0].rearrange("w (k p) -> (w k) p", p=P)).then_inc(small_landed, 16)
            act.dma_start(sink[:, :], row_bcast(attn_sink[0])).then_inc(small_landed, 16)
            act.dma_start(hng[:, :], row_bcast(head_norm_g[0])).then_inc(small_landed, 16)
            act.dma_start(router_b[:, 0:4], row_bcast(rg_b[0])).then_inc(small_landed, 16)
            act.dma_start(router_b[:, 4:20], row_bcast(re_b[0])).then_inc(small_landed, 16)
            with nc.allow_non_contiguous_dma(reason="16 gate biases"):
                act.dma_start(gbias[:, :], m_gate_b[0].rearrange("(g h) -> h g", h=M_HEADS)).then_inc(small_landed, 16)
            act.wait_ge(small_landed, 16 * 9)
            act.activation(crow, crow, ACT.Silu).then_inc(c_ready, 1)
            act.wait_ge(x_landed, 16 * REQS)
            act.wait_ge(ones_ready, 1)
            for t in range(TT):
                link(act.activation(sqjunk, xbuf[:, t, :], ACT.Square, accum_out=small[:, t:t + 1]))
            act.activation(small[:, 4:8], small[:, 0:4], ACT.Sqrt, scale=1.0 / D, bias=eps[:, 0:1]
                           ).then_inc(xsq_ready, 1)

            for k in range(1, KD, 2):
                name = f"xT{k}"
                wait_full(act, name)
                if k == 1:
                    act.wait_ge(dve_emptied, emptied_count("modT3"))
                    act.wait_ge(xn_ready, TT + 1)
                for r in range(REQS):
                    ins = act.activation(hT[:, k, r * SEQ:(r + 1) * SEQ], bank(name)[:, r * SEQ:(r + 1) * SEQ],
                                         ACT.Identity, scale=scale1[:, k, r:r + 1],
                                         bias=modT[:, k // 4, k % 4, r:r + 1])
                ins.then_inc(act_emptied, 1)

            def copy_raw(n):
                wait_full(act, f"raw{n}")
                if n >= 2:
                    wait_emptied(act, f"swap{n - 2}")
                act.activation(raw[n % 2], bank(f"raw{n}"), ACT.Copy).then_inc(act_emptied, 1)

            copy_raw(0)
            wait_full(act, "av")
            act.activation(rot_v[:, 2560:3072], bank("av"), ACT.Copy).then_inc(act_emptied, 1)
            act.wait_ge(forget_abs, 1)
            link(act.activation(rows_x, rows_x, ACT.Exp))
            act.activation(rows_x, rows_x, ACT.Ln, bias=1.0).then_inc(forget_ln, 1)
            for n in range(1, 5):
                copy_raw(n)
            for c in range(8):
                wait_emptied(act, f"conv{c}")
                act.activation(mqk[:, c, :], acc[c % 2], ACT.Silu).then_inc(conv_done, 1)
            for t in range(TT):
                wait_full(act, f"mv{t}")
                act.activation(mvb[:, t, :, 0:M_HD], bank(f"mv{t}").rearrange("p (h e) -> p h e", h=M_HEADS),
                               ACT.Copy).then_inc(act_emptied, 1)
            wait_full(act, "gateT")
            act.activation(gateT[:, 0], bank("gateT", 32).rearrange("p (d t h) -> p d t h", d=2, t=TT), ACT.Copy)
            act.activation(gateT[:, 1], bank("gateT", 64)[:, 32:64].rearrange("p (d t h) -> p d t h", d=2, t=TT),
                           ACT.Exp).then_inc(act_emptied, 1)
            for t in range(TT):
                wait_full(act, f"mo{t}")
                act.activation(og[:, t, :], bank(f"mo{t}"), ACT.Tanh, scale=0.5).then_inc(act_emptied, 1)

            def branch_gate(c):
                wait_full(act, f"bg{c}")
                act.activation(bgate[:, c, :], bank(f"bg{c}"), ACT.Tanh, scale=0.5).then_inc(act_emptied, 1)

            def softmax_exp(b):
                act.wait_ge(negmax_ready, b + 1)
                st = stat[:, b % 2]
                for h in range(A_HEADS):
                    act.activation(probs[:, b % 2, h, :], probs[:, b % 2, h, :], ACT.Exp,
                                   bias=st[:, 1, h:h + 1], accum_out=st[:, 3, h:h + 1])
                act.activation(st[:, 4, :], st[:, 2, :], ACT.Exp).then_inc(probs_ready, 1)

            def decay_exp(u):
                wait_emptied(act, f"mrow{u}")
                act.activation(ebuf[:, u % 2], ebuf[:, u % 2], ACT.Exp).then_inc(decay_ready, 1)

            for b in range(TT):
                softmax_exp(b)
                decay_exp(2 * b)
                branch_gate(4 * b)
                branch_gate(4 * b + 1)
                for n in (1, 3):
                    wait_full(act, f"pT{b}.{n}")
                    if b >= 1:
                        wait_full(act, f"pv{b - 1}")
                    act.activation(pTb[:, 4 * n:4 * n + 4, :], bank(f"pT{b}.{n}").rearrange("p (n t) -> p n t", t=P),
                                   ACT.Copy).then_inc(act_emptied, 1)
                decay_exp(2 * b + 1)
                branch_gate(4 * b + 2)
                branch_gate(4 * b + 3)
                wait_full(act, f"oT{b}")
                act.activation(oT[:, :, b * P:(b + 1) * P], bank(f"oT{b}").rearrange("p (k t) -> p k t", k=KM),
                               ACT.Copy).then_inc(act_emptied, 1)

            def spread(b, dst, scale):
                for n in range(2):
                    for r in range(REQS):
                        name = f"spread{b + n}.{r}"
                        wait_full(act, name)
                        act.activation(dst[:, r, n * COLS:(n + 1) * COLS], bank(name), ACT.Copy,
                                       scale=scale).then_inc(act_emptied, 1)

            spread(4, g1b, 0.5)
            act.wait_ge(hm_sq, 1)
            act.activation(small[:, 24:40], small[:, 8:24], ACT.Sqrt, scale=1.0 / M_HD, bias=eps[:, 0:1]
                           ).then_inc(hm_root, 1)
            for t in range(TT):
                wait_full(act, f"mT{t}")
                act.activation(mT[:, :, t * P:(t + 1) * P], bank(f"mT{t}").rearrange("p (k t) -> p k t", k=KM),
                               ACT.Copy).then_inc(act_emptied, 1)
            wait_full(act, "mT3")
            act.wait_ge(hm_ready, TT)
            spread(6, shift2, 1.0)
            for t in range(TT):
                wait_emptied(act, f"wo{t}.1")
                link(act.activation(sqjunk, xbuf[:, t, :], ACT.Square, accum_out=small[:, 40 + t:41 + t]))
                act.activation(small[:, 44 + t:45 + t], small[:, 40 + t:41 + t], ACT.Sqrt, scale=1.0 / D,
                               bias=eps[:, 0:1]).then_inc(x1_root, 1)
            for t in range(TT):
                for h in range(2):
                    wait_full(act, f"h2T{t}.{h}")
                    if t >= 2:
                        wait_full(act, f"logit{t - 2}")
                    act.activation(h2T[:, t % 2, 4 * h:4 * h + 4, :],
                                   bank(f"h2T{t}.{h}").rearrange("p (k t) -> p k t", t=P),
                                   ACT.Copy).then_inc(act_emptied, 1)
            spread(10, g2b, 1.0)
            act.wait_ge(gate_sum, 1)
            act.activation(route[:, 80:100], route[:, 80:100], ACT.Exp).then_inc(gate_exp, 1)

            def empty_x():
                act.activation(xsT[:, 0:4, :], psum[:, 3, :].rearrange("p (k t) -> p k t", k=4), ACT.Copy
                               ).then_inc(xT_act, 1)

            def silu(q):
                act.activation(sg[:, q, :], psum[:, 0, :], ACT.Silu).then_inc(silu_done, 1)

            def empty_he():
                act.activation(heT, psum[:, 2, :].rearrange("p (k t) -> p k t", k=KF), ACT.Copy
                               ).then_inc(heT_emptied, 1)

            def empty_y(q):
                act.activation(ybuf[:, q, 0:COLS], psum[:, 5, :], ACT.Copy).then_inc(y_act, 1)

            def store_y(s, q):
                act.dma_start(y_rows[bass.ds(s * P, P), :], ybuf[:, q, :]).then_inc(y_stored[q], 16)

            act.wait_ge(xT_full, 1)
            empty_x()
            act.wait_ge(gate_full, 1)
            silu(0)
            act.wait_ge(xT_full, 2)
            empty_x()
            act.wait_ge(heT_full, 1)
            empty_he()
            act.wait_ge(gate_full, 2)
            silu(1)
            act.wait_ge(down_full, 1)
            empty_y(0)
            act.wait_ge(y_act, 1)
            act.wait_ge(y_dve, 1)
            store_y(0, 0)
            act.wait_ge(xT_full, 3)
            empty_x()
            act.wait_ge(heT_full, 2)
            empty_he()
            act.wait_ge(gate_full, 3)
            act.wait_ge(he_ready, 1)
            silu(0)
            act.wait_ge(down_full, 2)
            empty_y(1)
            act.wait_ge(y_act, 2)
            act.wait_ge(y_dve, 2)
            store_y(1, 1)
            with act.Fori(1, (MOE_TILES - 1) // 2) as i:
                for n in range(2):
                    q = (1 + n) % 2
                    s = i * 2 + (1 + n)
                    act.wait_ge(xT_full, s + 1)
                    empty_x()
                    act.wait_ge(heT_full, s)
                    empty_he()
                    act.wait_ge(gate_full, s + 1)
                    act.wait_ge(he_ready, s - 1)
                    silu(q)
                    act.wait_ge(down_full, s)
                    act.wait_ge(y_stored[1 - q], i * 16)
                    empty_y(1 - q)
                    act.wait_ge(y_act, s)
                    act.wait_ge(y_dve, s)
                    store_y(i * 2 + n, 1 - q)
            last = MOE_TILES - 1
            act.wait_ge(heT_full, last + 1)
            empty_he()
            act.wait_ge(down_full, last + 1)
            act.wait_ge(y_stored[last % 2], 16 * (last // 2))
            empty_y(last % 2)
            act.wait_ge(y_act, last + 1)
            act.wait_ge(y_dve, last + 1)
            store_y(last, last % 2)

            for t in range(TT):
                act.wait_ge(x2_ready, t + 1)
                link(act.activation(junk, xbuf[:, t, :], ACT.Square, accum_out=small[:, 48 + t:49 + t]))
                act.activation(small[:, 52 + t:53 + t], small[:, 48 + t:49 + t], ACT.Sqrt, scale=1.0 / D,
                               bias=eps[:, 0:1]).then_inc(x2_root, 1)
            for t in range(TT):
                act.wait_ge(y_ready, t + 1)
                r, tt = t // TPR, t % TPR
                act.dma_start(y_out[r][0, tt * P:(tt + 1) * P, :], xbuf[:, t, :]).then_inc(out_stored, 16)
            act.wait_ge(out_stored, 16 * TT)

        @block.vector
        def _(dve):
            steps = [0]

            def link(ins):
                steps[0] += 1
                ins.then_inc(dve_chain, 1)
                dve.wait_ge(dve_chain, steps[0])

            def emptied(ins):
                ins.then_inc(dve_emptied, 1)

            link(dve.memset(mvb[:, :, :, M_HD:VW], 1.0))
            link(dve.memset(ones_row, 1.0))
            dve.memset(eps[:, :], EPS).then_inc(ones_ready, 1)
            wait_full(dve, "cT")
            emptied(dve.tensor_copy(cT[:, :, :], bank("cT")[:, 0:KD * REQS].rearrange("p (k r) -> p k r", k=KD)))
            wait_full(dve, "gainT")
            emptied(dve.tensor_copy(gainT[:, :], bank("gainT")[:, 0:32]))
            link(dve.tensor_scalar(nsink[:, :], sink[:, :], -1.0, None, ALU.mult))

            def ada_bias(b):
                name = f"ada{b}"
                wait_full(dve, name)
                dve.wait_ge(bias_landed, 16 * (b + 1))
                if b < 4 and b >= 2:
                    wait_full(dve, f"modT{b - 2}")
                elif b >= 4:
                    prev = f"modT{b - 2}" if b < 6 else f"spread{b - 2}.1"
                    wait_full(dve, prev)
                emptied(dve.tensor_tensor(modrow[:, b % 2, :], bank(name)[0:REQS, :], biasrow, ALU.add))

            def mod_turned(b):
                wait_full(dve, f"modT{b}")
                emptied(dve.tensor_copy(modT[:, b], bank(f"modT{b}")[:, 0:8].rearrange("p (c r) -> p c r", c=4)))

            dve.wait_ge(xsq_ready, 1)
            link(dve.reciprocal(small[:, 0:4], small[:, 4:8]))
            for t in range(TT):
                dve.tensor_scalar(xbuf[:, t, :], xbuf[:, t, :], small[:, t:t + 1], None, ALU.mult
                                  ).then_inc(xn_ready, 1)
            ada_bias(0)
            ada_bias(1)
            mod_turned(0)
            ada_bias(2)
            mod_turned(1)
            ada_bias(3)
            mod_turned(2)
            mod_turned(3)
            dve.wait_ge(dve_emptied, emptied_count("modT3"))
            for r in range(REQS):
                ins = dve.scalar_tensor_tensor(out=scale1[:, :, r],
                                               in0=modT[:, 2:4, :, r].rearrange("p b c -> p (b c)"),
                                               scalar=1.0, in1=gainT[:, 0:KD], op0=ALU.add, op1=ALU.mult)
                if r == 0:
                    link(ins)
                else:
                    ins.then_inc(xn_ready, 1)
            dve.wait_ge(xn_ready, TT + 1)
            for k in range(0, KD, 2):
                name = f"xT{k}"
                wait_full(dve, name)
                for r in range(REQS):
                    ins = dve.tensor_scalar(hT[:, k, r * SEQ:(r + 1) * SEQ], bank(name)[:, r * SEQ:(r + 1) * SEQ],
                                            scale1[:, k, r:r + 1], modT[:, k // 4, k % 4, r:r + 1],
                                            ALU.mult, ALU.add)
                emptied(ins)
            wait_block(dve, "kvg")
            gw = block_of("kvg").rearrange("p (k n) -> p k n", k=KD)
            link(dve.memset(gw[:, :, 384:512], 0.0))
            for g in range(4):
                ins = dve.tensor_copy(gw[:, :, 384 + 32 * g:388 + 32 * g], gw[:, :, 256 + 4 * g:260 + 4 * g])
            ins.then_inc(gpad_ready, 1)

            wait_full(dve, "gates")
            for g, slot in ((0, 0), (2, 1), (1, 2), (3, 3)):
                ins = dve.tensor_copy(rows[:, slot, :], bank("gates")[32 * g:32 * g + M_HEADS, :])
            emptied(ins)
            wait_emptied(dve, "gates")
            for g, slot in ((0, 0), (2, 1), (1, 2), (3, 3)):
                link(dve.tensor_scalar(rows[:, slot, :], rows[:, slot, :], gbias[:, g:g + 1], None, ALU.add))
            dve.scalar_tensor_tensor(out=rows_x, in0=rows[:, 2:4, :], scalar=-1.0, in1=rows[:, 2:4, :],
                                     op0=ALU.mult, op1=ALU.min).then_inc(forget_abs, 1)
            dve.wait_ge(forget_ln, 1)
            link(dve.scalar_tensor_tensor(out=rows[:, 2:4, :], in0=rows[:, 2:4, :], scalar=0.0, in1=rows_x,
                                          op0=ALU.min, op1=ALU.subtract))

            def scans(dst, src, first, first_op, second_op):
                for d in range(2):
                    for r in range(REQS):
                        o, i = dst[:, d, r * SEQ:(r + 1) * SEQ], src[:, d, r * SEQ:(r + 1) * SEQ]
                        a = i if first is None else first
                        if d == 1:
                            o, i, a = o[:, ::-1], i[:, ::-1], a[:, ::-1]
                        link(dve.tensor_tensor_scan(o, a, i, 0.0, first_op, second_op))

            log_f, cum, inp, run = rows[:, 2:4, :], rows_x, rows[:, 0:2, :], rows[:, 2:4, :]
            scans(cum, log_f, ones_row, ALU.mult, ALU.add)
            link(dve.tensor_tensor(inp, inp, cum, ALU.subtract))
            scans(run, inp, None, ALU.max, ALU.max)
            link(dve.scalar_tensor_tensor(out=cum, in0=cum, scalar=-1.0, in1=run, op0=ALU.mult, op1=ALU.subtract))
            dve.tensor_scalar(run, run, -1.0, None, ALU.mult).then_inc(rows_ready, 1)

            def rotate(n):
                wait_emptied(dve, f"raw{n}")
                two = lambda ap: ap.rearrange("p (r t) -> p r t", r=REQS)
                table = lambda c: const(c).rearrange("p (a t) -> p a t", a=1).to_broadcast([P, REQS, SEQ])
                link(dve.tensor_tensor(two(rot[:, n, :]), two(raw[n % 2]), table("cos"), ALU.mult))
                wait_full(dve, f"swap{n}")
                link(dve.tensor_tensor(two(tmp[:, :]), two(bank(f"swap{n}")), table("sin"), ALU.mult))
                emptied(dve.tensor_tensor(rot[:, n, :], rot[:, n, :], tmp[:, :], ALU.add))
                wait_emptied(dve, f"swap{n}")

            def conv(c):
                wait_full(dve, f"conv{c}")
                if c >= 2:
                    dve.wait_ge(conv_done, c - 1)
                a = acc[c % 2].rearrange("p (r t) -> p r t", r=REQS)
                u = bank(f"conv{c}").rearrange("p (r t) -> p r t", r=REQS)
                w = [gainT[:, 8 + 8 * j + c:9 + 8 * j + c] for j in range(3)]
                link(dve.tensor_scalar(a, u, w[1], None, ALU.mult))
                link(dve.scalar_tensor_tensor(out=a[:, :, 1:SEQ], in0=u[:, :, 0:SEQ - 1], scalar=w[0],
                                              in1=a[:, :, 1:SEQ], op0=ALU.mult, op1=ALU.add))
                emptied(dve.scalar_tensor_tensor(out=a[:, :, 0:SEQ - 1], in0=u[:, :, 1:SEQ], scalar=w[2],
                                                 in1=a[:, :, 0:SEQ - 1], op0=ALU.mult, op1=ALU.add))

            for n in range(4):
                rotate(n)
            conv(0)
            rotate(4)
            for c in range(1, 8):
                conv(c)

            def softmax_rows(b):
                st = stat[:, b % 2]
                if b >= 2:
                    wait_full(dve, f"oT{b - 2}")
                m = const("maskU" if b % TPR == 0 else "maskL")
                m = m.rearrange("p (a k) -> p a k", a=1).to_broadcast([P, 2, SEQ])
                for n in range(A_HEADS // 2):
                    name = f"score{b}.{n}"
                    wait_full(dve, name)
                    emptied(dve.scalar_tensor_tensor(
                        out=probs[:, b % 2, 2 * n:2 * n + 2, :],
                        in0=bank(name).rearrange("p (g k) -> p g k", g=2), scalar=A_HD ** -0.5, in1=m,
                        op0=ALU.mult, op1=ALU.add))
                wait_emptied(dve, f"score{b}.3")
                link(dve.tensor_reduce(st[:, 0, :], probs[:, b % 2], AX.X, ALU.max))
                link(dve.scalar_tensor_tensor(out=st[:, 1, :], in0=st[:, 0, :], scalar=-1.0, in1=nsink[:, :],
                                              op0=ALU.mult, op1=ALU.min))
                dve.tensor_tensor(st[:, 2, :], st[:, 1, :], sink[:, :], ALU.add).then_inc(negmax_ready, 1)

            def decays(u):
                r, h = u // M_HEADS, u % M_HEADS
                if u >= 2:
                    wait_full(dve, f"num{u - 2}.1")
                if u == 0:
                    wait_emptied(dve, "gateT")
                name = f"mrow{u}"
                wait_full(dve, name)
                e = ebuf[:, u % 2]
                L, U = const("maskL"), const("maskU")
                for d in range(2):
                    m = bank(name)[:, d * SEQ:(d + 1) * SEQ]
                    for s in range(TPR):
                        wide = s == d
                        col = gateT[:, 0, d, r * TPR + s, h:h + 1]
                        own = slice(s * P, (s + 1) * P)
                        mask = L if d == 0 else U
                        if not wide:
                            mask = L[:, 0:P] if d == 0 else U[:, P:2 * P]
                        ins = dve.scalar_tensor_tensor(
                            out=e[:, d, 0:SEQ] if wide else e[:, d, SEQ:SEQ + P],
                            in0=m if wide else m[:, own], scalar=col, in1=mask, op0=ALU.add, op1=ALU.add)
                emptied(ins)

            def weigh(u):
                dve.wait_ge(decay_ready, u + 1)
                name = f"qk{u}"
                wait_full(dve, name)
                e = ebuf[:, u % 2]
                for d in range(2):
                    for s in range(TPR):
                        wide = s == d
                        a = bank(name)[:, s * SEQ:(s + 1) * SEQ]
                        o = e[:, d, 0:SEQ] if wide else e[:, d, SEQ:SEQ + P]
                        ins = dve.scalar_tensor_tensor(out=o, in0=a if wide else a[:, s * P:(s + 1) * P],
                                                       scalar=M_HD ** -0.5, in1=o, op0=ALU.mult, op1=ALU.mult)
                emptied(ins)

            def normalise(u):
                r, h = u // M_HEADS, u % M_HEADS
                for d in range(2):
                    name = f"num{u}.{d}"
                    wait_full(dve, name)
                    v = bank(name)[:, 0:TPR * VW].rearrange("p (t e) -> p t e", t=TPR)
                    link(dve.tensor_tensor(mstat[:, d, 0, :], v[:, :, M_HD],
                                           gateT[:, 1, d, r * TPR:(r + 1) * TPR, h], ALU.max))
                    link(dve.scalar_tensor_tensor(out=mstat[:, d, 0, :], in0=v[:, :, M_HD], scalar=-1.0,
                                                  in1=mstat[:, d, 0, :], op0=ALU.mult, op1=ALU.max))
                    link(dve.reciprocal(mstat[:, d, 1, :], mstat[:, d, 0, :]))
                    for t in range(TPR):
                        o = hm[:, r * TPR + t, h * M_HD:(h + 1) * M_HD]
                        rec = mstat[:, d, 1, t:t + 1]
                        if d == 0:
                            ins = dve.tensor_scalar(o, v[:, t, 0:M_HD], rec, None, ALU.mult)
                        else:
                            ins = dve.scalar_tensor_tensor(out=o, in0=v[:, t, 0:M_HD], scalar=rec, in1=o,
                                                           op0=ALU.mult, op1=ALU.add)
                    emptied(ins)
                    wait_emptied(dve, name)

            for b in range(TT):
                softmax_rows(b)
                decays(2 * b)
                weigh(2 * b)
                for n in (0, 2):
                    wait_full(dve, f"pT{b}.{n}")
                    if b >= 1:
                        wait_full(dve, f"pv{b - 1}")
                    emptied(dve.tensor_copy(pTb[:, 4 * n:4 * n + 4, :],
                                            bank(f"pT{b}.{n}").rearrange("p (n t) -> p n t", t=P)))
                st = stat[:, b % 2]
                link(dve.tensor_tensor(st[:, 5, :], st[:, 3, :], st[:, 4, :], ALU.add))
                link(dve.reciprocal(st[:, 6, :], st[:, 5, :]))
                normalise(2 * b)
                decays(2 * b + 1)
                weigh(2 * b + 1)
                wait_full(dve, f"pv{b}")
                o = probs[:, b % 2].rearrange("p h k -> p (h k)")[:, 0:COLS].rearrange("p (h d) -> p h d", h=A_HEADS)
                emptied(dve.tensor_tensor(o, bank(f"pv{b}").rearrange("p (h d) -> p h d", h=A_HEADS),
                                          st[:, 6, :].rearrange("p (h a) -> p h a", a=1).to_broadcast([P, A_HEADS, A_HD]),
                                          ALU.mult))
                normalise(2 * b + 1)

            for t in range(TT):
                link(dve.tensor_tensor(tmp[:, :], hm[:, t, :], hm[:, t, :], ALU.mult))
                ins = dve.tensor_reduce(small[:, 8 + 4 * t:12 + 4 * t], tmp[:, :].rearrange("p (h e) -> p h e", h=M_HEADS),
                                        AX.X, ALU.add)
                if t < TT - 1:
                    link(ins)
            ins.then_inc(hm_sq, 1)
            ada_bias(4)
            ada_bias(5)
            dve.wait_ge(hm_root, 1)
            link(dve.reciprocal(small[:, 8:24], small[:, 24:40]))
            link(dve.tensor_scalar(small[:, 8:24], small[:, 8:24], 0.5, None, ALU.mult))
            wait_emptied(dve, "mo3")
            for t in range(TT):
                v = hm[:, t, :].rearrange("p (h e) -> p h e", h=M_HEADS)
                link(dve.tensor_tensor(v, v, small[:, 8 + 4 * t:12 + 4 * t].rearrange("p (h a) -> p h a", a=1)
                                       .to_broadcast([P, M_HEADS, M_HD]), ALU.mult))
                link(dve.tensor_tensor(hm[:, t, :], hm[:, t, :], hng[:, :], ALU.mult))
                dve.scalar_tensor_tensor(out=hm[:, t, :], in0=og[:, t, :], scalar=1.0, in1=hm[:, t, :],
                                         op0=ALU.add, op1=ALU.mult).then_inc(hm_ready, 1)

            wait_emptied(dve, "bg15")
            for j in range(KD):
                wait_full(dve, f"upa{j}")
                emptied(dve.scalar_tensor_tensor(out=bgate[:, j, :], in0=bgate[:, j, :], scalar=1.0,
                                                 in1=bank(f"upa{j}"), op0=ALU.add, op1=ALU.mult))
            wait_emptied(dve, "upa7")
            for j in range(KD):
                wait_full(dve, f"upm{j}")
                link(dve.scalar_tensor_tensor(out=bgate[:, KD + j, :], in0=bgate[:, KD + j, :], scalar=1.0,
                                              in1=bank(f"upm{j}"), op0=ALU.add, op1=ALU.mult))
                emptied(dve.tensor_tensor(bgate[:, j, :], bgate[:, j, :], bgate[:, KD + j, :], ALU.add))
            ada_bias(6)
            ada_bias(7)
            ada_bias(8)
            ada_bias(9)
            dve.wait_ge(late_landed, 16 * 2)
            for n in range(2):
                for r in range(REQS):
                    name = f"spread{8 + n}.{r}"
                    wait_full(dve, name)
                    emptied(dve.scalar_tensor_tensor(out=scale2[:, r, n * COLS:(n + 1) * COLS], in0=bank(name),
                                                     scalar=1.0, in1=gain2[:, n * COLS:(n + 1) * COLS],
                                                     op0=ALU.add, op1=ALU.mult))

            dve.wait_ge(x_again, 16 * REQS)
            wait_emptied(dve, "spread5.1")
            for h in range(2):
                for t in range(TT):
                    name = f"wo{t}.{h}"
                    wait_full(dve, name)
                    xs_ = xbuf[:, t, h * COLS:(h + 1) * COLS]
                    link(dve.tensor_tensor(tmp[:, :], bank(name), g1b[:, t // TPR, h * COLS:(h + 1) * COLS], ALU.mult))
                    emptied(dve.tensor_tensor(xs_, xs_, tmp[:, :], ALU.add))
                    wait_emptied(dve, name)
            wait_emptied(dve, "spread7.1")
            for t in range(TT):
                r = t // TPR
                dve.wait_ge(x1_root, t + 1)
                if t >= 2:
                    wait_full(dve, f"h2T{t - 2}.1")
                    dve.wait_ge(h2_stored[t % 2], 16 * (t // 2))
                link(dve.reciprocal(small[:, 40 + t:41 + t], small[:, 44 + t:45 + t]))
                link(dve.scalar_tensor_tensor(out=h2[:, t % 2, :], in0=xbuf[:, t, :], scalar=small[:, 40 + t:41 + t],
                                              in1=scale2[:, r, :], op0=ALU.mult, op1=ALU.mult))
                dve.tensor_tensor(h2[:, t % 2, :], h2[:, t % 2, :], shift2[:, r, :], ALU.add).then_inc(h2_ready, 1)
            logits = route[:, 0:80].rearrange("p (t n) -> p t n", t=TT)
            for t in range(TT):
                wait_full(dve, f"logit{t}")
                emptied(dve.tensor_tensor(logits[:, t, :], bank(f"logit{t}", 20), router_b[:, :], ALU.add))
            wait_emptied(dve, "logit3")
            ada_bias(10)
            ada_bias(11)

            def three(a, w, n=4):
                return route[:, a:a + w].rearrange("p (t n) -> p t n", n=n)

            def over(ap, n=4):
                return ap.rearrange("p (t a) -> p t a", a=1).to_broadcast([P, TT, n])

            best = small[:, 0:4]
            second = small[:, 4:8]
            grp_p = small[:, 8:12]
            t4 = small[:, 12:16]
            lo = small[:, 16:20]
            iota4 = lc["iota4"].rearrange("p (a n) -> p a n", a=1).to_broadcast([P, TT, 4])
            grp_hot, e_in, hot1, hot2, scr = (three(448, 16), three(464, 16), three(480, 16),
                                              three(496, 16), three(512, 16))

            def first_hot(out, vals, top):
                link(dve.tensor_tensor(out, vals, over(top), ALU.is_equal))
                link(dve.tensor_tensor(out, out, iota4, ALU.mult))
                link(dve.tensor_reduce(lo, out, AX.X, ALU.min))
                link(dve.tensor_tensor(out, iota4, over(lo), ALU.is_equal))

            g_log, e_log = logits[:, :, 0:N_GRP], logits[:, :, N_GRP:20]
            link(dve.tensor_reduce(best, g_log, AX.X, ALU.max))
            first_hot(grp_hot, g_log, best)
            gdiff = three(80, 16)
            link(dve.tensor_tensor(gdiff, g_log, over(best), ALU.subtract))
            prod = route[:, 192:256]
            p4 = prod.rearrange("p (t g k) -> p t g k", t=TT, g=N_GRP)
            for t in range(TT):
                link(dve.tensor_tensor(p4[:, t], e_log[:, t, :].rearrange("p (g k) -> p g k", g=N_GRP),
                                       grp_hot[:, t, :].rearrange("p (g a) -> p g a", a=1)
                                       .to_broadcast([P, N_GRP, PER_GRP]), ALU.mult))
            link(dve.tensor_reduce(e_in, p4.rearrange("p t g k -> p t k g"), AX.X, ALU.add))
            link(dve.tensor_reduce(best, e_in, AX.X, ALU.max))
            first_hot(hot1, e_in, best)
            link(dve.scalar_tensor_tensor(out=scr, in0=hot1, scalar=-BIG, in1=e_in, op0=ALU.mult, op1=ALU.add))
            link(dve.tensor_reduce(second, scr, AX.X, ALU.max))
            first_hot(hot2, scr, second)
            dve.tensor_tensor(route[:, 96:100], second, best, ALU.subtract).then_inc(gate_sum, 1)
            dve.wait_ge(gate_exp, 1)
            link(dve.tensor_reduce(t4, gdiff, AX.X, ALU.add))
            link(dve.reciprocal(grp_p, t4))
            link(dve.tensor_scalar(t4, route[:, 96:100], 1.0, None, ALU.add))
            link(dve.reciprocal(lo, t4))
            link(dve.tensor_tensor(topw[:, :, 0], lo, grp_p, ALU.mult))
            link(dve.tensor_tensor(topw[:, :, 1], topw[:, :, 0], route[:, 96:100], ALU.mult))
            c12 = [hmf[:, n * 64:(n + 1) * 64].rearrange("p (t e) -> p t e", t=TT) for n in range(2)]
            chosen = route[:, 128:192].rearrange("p (t e) -> p t e", t=TT)
            for n, hot in enumerate((hot1, hot2)):
                for t in range(TT):
                    c = c12[n][:, t, :].rearrange("p (g k) -> p g k", g=N_GRP)
                    link(dve.tensor_tensor(c, grp_hot[:, t, :].rearrange("p (g a) -> p g a", a=1)
                                           .to_broadcast([P, N_GRP, PER_GRP]),
                                           hot[:, t, :].rearrange("p (a k) -> p a k", a=1)
                                           .to_broadcast([P, N_GRP, PER_GRP]), ALU.mult))
            dve.tensor_tensor(chosen, c12[0], c12[1], ALU.add).then_inc(onehots_ready, 1)

            wait_full(dve, "rank")
            f = hmf[:, 128:]
            rank = f[:, 0:64]
            cnt = f[:, 64:80]
            tiles = f[:, 80:96]
            ends = f[:, 96:112]
            starts = f[:, 112:128]
            div = f[:, 128:192]
            mod = f[:, 192:256]
            link(dve.tensor_copy(rank, bank("rank", 64)))
            emptied(dve.tensor_copy(cnt, bank("rank", 80)[:, 64:80]))
            wait_emptied(dve, "rank")
            link(dve.tensor_scalar(tiles, cnt, 0.0, None, ALU.is_gt))
            for j in range(1, TT):
                link(dve.scalar_tensor_tensor(out=tiles, in0=cnt, scalar=float(j * P), in1=tiles,
                                              op0=ALU.is_gt, op1=ALU.add))
            link(dve.tensor_tensor_scan(ends, lc["ones"][:, 0:N_EXP], tiles, 0.0, ALU.mult, ALU.add))
            link(dve.tensor_tensor(starts, ends, tiles, ALU.subtract))
            link(dve.tensor_scalar(div, rank, float(P), None, ALU.is_ge))
            for j in range(2, TT):
                link(dve.scalar_tensor_tensor(out=div, in0=rank, scalar=float(j * P), in1=div,
                                              op0=ALU.is_ge, op1=ALU.add))
            link(dve.scalar_tensor_tensor(out=mod, in0=div, scalar=-float(P), in1=rank, op0=ALU.mult, op1=ALU.add))
            d3 = div.rearrange("p (t e) -> p t e", t=TT)
            m3 = mod.rearrange("p (t e) -> p t e", t=TT)
            link(dve.tensor_tensor(d3, d3, starts.rearrange("p (a e) -> p a e", a=1).to_broadcast([P, TT, N_EXP]), ALU.add))
            tile_of = f[:, 256:264].rearrange("p (t n) -> p t n", t=TT)
            place_of = f[:, 264:272].rearrange("p (t n) -> p t n", t=TT)
            scratch = f[:, 272:336].rearrange("p (t e) -> p t e", t=TT)
            for n in range(2):
                link(dve.tensor_tensor(scratch, d3, c12[n], ALU.mult))
                link(dve.tensor_reduce(tile_of[:, :, n], scratch, AX.X, ALU.add))
                link(dve.tensor_tensor(scratch, m3, c12[n], ALU.mult))
                link(dve.tensor_reduce(place_of[:, :, n], scratch, AX.X, ALU.add))
            link(dve.scalar_tensor_tensor(out=pos[:, :, :], in0=tile_of, scalar=float(P), in1=place_of,
                                          op0=ALU.mult, op1=ALU.add))
            for b in range(2):
                dve.wait_ge(h2_stored[b], 16 * (TT // 2))
            for t in range(TT):
                for n in range(2):
                    link(dve.tensor_scalar(hot_place[2 * t + n], lc["iota"], place_of[:, t, n:n + 1], None, ALU.is_equal))
                    dve.tensor_scalar(hot_tile[2 * t + n], lc["iota"][:, 0:24], tile_of[:, t, n:n + 1],
                                      lc["tokid"][:, t:t + 1], ALU.is_equal, ALU.mult
                                      ).then_inc(hot_slots_ready, 1)
            te = hmf[0:1, 512:512 + 24 * N_EXP].rearrange("p (s e) -> p s e", e=N_EXP)
            tf = hmf[0:1, 1024:1048]
            link(dve.tensor_tensor(te, ends[0:1, :].rearrange("p (a e) -> p a e", a=1).to_broadcast([1, 24, N_EXP]),
                                   lc["iota"][0:1, 0:24].rearrange("p (s a) -> p s a", a=1)
                                   .to_broadcast([1, 24, N_EXP]), ALU.is_le))
            link(dve.tensor_reduce(tf, te, AX.X, ALU.add))
            dve.tensor_scalar(tile_expert[:, :], tf, float(N_EXP - 1), None, ALU.min).then_inc(tiles_ready, 1)
            wait_full(dve, "ids")
            emptied(dve.tensor_copy(ids[:, :], bank("ids", 24)))

            def empty_x():
                dve.tensor_copy(xsT[:, 4:8, :], psum[:, 4, :].rearrange("p (k t) -> p k t", k=4)
                                ).then_inc(xT_dve, 1)

            def gated(q):
                dve.tensor_tensor(he[:, q, :], sg[:, q, :], psum[:, 1, :], ALU.mult).then_inc(he_ready, 1)

            def empty_y(q):
                dve.tensor_copy(ybuf[:, q, COLS:D], psum[:, 6, :]).then_inc(y_dve, 1)

            dve.wait_ge(xT_full, 1)
            empty_x()
            dve.wait_ge(silu_done, 1)
            dve.wait_ge(up_full, 1)
            gated(0)
            for s in (1, 2):
                dve.wait_ge(xT_full, s + 1)
                empty_x()
                dve.wait_ge(silu_done, s + 1)
                dve.wait_ge(up_full, s + 1)
                dve.wait_ge(heT_full, s - 1) if s >= 2 else None
                gated(s % 2)
                dve.wait_ge(down_full, s)
                empty_y((s - 1) % 2)
            with dve.Fori(1, (MOE_TILES - 1) // 2) as i:
                for n in range(2):
                    q = (1 + n) % 2
                    s = i * 2 + (1 + n)
                    dve.wait_ge(xT_full, s + 1)
                    empty_x()
                    dve.wait_ge(silu_done, s + 1)
                    dve.wait_ge(up_full, s + 1)
                    dve.wait_ge(heT_full, s - 1)
                    gated(q)
                    dve.wait_ge(down_full, s)
                    dve.wait_ge(y_stored[1 - q], i * 16)
                    empty_y(1 - q)
            last = MOE_TILES - 1
            dve.wait_ge(down_full, last + 1)
            dve.wait_ge(y_stored[last % 2], 16 * (last // 2))
            empty_y(last % 2)

            for t in range(TT):
                a, b = pair[(2 * t) % 4], pair[(2 * t + 1) % 4]
                for n in range(2):
                    dve.wait_ge(pair_landed[(2 * t + n) % 4], 16 * (t // 2 + 1))
                link(dve.tensor_scalar(a, a, topw[:, t, 0:1], None, ALU.mult))
                link(dve.scalar_tensor_tensor(out=a, in0=b, scalar=topw[:, t, 1:2], in1=a, op0=ALU.mult, op1=ALU.add))
                link(dve.tensor_tensor(a, a, g2b[:, t // TPR, :], ALU.mult))
                dve.tensor_tensor(xbuf[:, t, :], xbuf[:, t, :], a, ALU.add).then_inc(x2_ready, 1)
            dve.wait_ge(fgain_landed, 16)
            for t in range(TT):
                dve.wait_ge(x2_root, t + 1)
                link(dve.reciprocal(small[:, 48 + t:49 + t], small[:, 52 + t:53 + t]))
                dve.scalar_tensor_tensor(out=xbuf[:, t, :], in0=xbuf[:, t, :], scalar=small[:, 48 + t:49 + t],
                                         in1=fgain, op0=ALU.mult, op1=ALU.mult).then_inc(y_ready, 1)

        @block.gpsimd
        def _(pool):
            with nc.allow_non_contiguous_dma(reason="router weights"):
                pool.dma_start(router_w[:, :, 0:4], rg_w[0].rearrange("(k p) n -> p k n", p=P)).then_inc(router_landed, 16)
                pool.dma_start(router_w[:, :, 4:20], re_w[0].rearrange("(k p) n -> p k n", p=P)).then_inc(router_landed, 16)
            for b in range(12):
                if b >= 1:
                    wait_emptied(pool, f"ada{b - 1}")
                pool.dma_start(biasrow, ada_b[:, b * COLS:(b + 1) * COLS].to_broadcast([REQS, COLS])
                               ).then_inc(bias_landed, 16)
                if b == 5:
                    wait_full(pool, "oT3")
                    for r in range(REQS):
                        pool.dma_start(xbuf[:, 2 * r:2 * r + 2, :],
                                       x_in[r][0].rearrange("(t p) d -> p t d", p=P)).then_inc(x_again, 16)
                    wait_full(pool, "num7.1")
                    pool.dma_start(gain2, row_bcast(norm2_g[0])).then_inc(late_landed, 16)
                    pool.dma_start(late, late_consts).then_inc(late_landed, 16)
                if b == 9:
                    for t in range(TT):
                        pool.wait_ge(h2_ready, t + 1)
                        pool.dma_start(h2_rows[t * P:(t + 1) * P, :], h2[:, t % 2, :]).then_inc(h2_stored[t % 2], 16)
            wait_emptied(pool, "wo3.1")
            pool.dma_start(fgain, row_bcast(final_norm_g)).then_inc(fgain_landed, 16)

            for b in range(2):
                pool.wait_ge(h2_stored[b], 16 * (TT // 2))
            wait_emptied(pool, "ids")
            for s in range(MOE_TILES):
                if s >= 2:
                    pool.wait_ge(xT_full, s - 1)
                pool.indirect_dma_start(xs[:, s % 2, :], None, h2_rows,
                                        bass.IndirectOffsetOnAxis(ap=ids[:, s:s + 1], axis=0)
                                        ).then_inc(xs_landed[s % 2], 16)

            pool.wait_ge(y_stored[0], 16 * ((MOE_TILES + 1) // 2))
            pool.wait_ge(y_stored[1], 16 * (MOE_TILES // 2))
            for t in range(TT):
                for n in range(2):
                    if t >= 2:
                        pool.wait_ge(x2_ready, t - 1)
                    pool.indirect_dma_start(pair[(2 * t + n) % 4], None, y_rows,
                                            bass.IndirectOffsetOnAxis(ap=pos[:, t, n:n + 1], axis=0)
                                            ).then_inc(pair_landed[(2 * t + n) % 4], 16)


def shape_constants():
    f = np.float32
    i = np.arange(P)
    early = np.zeros((P, EARLY_W), f)
    late = np.zeros((P, LATE_W), f)

    def put(table, where, name, value):
        a, w = table[name]
        where[:, a:a + w] = value

    put(EARLY, early, "ident", np.eye(P, dtype=f))
    lower = np.where(i[None, :] >= i[:, None], 0.0, -BIG)
    upper = np.where(i[None, :] <= i[:, None], 0.0, -BIG)
    put(EARLY, early, "maskL", np.concatenate([lower, np.zeros((P, P))], 1))
    put(EARLY, early, "maskU", np.concatenate([np.zeros((P, P)), upper], 1))
    half = ROPE_DIM // 2
    inv = (f(1.0) / (f(ROPE_THETA) ** (np.arange(half, dtype=f) * f(2.0) / f(ROPE_DIM)))).astype(f)
    ang = (np.arange(SEQ, dtype=f)[None, :] * inv[:, None]).astype(f)
    cos, sin = np.cos(ang).astype(f), np.sin(ang).astype(f)
    ct, st, perm = np.ones((P, SEQ), f), np.zeros((P, SEQ), f), np.zeros((P, P), f)
    for base in range(0, P, A_HD):
        ct[base:base + half], ct[base + half:base + 2 * half] = cos, cos
        st[base:base + half], st[base + half:base + 2 * half] = -sin, sin
        for n in range(half):
            perm[base + half + n, base + n] = 1.0
            perm[base + n, base + half + n] = 1.0
    put(EARLY, early, "cos", ct)
    put(EARLY, early, "sin", st)
    put(EARLY, early, "perm", perm)
    put(LATE, late, "tri", (i[:, None] < i[None, :]).astype(f))
    put(LATE, late, "ones", 1.0)
    put(LATE, late, "iota", i[None, :].astype(f))
    put(LATE, late, "iota4", (np.arange(4) - 64.0)[None, :])
    put(LATE, late, "tokid", i[:, None] + P * np.arange(TT)[None, :])
    return {"early_consts": early, "late_consts": late}


INPUTS = ["x_prompt", "x_sample", "c_prompt", "c_sample", "ada_w", "ada_b", "norm1_g", "w_in", "conv_w",
          "m_gate_b", "attn_sink", "head_norm_g", "w_up_attn", "w_up_mlstm", "w_out", "norm2_g", "rg_w",
          "rg_b", "re_w", "re_b", "w_gate", "w_up", "w_down", "final_norm_g"]


def kernel(**inputs):
    import concourse.bacc as bacc
    from concourse.bass_utils import run_bass_kernel_spmd

    nc = bacc.Bacc("TRN2", target_bir_lowering=False, num_devices=1, dynamic_dma_scratch_size=SCRATCH)
    arrays = {name: np.ascontiguousarray(inputs[name]) for name in INPUTS}
    arrays.update(shape_constants())
    args = [nc.dram_tensor(n, a.shape, mybir.dt.from_np(a.dtype), kind="ExternalInput").ap()
            for n, a in arrays.items()]
    for name in ("y_prompt", "y_sample"):
        args.append(nc.dram_tensor(name, (1, SEQ, D), F32, kind="ExternalOutput").ap())
    hybrid_layer(nc, *args)
    r = run_bass_kernel_spmd(nc, [arrays], core_ids=[0])
    return r.results[0]["y_prompt"], r.results[0]["y_sample"]
```

```python
from contextlib import ExitStack

import numpy as np
import concourse.bass as bass
from concourse import mybir

F32 = mybir.dt.float32
F32R = mybir.dt.float32r
I32 = mybir.dt.int32
U32 = mybir.dt.uint32
ALU = mybir.AluOpType
ACT = mybir.ActivationFunctionType
AX = mybir.AxisListType

P = 128
D = 1024
KD = D // P
REQS, SEQ = 2, 256
TOK = REQS * SEQ
TT = TOK // P
TPR = SEQ // P
COLS = 512

A_HEADS, A_KV, A_HD = 8, 2, 64
PAIRS = A_HEADS // A_KV
ROPE_DIM, ROPE_THETA = 16, 500000.0
M_HEADS, M_HD = 4, 128
KM = M_HEADS
VW = M_HD + 1

OFF_AQ, OFF_AK, OFF_MQ, OFF_MK = 0, 512, 768, 1280
OFF_MV, OFF_MO, OFF_MG, OFF_BG = 1792, 2304, 2816, 2832

N_GRP, PER_GRP = 4, 4
N_EXP = N_GRP * PER_GRP
D_EXP = 512
KF = D_EXP // P
MAX_TILES = (2 * TOK + N_EXP * (P - 1)) // P
MAX_PAIRS = (MAX_TILES + 1) // 2
MIN_PAIRS = 2 * TOK // P // 2
EPS = 1e-6
BIG = 1e30

SMALL_LOADS = 11
RAW_SLOTS = 4
SPLIT_SLOTS = 2
PIECE = 1024
GAINS = 88
QUAD = 32
SCRATCH = 4096

EARLY = {"ident": (0, 128), "maskL": (128, 256), "maskU": (256, 256), "cos": (512, 256),
         "sin": (768, 256), "perm": (1024, 128), "pick": (1152, 2), "one": (1154, 1)}
EARLY_W = 1155
LATE = {"tri": (0, 128), "ones": (128, 128), "iota": (256, 128), "iota4": (384, 4), "tokid": (388, 4)}
LATE_W = 392

def list_pieces():
    pieces = [(f"ada{b}", j) for b in range(4) for j in range(4)]
    pieces += [("ak", 0), ("av", 0), ("mg", 0)]
    ada = iter([(f"ada{b}", j) for b in range(4, 12) for j in range(4)])
    for name, beside in (("aq", (1, 1, 1, 1)), ("mq", (2, 1, 2, 1)), ("mk", (2, 1, 2, 1)),
                         ("mv", (2, 2, 2, 2)), ("mo", (2, 2, 2, 2))):
        for j in range(4):
            pieces.append((name, j))
            pieces += [next(ada) for _ in range(beside[j])]
    pieces += [(name, j) for name in ("bg0", "bg1", "bg2", "bg3", "upa", "upm", "wo0", "wo1")
               for j in range(4)]
    return pieces


PIECES = list_pieces()
SPLITS = [p for p in PIECES if not p[0].startswith("ada")]


def projection_steps():
    steps, turn = [], None
    for name, j in PIECES[16:PIECES.index(("bg0", 0))]:
        steps.append(("piece", (name, j)))
        if name.startswith("ada"):
            turn = int(name[3:]) if j == 3 else turn
            continue
        if name == "aq":
            steps.append(("swap", j))
        elif (name, j) == ("mq", 0):
            steps.append(("swap", 4))
        elif (name, j) == ("mv", 3):
            steps.append(("gateT", None))
        if turn is not None:
            steps.append(("turn", turn))
            turn = None
    steps.append(("turn", turn))
    return steps


STEPS = projection_steps()


def finished_by(name, j):
    if name.startswith("ada"):
        return [(name, "v")] if j == 3 else []
    if name in ("mv", "mo"):
        return [(f"{name}{t}", "s") for t in range(TT)] if j == 3 else []
    if name in ("wo0", "wo1"):
        return [(f"wo{t}.{name[2]}", "v") for t in range(TT)] if j == 3 else []
    if name in ("upa", "upm"):
        return [(f"{name}{2 * j + n}", "v") for n in range(2)]
    if name in ("mq", "mk"):
        return [(f"conv{j + 4 * (name == 'mk')}", "v")]
    if name.startswith("bg"):
        return [(f"bg{4 * int(name[2:]) + j}", "s")]
    return [{"ak": ("raw0", "s"), "av": ("av", "s"), "mg": ("gates", "v"), "aq": (f"raw{j + 1}", "s")}[name]]


def list_groups():
    g = [("cT", "v"), ("gainT", "v"), ("ada0", "v"), ("ada1", "v"), ("modT0", "v"), ("ada2", "v"),
         ("modT1", "v"), ("ada3", "v"), ("modT2", "v"), ("modT3", "v")]
    g += [(f"xT{k}", "s") for k in range(KD)]
    for kind, what in STEPS:
        g += {"piece": lambda: finished_by(*what), "swap": lambda: [(f"swap{what}", "v")],
              "turn": lambda: [(f"modT{what}", "v")], "gateT": lambda: [("gateT", "s")]}[kind]()
    for b in range(TT):
        bg = [(f"bg{4 * b + n}", "s") for n in range(4)]
        g += [(f"score{b}.{j}", "v") for j in range(PAIRS)]
        g += [(f"mrow{2 * b}", "v"), (f"qk{2 * b}", "v"), bg[0], bg[1]]
        g += [(f"pT{b}.{n}", "vs"[n % 2]) for n in range(4)]
        g += [(f"num{2 * b}.0", "v"), (f"num{2 * b}.1", "v")]
        g += [(f"mrow{2 * b + 1}", "v"), (f"qk{2 * b + 1}", "v"), bg[2], (f"pv{b}", "v")]
        g += [(f"num{2 * b + 1}.0", "v"), (f"num{2 * b + 1}.1", "v"), bg[3], (f"oT{b}", "s")]
    g += [(f"spread{b}.{r}", "s") for b in range(4, 8) for r in range(REQS)]
    g += [(f"upa{j}", "v") for j in range(KD)]
    g += [(f"mT{t}", "v") for t in range(TT)]
    g += [(f"upm{j}", "v") for j in range(KD)]
    g += [(f"spread{b}.{r}", "s") for b in range(8, 10) for r in range(REQS)]
    g += [(f"wo{t}.{h}", "v") for h in range(2) for t in range(TT)]
    for t in range(TT):
        g += [(f"h2T{t}.0", "s"), (f"h2T{t}.1", "s"), (f"logit{t}", "v")]
    g += [(f"spread{b}.{r}", "s") for b in range(10, 12) for r in range(REQS)]
    g += [("rank", "v"), ("ids", "v")]
    return g


GROUPS = list_groups()
INDEX = {name: n for n, (name, _) in enumerate(GROUPS)}
BANKS = 8


def emptied_count(name):
    n = INDEX[name]
    return sum(1 for _, e in GROUPS[:n + 1] if e == GROUPS[n][1])


PARTS = [p for p in PIECES if not finished_by(*p)]
SPREADS = [name for name, _ in GROUPS if name.startswith("spread")]


def hybrid_layer(nc, x_prompt, x_sample, c_prompt, c_sample, ada_w, ada_b, norm1_g, w_in, conv_w,
                 m_gate_b, attn_sink, head_norm_g, w_up_attn, w_up_mlstm, w_out, norm2_g, rg_w,
                 rg_b, re_w, re_b, w_gate, w_up, w_down, final_norm_g, early_consts, late_consts,
                 y_prompt, y_sample):
    ctx = ExitStack()
    with ctx:
        address = {}

        def sb(name, shape, dt=F32):
            address[name] = (nc.sbuf_base + 31) // 32 * 32
            return ctx.enter_context(nc.sbuf_tensor(name, shape, dt))

        def placed_over(name, place, first, shape, dt=F32R):
            return nc.alloc_sbuf_tensor_at(name, shape, dt, offset=address[place] + 4 * first)

        def sem(name):
            return ctx.enter_context(nc.semaphore(name))

        x_in = [x_prompt, x_sample]
        y_out = [y_prompt, y_sample]

        front_ring = sb("front_ring", [P, 3, 4096])
        raw_ring = front_ring[:, 0, :].rearrange("p (s n) -> p s n", s=RAW_SLOTS)
        high_ring = placed_over("high_ring", "front_ring", 4096, [P, SPLIT_SLOTS, PIECE])
        low_ring = placed_over("low_ring", "front_ring", 4096 + SPLIT_SLOTS * PIECE, [P, SPLIT_SLOTS, PIECE])
        h_low = placed_over("h_low", "front_ring", 8192, [P, KD, TOK])
        slot3 = sb("slot3", [P, 4096])
        slots45 = sb("slots45", [P, 2, 4096])
        xbuf = sb("xbuf", [P, TT, D])
        inout = sb("inout", [P, 4096])
        h_high = placed_over("h_high", "inout", 0, [P, KD, TOK])
        g1b = sb("g1b", [P, REQS, D])
        rot_pT = sb("rot_pT", [P, 5120])
        rot_v = rot_pT[:, 0:3072]
        pTflat = rot_pT[:, 3072:5120]
        mqk = sb("mqk", [P, 8, TOK])
        mvb = sb("mvb", [P, TT, M_HEADS, VW])
        og = sb("og", [P, TT, COLS])
        pTb = pTflat.rearrange("p (a b) -> p a b", a=16)
        hm = sb("hm", [P, TT, COLS])
        oT = sb("oT", [P, KM, TOK])
        tmp = sb("tmp", [P, COLS])
        modrow = sb("modrow", [P, 2, COLS])
        early = sb("early", [P, EARLY_W])
        hng = sb("hng", [P, COLS])
        cT = sb("cT", [P, KD, QUAD])
        gainT = sb("gainT", [P, GAINS])
        modT = sb("modT", [P, 12, 4, REQS])
        scale1 = sb("scale1", [P, KD, REQS])
        small = sb("small", [P, 64])
        sink = sb("sink", [P, A_HEADS])
        nsink = sb("nsink", [P, A_HEADS])
        stat = sb("stat", [P, 2, 8, A_HEADS])
        gateT = sb("gateT", [P, 2, 2, TT, M_HEADS])
        mstat = sb("mstat", [P, 2, 2, 2])
        gbias = sb("gbias", [M_HEADS, 4])
        router_b = sb("router_b", [P, 20])
        eps = sb("eps", [P, 1])

        psum = ctx.enter_context(nc.psum_tensor("psum", [P, BANKS, COLS], F32))
        h2_rows = nc.dram_tensor("h2_rows", [TOK, D], F32, kind="Internal").ap()
        y_rows = nc.dram_tensor("y_rows", [2 * MAX_PAIRS * P, D], F32, kind="Internal").ap()

        ebuf = g1b[:, :, :].rearrange("p r d -> p (r d)")[:, 0:1536].rearrange(
            "p (b d n) -> p b d n", b=2, d=2)
        crow = hm[0:REQS, 0:2, :].rearrange("p a b -> p (a b)")
        gains = slot3[0:GAINS, 3840:3968]
        def const(name):
            a, w = EARLY[name]
            return early[:, a:a + w]

        ident, perm = const("ident"), const("perm")
        rows = slot3[0:M_HEADS, 0:2048].rearrange("p (g t) -> p g t", g=4)
        rows_x = slot3[0:M_HEADS, 2048:3072].rearrange("p (g t) -> p g t", g=2)
        ones_row = slot3[0:M_HEADS, 3072:3328]
        bgate = slots45[:, :, :].rearrange("p s (c t) -> p (s c) t", t=TOK)
        probs = xbuf[:, :, :].rearrange("p (b a) n -> p b (a n)", b=2).rearrange(
            "p b (h k) -> p b h k", h=A_HEADS)
        rot = rot_v[:, 0:2560].rearrange("p (c t) -> p c t", c=5)
        av = rot_v[:, 2560:3072].rearrange("p (t f) -> p t f", t=TT)
        o_parts = [h_high[:, 0:KM, :], h_high[:, KM:KD, :]]
        m_parts = [h_low[:, 0:KM, :], h_low[:, KM:KD, :]]
        merged = [placed_over("merged_high", "slots45", 4096, [P, KD, TOK]),
                  placed_over("merged_low", "rot_pT", 0, [P, KD, TOK])]
        hbuf = [pTflat[:, n * 512:(n + 1) * 512] for n in range(4)]
        raw = [pTflat[:, n * 512:(n + 1) * 512] for n in range(2)]
        acc = [pTflat[:, 1024 + n * 512:1536 + n * 512] for n in range(2)]
        mqkf = mqk[:, :, :].rearrange("p a b -> p (a b)")
        scale2 = mqkf[:, 0:2048].rearrange("p (r d) -> p r d", r=REQS)
        shift2 = mqkf[:, 2048:4096].rearrange("p (r d) -> p r d", r=REQS)
        g2b = og[:, :, :].rearrange("p a b -> p (a b)").rearrange("p (r d) -> p r d", r=REQS)
        mvf = mvb[:, :, :, :].rearrange("p a b c -> p (a b c)")
        late = mvf[:, D:D + LATE_W]
        lc = {n: late[:, a:a + w] for n, (a, w) in LATE.items()}
        route = mvf[:, D + LATE_W:D + LATE_W + 640]
        h2 = pTflat.rearrange("p (b d) -> p b d", b=2)
        hmf = hm[:, :, :].rearrange("p a b -> p (a b)")
        h2T = hmf.rearrange("p (b k t) -> p b k t", b=2, k=KD)
        hTf = inout[:, :]
        xs = hTf[:, 0:2048].rearrange("p (b d) -> p b d", b=2)
        ybuf = hTf[:, 2048:4096].rearrange("p (b d) -> p b d", b=2)
        xsT = rot_v[:, 0:1024].rearrange("p (k t) -> p k t", k=KD)
        sg = rot_v[:, 1024:2048].rearrange("p (b f) -> p b f", b=2)
        oTf = oT[:, :, :].rearrange("p a b -> p (a b)")
        he = oTf[:, 0:1024].rearrange("p (b f) -> p b f", b=2)
        heT = oTf[:, 1024:1536].rearrange("p (k t) -> p k t", k=KF)
        router_w = oTf[:, 1536:1696].rearrange("p (k n) -> p k n", k=KD)
        fgain = g1b[:, 0, :]
        junk = g1b[:, 1, :]
        sqjunk = hTf[:, 0:1024]
        pair = [mqkf[:, n * D:(n + 1) * D] for n in range(4)]
        ids = placed_over("ids", "mvb", 0, [P, 2 * MAX_PAIRS], U32)
        pos = sb("pos", [P, TT, 2], U32)
        topw = mvf[:, 32:40].rearrange("p (t n) -> p t n", n=2)
        tile_expert = sb("tile_expert", [1, 2 * MAX_PAIRS + 1], I32)

        hot_place = [pTflat[:, n * P:(n + 1) * P] for n in range(2 * TT)]
        ids_now = sb("ids_now", [P, 2], U32)
        hot_tile = [route[:, 256 + n * 24:280 + n * 24] for n in range(2 * TT)]

        moe_slot = [slot3[:, :], slots45[:, 0, :], front_ring[:, 1, :], slots45[:, 1, :],
                    front_ring[:, 2, :], front_ring[:, 0, :]]

        landed = [sem(f"landed{i}") for i in range(RAW_SLOTS)]
        part_used = sem("part_used")
        high_ready = sem("high_ready")
        low_ready = sem("low_ready")
        h_high_ready = sem("h_high_ready")
        h_ready = sem("h_ready")
        oT_high = sem("oT_high")
        oT_ready = sem("oT_ready")
        mT_high = sem("mT_high")
        merged_high = sem("merged_high")
        merged_ready = sem("merged_ready")
        diag_ready = sem("diag_ready")
        moe_landed = [sem(f"moe_landed{i}") for i in range(6)]
        x_landed = sem("x_landed")
        x_again = sem("x_again")
        small_landed = sem("small_landed")
        early_landed = sem("early_landed")
        late_landed = sem("late_landed")
        router_landed = sem("router_landed")
        fgain_landed = sem("fgain_landed")
        psum_full = sem("psum_full")
        dve_emptied = sem("dve_emptied")
        act_emptied = sem("act_emptied")
        dve_chain = sem("dve_chain")
        act_chain = sem("act_chain")
        pool_chain = sem("pool_chain")
        c_ready = sem("c_ready")
        xsq_ready = sem("xsq_ready")
        xn_ready = sem("xn_ready")
        conv_done = sem("conv_done")
        forget_abs = sem("forget_abs")
        forget_ln = sem("forget_ln")
        rows_ready = sem("rows_ready")
        ones_ready = sem("ones_ready")
        negmax_ready = sem("negmax_ready")
        probs_ready = sem("probs_ready")
        decay_ready = sem("decay_ready")
        hm_sq = sem("hm_sq")
        hm_root = sem("hm_root")
        hm_ready = sem("hm_ready")
        x1_root = sem("x1_root")
        h2_ready = sem("h2_ready")
        h2_stored = [sem(f"h2_stored{i}") for i in range(2)]
        gate_sum = sem("gate_sum")
        gate_exp = sem("gate_exp")
        onehots_ready = sem("onehots_ready")
        hot_slots_ready = sem("hot_slots_ready")
        tiles_ready = sem("tiles_ready")
        zeros_ready = sem("zeros_ready")
        zeros_stored = sem("zeros_stored")
        rows_stored = sem("rows_stored")
        xs_landed = [sem(f"xs_landed{i}") for i in range(2)]
        xT_full = sem("xT_full")
        xT_act = sem("xT_act")
        xT_dve = sem("xT_dve")
        gate_full = sem("gate_full")
        up_full = sem("up_full")
        silu_done = sem("silu_done")
        he_ready = sem("he_ready")
        heT_full = sem("heT_full")
        heT_emptied = sem("heT_emptied")
        down_full = sem("down_full")
        y_act = sem("y_act")
        y_dve = sem("y_dve")
        y_stored = [sem(f"y_stored{i}") for i in range(2)]
        pair_landed = [sem(f"pair_landed{i}") for i in range(4)]
        x2_ready = sem("x2_ready")
        x2_root = sem("x2_root")
        y_ready = sem("y_ready")
        out_stored = sem("out_stored")

        slot_count, piece_landed = [0] * RAW_SLOTS, []
        for n, (name, _) in enumerate(PIECES):
            slot_count[n % RAW_SLOTS] += 16 * (2 if name == "aq" else 1)
            piece_landed.append(slot_count[n % RAW_SLOTS])

        def raw_piece(piece):
            return raw_ring[:, PIECES.index(piece) % RAW_SLOTS, :]

        def wait_piece(eng, piece):
            n = PIECES.index(piece)
            eng.wait_ge(landed[n % RAW_SLOTS], piece_landed[n])

        def split_piece(piece, k):
            n = SPLITS.index(piece) % SPLIT_SLOTS
            return [ring[:, n, :].rearrange("p (k n) -> p k n", k=k) for ring in (high_ring, low_ring)]

        def wait_used(eng, piece):
            if piece in PARTS:
                eng.wait_ge(part_used, PARTS.index(piece) + 1)
            else:
                wait_full(eng, finished_by(*piece)[-1][0])

        def bank(name, width=COLS):
            return psum[:, INDEX[name] % BANKS, 0:width]

        def wait_full(eng, name):
            eng.wait_ge(psum_full, INDEX[name] + 1)

        def wait_emptied(eng, name):
            eng.wait_ge(dve_emptied if GROUPS[INDEX[name]][1] == "v" else act_emptied,
                        emptied_count(name))

        def wait_bank(eng, name):
            if INDEX[name] >= BANKS:
                wait_emptied(eng, GROUPS[INDEX[name] - BANKS][0])

        def row_bcast(ap, n=P):
            return ap.rearrange("(a n) -> a n", a=1).to_broadcast([n, ap.shape[0]])

        def load_last_pair(eng):
            eng.wait_ge(tiles_ready, 1)
            return eng.value_load(tile_expert[0:1, 2 * MAX_PAIRS:2 * MAX_PAIRS + 1],
                                  min_val=MIN_PAIRS - 1, max_val=MAX_PAIRS - 1)

        block = ctx.enter_context(nc.Block())

        @block.sync
        def _(sp):
            for r in range(REQS):
                sp.dma_start(xbuf[:, 2 * r:2 * r + 2, :],
                             x_in[r][0].rearrange("(t p) d -> p t d", p=P)).then_inc(x_landed, 16)
            def load_piece(piece):
                name, j = piece
                n = PIECES.index(piece)
                slot, done = raw_piece(piece), landed[n % RAW_SLOTS]
                deep = slot.rearrange("p (k n) -> p k n", k=2)
                if name.startswith("ada"):
                    src = ada_w[0, :, int(name[3:]) * COLS:(int(name[3:]) + 1) * COLS]
                elif name in ("wo0", "wo1"):
                    src = w_out[0, :, int(name[2]) * COLS:(int(name[2]) + 1) * COLS]
                elif name in ("mv", "mo"):
                    a = OFF_MV if name == "mv" else OFF_MO
                    src = w_in[0, :, a:a + COLS]
                elif name in ("upa", "upm"):
                    src = (w_up_attn if name == "upa" else w_up_mlstm)[0, :, j * 256:(j + 1) * 256]
                    sp.dma_start(slot.rearrange("p (k n) -> p k n", k=KM),
                                 src.rearrange("(k p) n -> p k n", p=P)).then_inc(done, 16)
                    return
                else:
                    wide = slot.rearrange("p (k n) -> p k n", k=KD)
                    if name == "aq":
                        for n, h in enumerate((j, j + PAIRS)):
                            sp.dma_start(wide[:, :, n * A_HD:(n + 1) * A_HD],
                                         w_in[0, :, OFF_AQ + h * A_HD:OFF_AQ + (h + 1) * A_HD]
                                         .rearrange("(k p) n -> p k n", p=P)).then_inc(done, 16)
                        return
                    if name == "mg":
                        a, wide = OFF_MG, slot[:, 0:KD * 16].rearrange("p (k n) -> p k n", k=KD)
                    elif name.startswith("bg"):
                        a = OFF_BG + (4 * int(name[2:]) + j) * P
                    else:
                        a = {"ak": OFF_AK, "av": OFF_AK + P, "mq": OFF_MQ, "mk": OFF_MK}[name] + j * P
                    sp.dma_start(wide, w_in[0, :, a:a + (16 if name == "mg" else P)]
                                 .rearrange("(k p) n -> p k n", p=P)).then_inc(done, 16)
                    return
                sp.dma_start(deep, src[j * 256:(j + 1) * 256, :].rearrange("(k p) n -> p k n", p=P)
                             ).then_inc(done, 16)

            for n, piece in enumerate(PIECES):
                if n >= RAW_SLOTS:
                    old = PIECES[n - RAW_SLOTS]
                    if old in SPLITS:
                        sp.wait_ge(low_ready, SPLITS.index(old) + 1)
                    else:
                        wait_used(sp, old)
                load_piece(piece)

            def expert(s):
                return sp.value_load(tile_expert[0:1, bass.ds(s, 1)], min_val=0, max_val=N_EXP - 1)

            def load_in(e, q, which):
                w = (w_gate, w_up)[which]
                sp.dma_start(moe_slot[3 * q + which],
                             w[0, bass.ds(e, 1)].rearrange("e (p k) n -> (e p) (k n)", k=KD)
                             ).then_inc(moe_landed[3 * q + which], 16)

            def load_down(e, q):
                sp.dma_start(moe_slot[3 * q + 2],
                             w_down[0, bass.ds(e, 1)].rearrange("e (p k) n -> (e p) (k n)", k=KF)
                             ).then_inc(moe_landed[3 * q + 2], 16)

            last_pair = load_last_pair(sp)
            before = expert(0)
            load_in(before, 0, 0)
            wait_full(sp, "wo3.1")
            load_in(before, 0, 1)
            e = expert(1)
            load_in(e, 1, 0)
            load_in(e, 1, 1)
            load_down(before, 1)

            def tile_loads(s, q):
                e, before = expert(s), expert(s - 1)
                sp.wait_ge(gate_full, s - 1)
                load_in(e, q, 0)
                sp.wait_ge(up_full, s - 1)
                load_in(e, q, 1)
                sp.wait_ge(xT_full, s)
                load_down(before, q)

            with sp.Fori(1, last_pair + 1) as i:
                tile_loads(i * 2, 0)
                tile_loads(i * 2 + 1, 1)
            e = expert(last_pair * 2 + 1)
            sp.wait_ge(down_full, last_pair * 2)
            load_down(e, 0)

        @block.tensor
        def _(pe):
            def product(name, out, lhs, rhs, count):
                for k in range(count):
                    mm = pe.matmul(out, lhs(k), rhs(k), start=(k == 0), stop=(k == count - 1))
                mm.then_inc(psum_full, 1)

            def split_product(out, lhs, rhs, count, start=True, stop=True):
                for k in range(count):
                    for a, b in ((1, 0), (0, 1), (0, 0)):
                        mm = pe.matmul(out, lhs(a, k), rhs(b, k), start=(start and k == 0 and a == 1),
                                       stop=(stop and k == count - 1 and (a, b) == (0, 0)))
                return mm

            h_parts = [h_high, h_low]

            def wait_split(piece):
                pe.wait_ge(low_ready, SPLITS.index(piece) + 1)

            def columns_out(piece):
                name = finished_by(*piece)[0][0]
                wait_bank(pe, name)
                wait_split(piece)
                w = split_piece(piece, KD)
                split_product(bank(name), lambda a, k: w[a][:, k, :], lambda b, k: h_parts[b][:, k, :], KD
                              ).then_inc(psum_full, 1)

            def tokens_out(piece, names, parts):
                j = piece[1]
                if j == 0:
                    for name in names:
                        wait_bank(pe, name)
                wait_split(piece)
                w = split_piece(piece, 2)
                for t, name in enumerate(names):
                    mm = split_product(bank(name), lambda a, k: parts[a][:, 2 * j + k, t * P:(t + 1) * P],
                                       lambda b, k: w[b][:, k, :], 2, start=(j == 0), stop=(j == 3))
                    if j == 3:
                        mm.then_inc(psum_full, 1)
                if j < 3:
                    mm.then_inc(part_used, 1)

            def widen(piece, parts):
                wait_split(piece)
                w = split_piece(piece, KM)
                for n, (name, _) in enumerate(finished_by(*piece)):
                    wait_bank(pe, name)
                    split_product(bank(name), lambda a, k: w[a][:, k, n * P:(n + 1) * P],
                                  lambda b, k: parts[b][:, k, :], KM).then_inc(psum_full, 1)

            def transposes(name, srcs, idn=None):
                wait_bank(pe, name)
                out = bank(name).rearrange("p (n t) -> p n t", t=P)
                for n, s in enumerate(srcs):
                    mm = pe.transpose(out[:, n, :], s, ident)
                mm.then_inc(psum_full, 1)

            def ada(piece):
                name, j = piece
                if j == 0:
                    wait_bank(pe, name)
                wait_piece(pe, piece)
                w = raw_piece(piece).rearrange("p (k n) -> p k n", k=2)
                for n in range(2):
                    g = (2 * j + n) % 4
                    mm = pe.matmul(bank(name)[g * QUAD:(g + 1) * QUAD, :], cT[:, 2 * j + n, :], w[:, n, :],
                                   start=(j < 2), stop=(j >= 2))
                mm.then_inc(psum_full if j == 3 else part_used, 1)

            def mod_turn(b):
                name = f"modT{b}"
                wait_bank(pe, name)
                wait_emptied(pe, f"ada{b}")
                for c in range(4):
                    mm = pe.matmul(bank(name)[:, c * REQS:(c + 1) * REQS],
                                   modrow[:, b % 2, c * P:(c + 1) * P], const("pick"), start=True, stop=True)
                mm.then_inc(psum_full, 1)

            def spread(first, last):
                for b in range(first, last):
                    for r in range(REQS):
                        name = f"spread{b}.{r}"
                        n = SPREADS.index(name)
                        wait_bank(pe, name)
                        pe.wait_ge(diag_ready, n + 1)
                        pe.matmul(bank(name), const("one").to_broadcast([P, P]), modrow[:, n % 2, :],
                                  start=True, stop=True).then_inc(psum_full, 1)

            pe.wait_ge(early_landed, 16)
            pe.wait_ge(c_ready, 1)
            for k in range(KD):
                mm = pe.transpose(bank("cT")[:, k * REQS:(k + 1) * REQS], crow[:, k * P:(k + 1) * P],
                                  ident[0:REQS, 0:REQS])
            mm.then_inc(psum_full, 1)
            pe.wait_ge(small_landed, 16 * SMALL_LOADS)
            pe.transpose(bank("gainT", GAINS), gains, ident[0:GAINS, 0:GAINS]).then_inc(psum_full, 1)
            wait_emptied(pe, "cT")
            for b in range(4):
                for j in range(4):
                    ada((f"ada{b}", j))
                if b >= 1:
                    mod_turn(b - 1)
            mod_turn(3)
            pe.wait_ge(xn_ready, TT)
            for k in range(KD):
                transposes(f"xT{k}", [xbuf[:, t, k * P:(k + 1) * P] for t in range(TT)])
            pe.wait_ge(h_ready, KD)

            def attention_values(piece):
                wait_bank(pe, "av")
                wait_split(piece)
                w = split_piece(piece, KD)
                for t in range(TT):
                    mm = split_product(bank("av")[:, t * P:(t + 1) * P],
                                       lambda a, k: h_parts[a][:, k, t * P:(t + 1) * P],
                                       lambda b, k: w[b][:, k, :], KD)
                mm.then_inc(psum_full, 1)

            def swap(n):
                wait_bank(pe, f"swap{n}")
                wait_emptied(pe, f"raw{n}")
                pe.matmul(bank(f"swap{n}"), perm, raw[n % 2], start=True, stop=True).then_inc(psum_full, 1)

            def turn_gates():
                pe.wait_ge(rows_ready, 1)
                wait_bank(pe, "gateT")
                for kind in range(2):
                    for d in range(2):
                        for t in range(TT):
                            c = ((kind * 2 + d) * TT + t) * M_HEADS
                            src = rows if kind == 0 else rows_x
                            mm = pe.transpose(bank("gateT")[:, c:c + M_HEADS], src[:, d, t * P:(t + 1) * P],
                                              ident[0:M_HEADS, 0:M_HEADS])
                mm.then_inc(psum_full, 1)

            for kind, what in STEPS:
                if kind == "swap":
                    swap(what)
                elif kind == "turn":
                    mod_turn(what)
                elif kind == "gateT":
                    turn_gates()
                elif what[0].startswith("ada"):
                    ada(what)
                elif what[0] == "av":
                    attention_values(what)
                elif what[0] in ("mv", "mo"):
                    tokens_out(what, [f"{what[0]}{t}" for t in range(TT)], h_parts)
                else:
                    columns_out(what)

            def branch_gate(c):
                columns_out((f"bg{c // 4}", c % 4))

            def scores(b):
                r = b // TPR
                if b == 0:
                    wait_emptied(pe, "swap4")
                for n in range(A_HEADS // 2):
                    name = f"score{b}.{n}"
                    wait_bank(pe, name)
                    for h in (2 * n, 2 * n + 1):
                        at, j = h // PAIRS * A_HD, h % PAIRS
                        mm = pe.matmul(bank(name)[:, (h % 2) * SEQ:(h % 2 + 1) * SEQ],
                                       rot[at:at + A_HD, 1 + j, b * P:(b + 1) * P],
                                       rot[at:at + A_HD, 0, r * SEQ:(r + 1) * SEQ],
                                       start=True, stop=True)
                    mm.then_inc(psum_full, 1)

            def mlstm_scores(u):
                r, h = u // M_HEADS, u % M_HEADS
                name = f"mrow{u}"
                wait_bank(pe, name)
                for d in range(2):
                    mm = pe.matmul(bank(name)[:, d * SEQ:(d + 1) * SEQ],
                                   ident[0:M_HEADS, h:h + 1].to_broadcast([M_HEADS, P]),
                                   rows[:, 2 + d, r * SEQ:(r + 1) * SEQ], start=True, stop=True)
                mm.then_inc(psum_full, 1)
                if u == 0:
                    pe.wait_ge(conv_done, 8)
                name = f"qk{u}"
                wait_bank(pe, name)
                for s in range(TPR):
                    mm = pe.matmul(bank(name)[:, s * SEQ:(s + 1) * SEQ],
                                   mqk[:, 4 + h, r * SEQ + s * P:r * SEQ + (s + 1) * P],
                                   mqk[:, h, r * SEQ:(r + 1) * SEQ], start=True, stop=True)
                mm.then_inc(psum_full, 1)

            def mlstm_values(u):
                r, h = u // M_HEADS, u % M_HEADS
                wait_emptied(pe, f"qk{u}")
                if u == 0:
                    wait_emptied(pe, "mv3")
                    pe.wait_ge(ones_ready, 1)
                e = ebuf[:, u % 2]
                v = [mvb[:, r * TPR + s, h, :] for s in range(TPR)]
                plan = [[(0, [(0, 0)]), (1, [(128, 0), (256, 1)])],
                        [(0, [(0, 1), (256, 0)]), (1, [(128, 1)])]]
                for d in range(2):
                    name = f"num{u}.{d}"
                    wait_bank(pe, name)
                    for t, parts in plan[d]:
                        for n, (col, s) in enumerate(parts):
                            mm = pe.matmul(bank(name)[:, t * VW:(t + 1) * VW], e[:, d, col:col + P],
                                           v[s], start=(n == 0), stop=(n == len(parts) - 1))
                    mm.then_inc(psum_full, 1)

            def turn_probs(b):
                pe.wait_ge(probs_ready, b + 1)
                for n in range(4):
                    transposes(f"pT{b}.{n}", [probs[:, b % 2, 2 * n + i // 2, (i % 2) * P:(i % 2 + 1) * P]
                                              for i in range(4)])

            def attend(b):
                r = b // TPR
                wait_emptied(pe, f"pT{b}.2")
                wait_emptied(pe, f"pT{b}.3")
                if b == 0:
                    wait_emptied(pe, "av")
                wait_bank(pe, f"pv{b}")
                for h in range(A_HEADS):
                    for s in range(TPR):
                        kv = h // PAIRS
                        mm = pe.matmul(bank(f"pv{b}")[:, h * 64:(h + 1) * 64], pTb[:, 2 * h + s, :],
                                       av[:, r * TPR + s, kv * 64:(kv + 1) * 64],
                                       start=(s == 0), stop=(s == 1))
                mm.then_inc(psum_full, 1)

            for b in range(TT):
                scores(b)
                mlstm_scores(2 * b)
                branch_gate(4 * b)
                branch_gate(4 * b + 1)
                turn_probs(b)
                mlstm_values(2 * b)
                mlstm_scores(2 * b + 1)
                branch_gate(4 * b + 2)
                attend(b)
                mlstm_values(2 * b + 1)
                branch_gate(4 * b + 3)
                wait_emptied(pe, f"pv{b}")
                o = probs[:, b % 2].rearrange("p h k -> p (h k)")
                transposes(f"oT{b}", [o[:, k * P:(k + 1) * P] for k in range(KM)])

            spread(4, 8)
            pe.wait_ge(oT_ready, 2)
            for j in range(4):
                widen(("upa", j), o_parts)
            for t in range(TT):
                pe.wait_ge(hm_ready, t + 1)
                transposes(f"mT{t}", [hm[:, t, k * P:(k + 1) * P] for k in range(KM)])
            wait_emptied(pe, "mT3")
            for j in range(4):
                widen(("upm", j), m_parts)
            spread(8, 10)
            for h in range(2):
                for j in range(4):
                    if h == 0:
                        pe.wait_ge(merged_ready, 2 * j + 2)
                    tokens_out((f"wo{h}", j), [f"wo{t}.{h}" for t in range(TT)], merged)
            pe.wait_ge(router_landed, 16 * 2)
            for t in range(TT):
                pe.wait_ge(h2_ready, t + 1)
                for h in range(2):
                    transposes(f"h2T{t}.{h}", [h2[:, t % 2, (4 * h + n) * P:(4 * h + n + 1) * P]
                                               for n in range(4)])
                name = f"logit{t}"
                wait_bank(pe, name)
                wait_emptied(pe, f"h2T{t}.1")
                product(name, bank(name, 20), lambda k: h2T[:, t % 2, k, :],
                        lambda k: router_w[:, k, :], KD)
            spread(10, 12)

            pe.wait_ge(onehots_ready, 1)
            pe.wait_ge(late_landed, 16)
            name = "rank"
            wait_bank(pe, name)
            chosen = route[:, 128:192].rearrange("p (t e) -> p t e", t=TT)
            for t in range(TT + 1):
                out = bank(name)[:, t * N_EXP:(t + 1) * N_EXP]
                for b in range(min(t, TT)):
                    mm = pe.matmul(out, lc["ones"], chosen[:, b, :], start=(b == 0),
                                   stop=(t == TT and b == TT - 1))
                if t < TT:
                    mm = pe.matmul(out, lc["tri"], chosen[:, t, :], start=(t == 0), stop=True)
            mm.then_inc(psum_full, 1)
            name = "ids"
            wait_bank(pe, name)
            for n in range(2 * TT):
                pe.wait_ge(hot_slots_ready, n + 1)
                mm = pe.matmul(bank(name, 2 * MAX_PAIRS), hot_place[n], hot_tile[n], start=(n == 0),
                               stop=(n == 2 * TT - 1))
            mm.then_inc(psum_full, 1)

            bank_gate, bank_up, bank_heT = psum[:, 0, :], psum[:, 1, :], psum[:, 2, :]
            wait_emptied(pe, "ids")
            wait_emptied(pe, "rank")
            wait_emptied(pe, "spread11.1")

            def weights(q, part, k):
                return moe_slot[3 * q + part].rearrange("p (k n) -> p k n", k=k)

            def turn_x(s, q, nth):
                pe.wait_ge(xs_landed[q], 16 * nth)
                v = xs[:, q, :].rearrange("t (p k) -> t k p", k=KD)
                for k in range(KD):
                    mm = pe.transpose(psum[:, 3 + k // 4, (k % 4) * P:(k % 4 + 1) * P], v[:, k, :], ident)
                mm.then_inc(xT_full, 1)

            def expand(s, q, nth, part):
                w = weights(q, part, KD)
                out, done = (bank_gate, gate_full) if part == 0 else (bank_up, up_full)
                pe.wait_ge(moe_landed[3 * q + part], 16 * nth)
                for k in range(KD):
                    mm = pe.matmul(out, xsT[:, k, :], w[:, k, :], start=(k == 0), stop=(k == KD - 1))
                mm.then_inc(done, 1)

            def turn_he(q):
                v = he[:, q, :].rearrange("t (p k) -> t k p", k=KF)
                for k in range(KF):
                    mm = pe.transpose(bank_heT[:, k * P:(k + 1) * P], v[:, k, :], ident)
                mm.then_inc(heT_full, 1)

            def contract(q, nth):
                w = weights(q, 2, KF)
                pe.wait_ge(moe_landed[3 * q + 2], 16 * nth)
                for h in range(2):
                    for k in range(KF):
                        mm = pe.matmul(psum[:, 5 + h, :], heT[:, k, :], w[:, k, h * COLS:(h + 1) * COLS],
                                       start=(k == 0), stop=(k == KF - 1))
                mm.then_inc(down_full, 1)

            turn_x(0, 0, 1)
            pe.wait_ge(xT_act, 1)
            pe.wait_ge(xT_dve, 1)
            expand(0, 0, 1, 0)
            expand(0, 0, 1, 1)

            def tile_step(s, q, fills, fills_down, first=False):
                turn_x(s, q, fills)
                pe.wait_ge(he_ready, s)
                turn_he(1 - q)
                pe.wait_ge(xT_act, s + 1)
                pe.wait_ge(xT_dve, s + 1)
                pe.wait_ge(silu_done, s)
                expand(s, q, fills, 0)
                expand(s, q, fills, 1)
                pe.wait_ge(heT_emptied, s)
                if not first:
                    pe.wait_ge(y_act, s - 1)
                    pe.wait_ge(y_dve, s - 1)
                contract(q, fills_down)

            tile_step(1, 1, 1, 1, first=True)
            last_pair = load_last_pair(pe)
            with pe.Fori(1, last_pair + 1) as i:
                tile_step(i * 2, 0, i + 1, i)
                tile_step(i * 2 + 1, 1, i + 1, i + 1)
            pe.wait_ge(he_ready, last_pair * 2 + 2)
            turn_he(1)
            pe.wait_ge(heT_emptied, last_pair * 2 + 2)
            pe.wait_ge(y_act, last_pair * 2 + 1)
            pe.wait_ge(y_dve, last_pair * 2 + 1)
            contract(0, last_pair + 1)

        @block.scalar
        def _(act):
            steps = [0]

            def link(ins):
                steps[0] += 1
                ins.then_inc(act_chain, 1)
                act.wait_ge(act_chain, steps[0])

            act.dma_start(crow[0:1, :], c_prompt).then_inc(small_landed, 16)
            act.dma_start(crow[1:2, :], c_sample).then_inc(small_landed, 16)
            act.dma_start(early[:, :], early_consts).then_inc(early_landed, 16)
            act.dma_start(gains[0:KD, :], norm1_g.rearrange("a (k p) -> (a k) p", p=P)).then_inc(small_landed, 16)
            act.dma_start(gains[KD:32, :], conv_w[0].rearrange("w (k p) -> (w k) p", p=P)).then_inc(small_landed, 16)
            act.dma_start(gains[32:40, :], norm2_g.rearrange("a (k p) -> (a k) p", p=P)).then_inc(small_landed, 16)
            act.dma_start(gains[40:GAINS, :], ada_b.rearrange("a (k p) -> (a k) p", p=P)).then_inc(small_landed, 16)
            act.dma_start(sink[:, :], row_bcast(attn_sink[0])).then_inc(small_landed, 16)
            act.dma_start(hng[:, :], row_bcast(head_norm_g[0])).then_inc(small_landed, 16)
            act.dma_start(router_b[:, 0:4], row_bcast(rg_b[0])).then_inc(small_landed, 16)
            act.dma_start(router_b[:, 4:20], row_bcast(re_b[0])).then_inc(small_landed, 16)
            with nc.allow_non_contiguous_dma(reason="16 gate biases"):
                act.dma_start(gbias[:, :], m_gate_b[0].rearrange("(g h) -> h g", h=M_HEADS)).then_inc(small_landed, 16)
            act.wait_ge(small_landed, 16 * SMALL_LOADS)
            act.activation(crow, crow, ACT.Silu).then_inc(c_ready, 1)
            act.wait_ge(x_landed, 16 * REQS)
            act.wait_ge(ones_ready, 1)
            for t in range(TT):
                link(act.activation(sqjunk, xbuf[:, t, :], ACT.Square, accum_out=small[:, t:t + 1]))
            act.activation(small[:, 4:8], small[:, 0:4], ACT.Sqrt, scale=1.0 / D, bias=eps[:, 0:1]
                           ).then_inc(xsq_ready, 1)

            def split_high(n):
                if n >= len(SPLITS):
                    return
                piece = SPLITS[n]
                wait_piece(act, piece)
                src, dst = raw_piece(piece), split_piece(piece, KD)[0]
                if piece[0] == "mg":
                    src = src[:, 0:KD * 16].rearrange("p (k n) -> p k n", k=KD)
                    for g in range(4):
                        ins = act.activation(dst[:, :, QUAD * g:QUAD * g + M_HEADS],
                                             src[:, :, M_HEADS * g:M_HEADS * (g + 1)], ACT.Copy)
                    ins.then_inc(high_ready, 1)
                else:
                    act.activation(dst, src.rearrange("p (k n) -> p k n", k=KD), ACT.Copy
                                   ).then_inc(high_ready, 1)

            def next_high(piece):
                wait_used(act, piece)
                split_high(SPLITS.index(piece) + SPLIT_SLOTS)

            for n in range(SPLIT_SLOTS):
                split_high(n)
            for k in range(KD):
                name = f"xT{k}"
                wait_full(act, name)
                if k == 0:
                    act.wait_ge(dve_emptied, emptied_count("modT3"))
                    act.wait_ge(xn_ready, TT + 1)
                if k >= 4:
                    act.wait_ge(h_ready, k - 3)
                for r in range(REQS):
                    ins = act.activation(hbuf[k % 4][:, r * SEQ:(r + 1) * SEQ], bank(name)[:, r * SEQ:(r + 1) * SEQ],
                                         ACT.Identity, scale=scale1[:, k, r:r + 1],
                                         bias=modT[:, k // 4, k % 4, r:r + 1])
                ins.then_inc(act_emptied, 1)

            def copy_raw(n):
                wait_full(act, f"raw{n}")
                if n >= 2:
                    wait_emptied(act, f"swap{n - 2}")
                act.activation(raw[n % 2], bank(f"raw{n}"), ACT.Copy).then_inc(act_emptied, 1)

            for kind, what in STEPS:
                if kind == "gateT":
                    wait_full(act, "gateT")
                    act.activation(gateT[:, 0], bank("gateT", 32).rearrange("p (d t h) -> p d t h", d=2, t=TT),
                                   ACT.Copy)
                    act.activation(gateT[:, 1], bank("gateT", 64)[:, 32:64].rearrange(
                        "p (d t h) -> p d t h", d=2, t=TT), ACT.Exp).then_inc(act_emptied, 1)
                if kind != "piece" or what not in SPLITS:
                    continue
                name, j = what
                next_high(what)
                if name == "ak":
                    copy_raw(0)
                elif name == "av":
                    act.activation(rot_v[:, 2560:3072], bank("av"), ACT.Copy).then_inc(act_emptied, 1)
                elif name == "mg":
                    act.wait_ge(forget_abs, 1)
                    link(act.activation(rows_x, rows_x, ACT.Exp))
                    act.activation(rows_x, rows_x, ACT.Ln, bias=1.0).then_inc(forget_ln, 1)
                elif name == "aq":
                    copy_raw(j + 1)
                elif name in ("mq", "mk"):
                    c = j + 4 * (name == "mk")
                    wait_emptied(act, f"conv{c}")
                    act.activation(mqk[:, c, :], acc[c % 2], ACT.Silu).then_inc(conv_done, 1)
                elif j == 3 and name == "mv":
                    for t in range(TT):
                        wait_full(act, f"mv{t}")
                        act.activation(mvb[:, t, :, 0:M_HD],
                                       bank(f"mv{t}").rearrange("p (h e) -> p h e", h=M_HEADS),
                                       ACT.Copy).then_inc(act_emptied, 1)
                elif j == 3 and name == "mo":
                    act.wait_ge(zeros_stored, 16 * 2 * (MAX_PAIRS - MIN_PAIRS))
                    for t in range(TT):
                        wait_full(act, f"mo{t}")
                        act.activation(og[:, t, :], bank(f"mo{t}"), ACT.Tanh, scale=0.5).then_inc(act_emptied, 1)

            def branch_gate(c):
                next_high((f"bg{c // 4}", c % 4))
                act.activation(bgate[:, c, :], bank(f"bg{c}"), ACT.Tanh, scale=0.5).then_inc(act_emptied, 1)

            def softmax_exp(b):
                act.wait_ge(negmax_ready, b + 1)
                st = stat[:, b % 2]
                for h in range(A_HEADS):
                    act.activation(probs[:, b % 2, h, :], probs[:, b % 2, h, :], ACT.Exp,
                                   bias=st[:, 1, h:h + 1], accum_out=st[:, 3, h:h + 1])
                act.activation(st[:, 4, :], st[:, 2, :], ACT.Exp).then_inc(probs_ready, 1)

            def decay_exp(u):
                wait_emptied(act, f"mrow{u}")
                act.activation(ebuf[:, u % 2], ebuf[:, u % 2], ACT.Exp).then_inc(decay_ready, 1)

            for b in range(TT):
                softmax_exp(b)
                decay_exp(2 * b)
                branch_gate(4 * b)
                branch_gate(4 * b + 1)
                for n in (1, 3):
                    wait_full(act, f"pT{b}.{n}")
                    if b >= 1:
                        wait_full(act, f"pv{b - 1}")
                    act.activation(pTb[:, 4 * n:4 * n + 4, :], bank(f"pT{b}.{n}").rearrange("p (n t) -> p n t", t=P),
                                   ACT.Copy).then_inc(act_emptied, 1)
                decay_exp(2 * b + 1)
                branch_gate(4 * b + 2)
                branch_gate(4 * b + 3)
                wait_full(act, f"oT{b}")
                act.activation(oT[:, :, b * P:(b + 1) * P], bank(f"oT{b}").rearrange("p (k t) -> p k t", k=KM),
                               ACT.Copy).then_inc(act_emptied, 1)

            wait_emptied(act, "oT3")
            for n in range(2):
                act.activation(o_parts[0][:, 2 * n:2 * n + 2, :], oT[:, 2 * n:2 * n + 2, :], ACT.Copy
                               ).then_inc(oT_high, 1)

            def spread(b, dst):
                for n in range(2):
                    for r in range(REQS):
                        name = f"spread{b + n}.{r}"
                        wait_full(act, name)
                        act.activation(dst[:, r, n * COLS:(n + 1) * COLS], bank(name), ACT.Copy
                                       ).then_inc(act_emptied, 1)

            spread(4, g1b)
            spread(6, shift2)
            act.wait_ge(hm_sq, 1)
            act.activation(small[:, 24:40], small[:, 8:24], ACT.Sqrt, scale=1.0 / M_HD, bias=eps[:, 0:1]
                           ).then_inc(hm_root, 1)
            for j in range(4):
                next_high(("upa", j))
            for t in range(TT):
                wait_full(act, f"mT{t}")
                act.activation(m_parts[0][:, :, t * P:(t + 1) * P],
                               bank(f"mT{t}").rearrange("p (k t) -> p k t", k=KM), ACT.Copy).then_inc(mT_high, 1)
            for j in range(4):
                next_high(("upm", j))
                for n in (2 * j, 2 * j + 1):
                    wait_emptied(act, f"upm{n}")
                    act.activation(merged[0][:, n, :], bgate[:, n, :], ACT.Copy).then_inc(merged_high, 1)
            spread(8, scale2)
            for h in range(2):
                for j in range(4):
                    if (h, j) < (1, 2):
                        next_high((f"wo{h}", j))
            for t in range(TT):
                wait_emptied(act, f"wo{t}.1")
                link(act.activation(sqjunk, xbuf[:, t, :], ACT.Square, accum_out=small[:, 40 + t:41 + t]))
                act.activation(small[:, 44 + t:45 + t], small[:, 40 + t:41 + t], ACT.Sqrt, scale=1.0 / D,
                               bias=eps[:, 0:1]).then_inc(x1_root, 1)
            for t in range(TT):
                for h in range(2):
                    wait_full(act, f"h2T{t}.{h}")
                    if t >= 2:
                        wait_full(act, f"logit{t - 2}")
                    act.activation(h2T[:, t % 2, 4 * h:4 * h + 4, :],
                                   bank(f"h2T{t}.{h}").rearrange("p (k t) -> p k t", t=P),
                                   ACT.Copy).then_inc(act_emptied, 1)
            spread(10, g2b)
            act.wait_ge(gate_sum, 1)
            act.activation(route[:, 80:100], route[:, 80:100], ACT.Exp).then_inc(gate_exp, 1)

            def empty_x():
                act.activation(xsT[:, 0:4, :], psum[:, 3, :].rearrange("p (k t) -> p k t", k=4), ACT.Copy
                               ).then_inc(xT_act, 1)

            def silu(q):
                act.activation(sg[:, q, :], psum[:, 0, :], ACT.Silu).then_inc(silu_done, 1)

            def empty_he():
                act.activation(heT, psum[:, 2, :].rearrange("p (k t) -> p k t", k=KF), ACT.Copy
                               ).then_inc(heT_emptied, 1)

            def empty_y(q):
                act.activation(ybuf[:, q, 0:COLS], psum[:, 5, :], ACT.Copy).then_inc(y_act, 1)

            act.wait_ge(xT_full, 1)
            empty_x()
            act.wait_ge(gate_full, 1)
            silu(0)

            def tile_step(s, q, stored):
                act.wait_ge(xT_full, s + 1)
                empty_x()
                act.wait_ge(heT_full, s)
                empty_he()
                act.wait_ge(gate_full, s + 1)
                if stored is not None:
                    act.wait_ge(he_ready, s - 1)
                silu(q)
                last_row(s, 1 - q, stored)

            def last_row(s, q, stored):
                act.wait_ge(down_full, s)
                if stored is not None:
                    act.wait_ge(y_stored[q], stored * 16)
                empty_y(q)
                act.wait_ge(y_act, s)
                act.wait_ge(y_dve, s)
                act.dma_start(y_rows[bass.ds((s - 1) * P, P), :], ybuf[:, q, :]).then_inc(y_stored[q], 16)

            tile_step(1, 1, None)
            act.wait_ge(he_ready, 1)
            tile_step(2, 0, None)
            tile_step(3, 1, 1)
            last_pair = load_last_pair(act)
            with act.Fori(2, last_pair + 1) as i:
                tile_step(i * 2, 0, i - 1)
                tile_step(i * 2 + 1, 1, i)
            act.wait_ge(heT_full, last_pair * 2 + 2)
            empty_he()
            last_row(last_pair * 2 + 2, 1, last_pair)
            act.wait_ge(y_stored[0], last_pair * 16 + 16)
            act.wait_ge(y_stored[1], last_pair * 16 + 16)
            act.activation(small[:, 56:57], eps[:, :], ACT.Copy).then_inc(rows_stored, 1)

            for t in range(TT):
                act.wait_ge(x2_ready, t + 1)
                link(act.activation(junk, xbuf[:, t, :], ACT.Square, accum_out=small[:, 48 + t:49 + t]))
                act.activation(small[:, 52 + t:53 + t], small[:, 48 + t:49 + t], ACT.Sqrt, scale=1.0 / D,
                               bias=eps[:, 0:1]).then_inc(x2_root, 1)
            for t in range(TT):
                act.wait_ge(y_ready, t + 1)
                r, tt = t // TPR, t % TPR
                act.dma_start(y_out[r][0, tt * P:(tt + 1) * P, :], xbuf[:, t, :]).then_inc(out_stored, 16)
            act.wait_ge(out_stored, 16 * TT)

        @block.vector
        def _(dve):
            steps = [0]

            def link(ins):
                steps[0] += 1
                ins.then_inc(dve_chain, 1)
                dve.wait_ge(dve_chain, steps[0])

            def emptied(ins):
                ins.then_inc(dve_emptied, 1)

            link(dve.memset(mvb[:, :, :, M_HD:VW], 1.0))
            link(dve.memset(ones_row, 1.0))
            link(dve.memset(cT[:, :, :], 0.0))
            dve.memset(eps[:, :], EPS).then_inc(ones_ready, 1)
            wait_full(dve, "cT")
            emptied(dve.tensor_copy(cT[:, :, 0:REQS], bank("cT")[:, 0:KD * REQS].rearrange("p (k r) -> p k r", k=KD)))
            wait_full(dve, "gainT")
            emptied(dve.tensor_copy(gainT[:, :], bank("gainT", GAINS)))
            link(dve.tensor_scalar(nsink[:, :], sink[:, :], -1.0, None, ALU.mult))

            def empty_ada(b):
                name = f"ada{b}"
                wait_full(dve, name)
                if b >= 2:
                    wait_full(dve, f"modT{b - 2}")
                emptied(dve.tensor_copy(modrow[:, b % 2, :], bank(name)))

            def mod_turned(b):
                wait_full(dve, f"modT{b}")
                over_r = lambda a: gainT[:, a:a + 4].rearrange("p (c r) -> p c r", r=1).to_broadcast([P, 4, REQS])
                m = modT[:, b]
                ins = dve.tensor_tensor(m, bank(f"modT{b}", 8).rearrange("p (c r) -> p c r", c=4),
                                        over_r(40 + 4 * b), ALU.add)
                if b in (4, 5):
                    link(ins)
                    ins = dve.tensor_scalar(m, m, 0.5, None, ALU.mult)
                elif b in (8, 9):
                    link(ins)
                    ins = dve.scalar_tensor_tensor(out=m, in0=m, scalar=1.0, in1=over_r(32 + 4 * (b - 8)),
                                                   op0=ALU.add, op1=ALU.mult)
                emptied(ins)

            def diagonals(first, last):
                for b in range(first, last):
                    for r in range(REQS):
                        n = SPREADS.index(f"spread{b}.{r}")
                        if n >= 2:
                            wait_full(dve, SPREADS[n - 2])
                        dve.tensor_tensor(modrow[:, n % 2, :].rearrange("p (c n) -> p c n", c=4),
                                          ident.rearrange("p (c n) -> p c n", c=1).to_broadcast([P, 4, P]),
                                          modT[:, b, :, r:r + 1].to_broadcast([P, 4, P]), ALU.mult
                                          ).then_inc(diag_ready, 1)

            dve.wait_ge(xsq_ready, 1)
            link(dve.reciprocal(small[:, 0:4], small[:, 4:8]))
            for t in range(TT):
                dve.tensor_scalar(xbuf[:, t, :], xbuf[:, t, :], small[:, t:t + 1], None, ALU.mult
                                  ).then_inc(xn_ready, 1)
            empty_ada(0)
            empty_ada(1)
            mod_turned(0)
            empty_ada(2)
            mod_turned(1)
            empty_ada(3)
            mod_turned(2)
            mod_turned(3)
            dve.wait_ge(dve_emptied, emptied_count("modT3"))
            for r in range(REQS):
                ins = dve.scalar_tensor_tensor(out=scale1[:, :, r],
                                               in0=modT[:, 2:4, :, r].rearrange("p b c -> p (b c)"),
                                               scalar=1.0, in1=gainT[:, 0:KD], op0=ALU.add, op1=ALU.mult)
                if r == 0:
                    link(ins)
                else:
                    ins.then_inc(xn_ready, 1)
            dve.wait_ge(xn_ready, TT + 1)
            for k in range(KD):
                wait_emptied(dve, f"xT{k}")
                dve.tensor_copy(h_high[:, k, :], hbuf[k % 4]).then_inc(h_high_ready, 1)
                dve.wait_ge(h_high_ready, k + 1)
                dve.tensor_tensor(h_low[:, k, :], hbuf[k % 4], h_high[:, k, :].bitcast(F32), ALU.subtract
                                  ).then_inc(h_ready, 1)

            def gate_rows():
                wait_full(dve, "gates")
                for g, slot in ((0, 0), (2, 1), (1, 2), (3, 3)):
                    ins = dve.tensor_copy(rows[:, slot, :], bank("gates")[32 * g:32 * g + M_HEADS, :])
                emptied(ins)
                wait_emptied(dve, "gates")
                for g, slot in ((0, 0), (2, 1), (1, 2), (3, 3)):
                    link(dve.tensor_scalar(rows[:, slot, :], rows[:, slot, :], gbias[:, g:g + 1], None, ALU.add))
                dve.scalar_tensor_tensor(out=rows_x, in0=rows[:, 2:4, :], scalar=-1.0, in1=rows[:, 2:4, :],
                                         op0=ALU.mult, op1=ALU.min).then_inc(forget_abs, 1)
                dve.wait_ge(forget_ln, 1)
                link(dve.scalar_tensor_tensor(out=rows[:, 2:4, :], in0=rows[:, 2:4, :], scalar=0.0, in1=rows_x,
                                              op0=ALU.min, op1=ALU.subtract))

                def scans(dst, src, first, first_op, second_op):
                    for d in range(2):
                        for r in range(REQS):
                            o, i = dst[:, d, r * SEQ:(r + 1) * SEQ], src[:, d, r * SEQ:(r + 1) * SEQ]
                            a = i if first is None else first
                            if d == 1:
                                o, i, a = o[:, ::-1], i[:, ::-1], a[:, ::-1]
                            link(dve.tensor_tensor_scan(o, a, i, 0.0, first_op, second_op))

                log_f, cum, inp, run = rows[:, 2:4, :], rows_x, rows[:, 0:2, :], rows[:, 2:4, :]
                scans(cum, log_f, ones_row, ALU.mult, ALU.add)
                link(dve.tensor_tensor(inp, inp, cum, ALU.subtract))
                scans(run, inp, None, ALU.max, ALU.max)
                link(dve.scalar_tensor_tensor(out=cum, in0=cum, scalar=-1.0, in1=run, op0=ALU.mult, op1=ALU.subtract))
                dve.tensor_scalar(run, run, -1.0, None, ALU.mult).then_inc(rows_ready, 1)

            def rotate(n):
                wait_emptied(dve, f"raw{n}")
                two = lambda ap: ap.rearrange("p (r t) -> p r t", r=REQS)
                table = lambda c: const(c).rearrange("p (a t) -> p a t", a=1).to_broadcast([P, REQS, SEQ])
                link(dve.tensor_tensor(two(rot[:, n, :]), two(raw[n % 2]), table("cos"), ALU.mult))
                wait_full(dve, f"swap{n}")
                link(dve.tensor_tensor(two(tmp[:, :]), two(bank(f"swap{n}")), table("sin"), ALU.mult))
                emptied(dve.tensor_tensor(rot[:, n, :], rot[:, n, :], tmp[:, :], ALU.add))
                wait_emptied(dve, f"swap{n}")

            def conv(c):
                wait_full(dve, f"conv{c}")
                if c >= 2:
                    dve.wait_ge(conv_done, c - 1)
                a = acc[c % 2].rearrange("p (r t) -> p r t", r=REQS)
                u = bank(f"conv{c}").rearrange("p (r t) -> p r t", r=REQS)
                w = [gainT[:, 8 + 8 * j + c:9 + 8 * j + c] for j in range(3)]
                link(dve.tensor_scalar(a, u, w[1], None, ALU.mult))
                link(dve.scalar_tensor_tensor(out=a[:, :, 1:SEQ], in0=u[:, :, 0:SEQ - 1], scalar=w[0],
                                              in1=a[:, :, 1:SEQ], op0=ALU.mult, op1=ALU.add))
                emptied(dve.scalar_tensor_tensor(out=a[:, :, 0:SEQ - 1], in0=u[:, :, 1:SEQ], scalar=w[2],
                                                 in1=a[:, :, 0:SEQ - 1], op0=ALU.mult, op1=ALU.add))

            for kind, what in STEPS:
                if kind == "swap":
                    rotate(what)
                elif kind == "turn":
                    mod_turned(what)
                elif kind == "piece":
                    name, j = what
                    if name == "mg":
                        gate_rows()
                    elif name in ("mq", "mk"):
                        conv(j + 4 * (name == "mk"))
                    elif name.startswith("ada") and j == 3:
                        empty_ada(int(name[3:]))

            def softmax_rows(b):
                st = stat[:, b % 2]
                if b >= 2:
                    wait_full(dve, f"oT{b - 2}")
                m = const("maskU" if b % TPR == 0 else "maskL")
                m = m.rearrange("p (a k) -> p a k", a=1).to_broadcast([P, 2, SEQ])
                for n in range(A_HEADS // 2):
                    name = f"score{b}.{n}"
                    wait_full(dve, name)
                    emptied(dve.scalar_tensor_tensor(
                        out=probs[:, b % 2, 2 * n:2 * n + 2, :],
                        in0=bank(name).rearrange("p (g k) -> p g k", g=2), scalar=A_HD ** -0.5, in1=m,
                        op0=ALU.mult, op1=ALU.add))
                wait_emptied(dve, f"score{b}.3")
                link(dve.tensor_reduce(st[:, 0, :], probs[:, b % 2], AX.X, ALU.max))
                link(dve.scalar_tensor_tensor(out=st[:, 1, :], in0=st[:, 0, :], scalar=-1.0, in1=nsink[:, :],
                                              op0=ALU.mult, op1=ALU.min))
                dve.tensor_tensor(st[:, 2, :], st[:, 1, :], sink[:, :], ALU.add).then_inc(negmax_ready, 1)

            def decays(u):
                r, h = u // M_HEADS, u % M_HEADS
                if u >= 2:
                    wait_full(dve, f"num{u - 2}.1")
                if u == 0:
                    wait_emptied(dve, "gateT")
                name = f"mrow{u}"
                wait_full(dve, name)
                e = ebuf[:, u % 2]
                L, U = const("maskL"), const("maskU")
                for d in range(2):
                    m = bank(name)[:, d * SEQ:(d + 1) * SEQ]
                    for s in range(TPR):
                        wide = s == d
                        col = gateT[:, 0, d, r * TPR + s, h:h + 1]
                        own = slice(s * P, (s + 1) * P)
                        mask = L if d == 0 else U
                        if not wide:
                            mask = L[:, 0:P] if d == 0 else U[:, P:2 * P]
                        ins = dve.scalar_tensor_tensor(
                            out=e[:, d, 0:SEQ] if wide else e[:, d, SEQ:SEQ + P],
                            in0=m if wide else m[:, own], scalar=col, in1=mask, op0=ALU.add, op1=ALU.add)
                emptied(ins)

            def weigh(u):
                dve.wait_ge(decay_ready, u + 1)
                name = f"qk{u}"
                wait_full(dve, name)
                e = ebuf[:, u % 2]
                for d in range(2):
                    for s in range(TPR):
                        wide = s == d
                        a = bank(name)[:, s * SEQ:(s + 1) * SEQ]
                        o = e[:, d, 0:SEQ] if wide else e[:, d, SEQ:SEQ + P]
                        ins = dve.scalar_tensor_tensor(out=o, in0=a if wide else a[:, s * P:(s + 1) * P],
                                                       scalar=M_HD ** -0.5, in1=o, op0=ALU.mult, op1=ALU.mult)
                emptied(ins)

            def normalise(u):
                r, h = u // M_HEADS, u % M_HEADS
                for d in range(2):
                    name = f"num{u}.{d}"
                    wait_full(dve, name)
                    v = bank(name)[:, 0:TPR * VW].rearrange("p (t e) -> p t e", t=TPR)
                    link(dve.tensor_tensor(mstat[:, d, 0, :], v[:, :, M_HD],
                                           gateT[:, 1, d, r * TPR:(r + 1) * TPR, h], ALU.max))
                    link(dve.scalar_tensor_tensor(out=mstat[:, d, 0, :], in0=v[:, :, M_HD], scalar=-1.0,
                                                  in1=mstat[:, d, 0, :], op0=ALU.mult, op1=ALU.max))
                    link(dve.reciprocal(mstat[:, d, 1, :], mstat[:, d, 0, :]))
                    for t in range(TPR):
                        o = hm[:, r * TPR + t, h * M_HD:(h + 1) * M_HD]
                        rec = mstat[:, d, 1, t:t + 1]
                        if d == 0:
                            ins = dve.tensor_scalar(o, v[:, t, 0:M_HD], rec, None, ALU.mult)
                        else:
                            ins = dve.scalar_tensor_tensor(out=o, in0=v[:, t, 0:M_HD], scalar=rec, in1=o,
                                                           op0=ALU.mult, op1=ALU.add)
                    emptied(ins)
                    wait_emptied(dve, name)

            for b in range(TT):
                softmax_rows(b)
                decays(2 * b)
                weigh(2 * b)
                for n in (0, 2):
                    wait_full(dve, f"pT{b}.{n}")
                    if b >= 1:
                        wait_full(dve, f"pv{b - 1}")
                    emptied(dve.tensor_copy(pTb[:, 4 * n:4 * n + 4, :],
                                            bank(f"pT{b}.{n}").rearrange("p (n t) -> p n t", t=P)))
                st = stat[:, b % 2]
                link(dve.tensor_tensor(st[:, 5, :], st[:, 3, :], st[:, 4, :], ALU.add))
                link(dve.reciprocal(st[:, 6, :], st[:, 5, :]))
                normalise(2 * b)
                decays(2 * b + 1)
                weigh(2 * b + 1)
                wait_full(dve, f"pv{b}")
                o = probs[:, b % 2].rearrange("p h k -> p (h k)")[:, 0:COLS].rearrange("p (h d) -> p h d", h=A_HEADS)
                emptied(dve.tensor_tensor(o, bank(f"pv{b}").rearrange("p (h d) -> p h d", h=A_HEADS),
                                          st[:, 6, :].rearrange("p (h a) -> p h a", a=1).to_broadcast([P, A_HEADS, A_HD]),
                                          ALU.mult))
                normalise(2 * b + 1)

            wait_emptied(dve, "modT11")
            diagonals(4, 5)
            for n in range(2):
                dve.wait_ge(oT_high, n + 1)
                dve.tensor_tensor(o_parts[1][:, 2 * n:2 * n + 2, :], oT[:, 2 * n:2 * n + 2, :],
                                  o_parts[0][:, 2 * n:2 * n + 2, :].bitcast(F32), ALU.subtract
                                  ).then_inc(oT_ready, 1)
            diagonals(5, 8)
            for t in range(TT):
                link(dve.tensor_tensor(tmp[:, :], hm[:, t, :], hm[:, t, :], ALU.mult))
                ins = dve.tensor_reduce(small[:, 8 + 4 * t:12 + 4 * t], tmp[:, :].rearrange("p (h e) -> p h e", h=M_HEADS),
                                        AX.X, ALU.add)
                if t < TT - 1:
                    link(ins)
            ins.then_inc(hm_sq, 1)
            dve.wait_ge(hm_root, 1)
            link(dve.reciprocal(small[:, 8:24], small[:, 24:40]))
            link(dve.tensor_scalar(small[:, 8:24], small[:, 8:24], 0.5, None, ALU.mult))
            wait_emptied(dve, "mo3")
            for t in range(TT):
                v = hm[:, t, :].rearrange("p (h e) -> p h e", h=M_HEADS)
                link(dve.tensor_tensor(v, v, small[:, 8 + 4 * t:12 + 4 * t].rearrange("p (h a) -> p h a", a=1)
                                       .to_broadcast([P, M_HEADS, M_HD]), ALU.mult))
                link(dve.tensor_tensor(hm[:, t, :], hm[:, t, :], hng[:, :], ALU.mult))
                dve.scalar_tensor_tensor(out=hm[:, t, :], in0=og[:, t, :], scalar=1.0, in1=hm[:, t, :],
                                         op0=ALU.add, op1=ALU.mult).then_inc(hm_ready, 1)

            wait_emptied(dve, "bg15")
            for j in range(KD):
                wait_full(dve, f"upa{j}")
                emptied(dve.scalar_tensor_tensor(out=bgate[:, j, :], in0=bgate[:, j, :], scalar=1.0,
                                                 in1=bank(f"upa{j}"), op0=ALU.add, op1=ALU.mult))
            for t in range(TT):
                dve.wait_ge(mT_high, t + 1)
                own = slice(t * P, (t + 1) * P)
                emptied(dve.tensor_tensor(m_parts[1][:, :, own],
                                          bank(f"mT{t}").rearrange("p (k t) -> p k t", k=KM),
                                          m_parts[0][:, :, own].bitcast(F32), ALU.subtract))
            for j in range(KD):
                wait_full(dve, f"upm{j}")
                link(dve.scalar_tensor_tensor(out=bgate[:, KD + j, :], in0=bgate[:, KD + j, :], scalar=1.0,
                                              in1=bank(f"upm{j}"), op0=ALU.add, op1=ALU.mult))
                emptied(dve.tensor_tensor(bgate[:, j, :], bgate[:, j, :], bgate[:, KD + j, :], ALU.add))
            diagonals(8, 10)

            dve.wait_ge(x_again, 16 * REQS)
            wait_emptied(dve, "spread5.1")
            for h in range(2):
                for t in range(TT):
                    name = f"wo{t}.{h}"
                    wait_full(dve, name)
                    xs_ = xbuf[:, t, h * COLS:(h + 1) * COLS]
                    link(dve.tensor_tensor(tmp[:, :], bank(name), g1b[:, t // TPR, h * COLS:(h + 1) * COLS], ALU.mult))
                    emptied(dve.tensor_tensor(xs_, xs_, tmp[:, :], ALU.add))
                    wait_emptied(dve, name)
            wait_emptied(dve, "spread9.1")
            wait_full(dve, "wo3.1")
            for t in range(TT):
                r = t // TPR
                dve.wait_ge(x1_root, t + 1)
                if t >= 2:
                    wait_full(dve, f"h2T{t - 2}.1")
                    dve.wait_ge(h2_stored[t % 2], 16 * (t // 2))
                link(dve.reciprocal(small[:, 40 + t:41 + t], small[:, 44 + t:45 + t]))
                link(dve.scalar_tensor_tensor(out=h2[:, t % 2, :], in0=xbuf[:, t, :], scalar=small[:, 40 + t:41 + t],
                                              in1=scale2[:, r, :], op0=ALU.mult, op1=ALU.mult))
                dve.tensor_tensor(h2[:, t % 2, :], h2[:, t % 2, :], shift2[:, r, :], ALU.add).then_inc(h2_ready, 1)
            logits = route[:, 0:80].rearrange("p (t n) -> p t n", t=TT)
            for t in range(TT):
                wait_full(dve, f"logit{t}")
                emptied(dve.tensor_tensor(logits[:, t, :], bank(f"logit{t}", 20), router_b[:, :], ALU.add))
            wait_emptied(dve, "logit3")
            dve.wait_ge(late_landed, 16)
            diagonals(10, 12)

            def three(a, w, n=4):
                return route[:, a:a + w].rearrange("p (t n) -> p t n", n=n)

            def over(ap, n=4):
                return ap.rearrange("p (t a) -> p t a", a=1).to_broadcast([P, TT, n])

            best = small[:, 0:4]
            second = small[:, 4:8]
            grp_p = small[:, 8:12]
            t4 = small[:, 12:16]
            lo = small[:, 16:20]
            iota4 = lc["iota4"].rearrange("p (a n) -> p a n", a=1).to_broadcast([P, TT, 4])
            grp_hot, e_in, hot1, hot2, scr = (three(448, 16), three(464, 16), three(480, 16),
                                              three(496, 16), three(512, 16))

            def first_hot(out, vals, top):
                link(dve.tensor_tensor(out, vals, over(top), ALU.is_equal))
                link(dve.tensor_tensor(out, out, iota4, ALU.mult))
                link(dve.tensor_reduce(lo, out, AX.X, ALU.min))
                link(dve.tensor_tensor(out, iota4, over(lo), ALU.is_equal))

            g_log, e_log = logits[:, :, 0:N_GRP], logits[:, :, N_GRP:20]
            link(dve.tensor_reduce(best, g_log, AX.X, ALU.max))
            first_hot(grp_hot, g_log, best)
            gdiff = three(80, 16)
            link(dve.tensor_tensor(gdiff, g_log, over(best), ALU.subtract))
            prod = route[:, 192:256]
            p4 = prod.rearrange("p (t g k) -> p t g k", t=TT, g=N_GRP)
            for t in range(TT):
                link(dve.tensor_tensor(p4[:, t], e_log[:, t, :].rearrange("p (g k) -> p g k", g=N_GRP),
                                       grp_hot[:, t, :].rearrange("p (g a) -> p g a", a=1)
                                       .to_broadcast([P, N_GRP, PER_GRP]), ALU.mult))
            link(dve.tensor_reduce(e_in, p4.rearrange("p t g k -> p t k g"), AX.X, ALU.add))
            link(dve.tensor_reduce(best, e_in, AX.X, ALU.max))
            first_hot(hot1, e_in, best)
            link(dve.scalar_tensor_tensor(out=scr, in0=hot1, scalar=-BIG, in1=e_in, op0=ALU.mult, op1=ALU.add))
            link(dve.tensor_reduce(second, scr, AX.X, ALU.max))
            first_hot(hot2, scr, second)
            dve.tensor_tensor(route[:, 96:100], second, best, ALU.subtract).then_inc(gate_sum, 1)
            dve.wait_ge(gate_exp, 1)
            link(dve.tensor_reduce(t4, gdiff, AX.X, ALU.add))
            link(dve.reciprocal(grp_p, t4))
            link(dve.tensor_scalar(t4, route[:, 96:100], 1.0, None, ALU.add))
            link(dve.reciprocal(lo, t4))
            link(dve.tensor_tensor(topw[:, :, 0], lo, grp_p, ALU.mult))
            link(dve.tensor_tensor(topw[:, :, 1], topw[:, :, 0], route[:, 96:100], ALU.mult))
            c12 = [hmf[:, n * 64:(n + 1) * 64].rearrange("p (t e) -> p t e", t=TT) for n in range(2)]
            chosen = route[:, 128:192].rearrange("p (t e) -> p t e", t=TT)
            for n, hot in enumerate((hot1, hot2)):
                for t in range(TT):
                    c = c12[n][:, t, :].rearrange("p (g k) -> p g k", g=N_GRP)
                    link(dve.tensor_tensor(c, grp_hot[:, t, :].rearrange("p (g a) -> p g a", a=1)
                                           .to_broadcast([P, N_GRP, PER_GRP]),
                                           hot[:, t, :].rearrange("p (a k) -> p a k", a=1)
                                           .to_broadcast([P, N_GRP, PER_GRP]), ALU.mult))
            dve.tensor_tensor(chosen, c12[0], c12[1], ALU.add).then_inc(onehots_ready, 1)

            wait_full(dve, "rank")
            f = hmf[:, 128:]
            rank = f[:, 0:64]
            cnt = f[:, 64:80]
            tiles = f[:, 80:96]
            ends = f[:, 96:112]
            starts = f[:, 112:128]
            div = f[:, 128:192]
            mod = f[:, 192:256]
            link(dve.tensor_copy(rank, bank("rank", 64)))
            emptied(dve.tensor_copy(cnt, bank("rank", 80)[:, 64:80]))
            wait_emptied(dve, "rank")
            link(dve.tensor_scalar(tiles, cnt, 0.0, None, ALU.is_gt))
            for j in range(1, TT):
                link(dve.scalar_tensor_tensor(out=tiles, in0=cnt, scalar=float(j * P), in1=tiles,
                                              op0=ALU.is_gt, op1=ALU.add))
            link(dve.tensor_tensor_scan(ends, lc["ones"][:, 0:N_EXP], tiles, 0.0, ALU.mult, ALU.add))
            link(dve.tensor_tensor(starts, ends, tiles, ALU.subtract))
            link(dve.tensor_scalar(div, rank, float(P), None, ALU.is_ge))
            for j in range(2, TT):
                link(dve.scalar_tensor_tensor(out=div, in0=rank, scalar=float(j * P), in1=div,
                                              op0=ALU.is_ge, op1=ALU.add))
            link(dve.scalar_tensor_tensor(out=mod, in0=div, scalar=-float(P), in1=rank, op0=ALU.mult, op1=ALU.add))
            d3 = div.rearrange("p (t e) -> p t e", t=TT)
            m3 = mod.rearrange("p (t e) -> p t e", t=TT)
            link(dve.tensor_tensor(d3, d3, starts.rearrange("p (a e) -> p a e", a=1).to_broadcast([P, TT, N_EXP]), ALU.add))
            tile_of = f[:, 256:264].rearrange("p (t n) -> p t n", t=TT)
            place_of = f[:, 264:272].rearrange("p (t n) -> p t n", t=TT)
            scratch = f[:, 272:336].rearrange("p (t e) -> p t e", t=TT)
            for n in range(2):
                link(dve.tensor_tensor(scratch, d3, c12[n], ALU.mult))
                link(dve.tensor_reduce(tile_of[:, :, n], scratch, AX.X, ALU.add))
                link(dve.tensor_tensor(scratch, m3, c12[n], ALU.mult))
                link(dve.tensor_reduce(place_of[:, :, n], scratch, AX.X, ALU.add))
            link(dve.scalar_tensor_tensor(out=pos[:, :, :], in0=tile_of, scalar=float(P), in1=place_of,
                                          op0=ALU.mult, op1=ALU.add))
            for b in range(2):
                dve.wait_ge(h2_stored[b], 16 * (TT // 2))
            for t in range(TT):
                for n in range(2):
                    link(dve.tensor_scalar(hot_place[2 * t + n], lc["iota"], place_of[:, t, n:n + 1], None, ALU.is_equal))
                    dve.tensor_scalar(hot_tile[2 * t + n], lc["iota"][:, 0:2 * MAX_PAIRS], tile_of[:, t, n:n + 1],
                                      lc["tokid"][:, t:t + 1], ALU.is_equal, ALU.mult
                                      ).then_inc(hot_slots_ready, 1)
            te = hmf[0:1, 512:512 + 2 * MAX_PAIRS * N_EXP].rearrange("p (s e) -> p s e", e=N_EXP)
            tf = hmf[0:1, 1024:1024 + 2 * MAX_PAIRS]
            link(dve.tensor_tensor(te, ends[0:1, :].rearrange("p (a e) -> p a e", a=1).to_broadcast([1, 2 * MAX_PAIRS, N_EXP]),
                                   lc["iota"][0:1, 0:2 * MAX_PAIRS].rearrange("p (s a) -> p s a", a=1)
                                   .to_broadcast([1, 2 * MAX_PAIRS, N_EXP]), ALU.is_le))
            link(dve.tensor_reduce(tf, te, AX.X, ALU.add))
            link(dve.tensor_scalar(tile_expert[:, 0:2 * MAX_PAIRS], tf, float(N_EXP - 1), None, ALU.min))
            below = hmf[0:1, 1024:1024 + MAX_PAIRS - 1]
            n_pairs = hmf[0:1, 1100:1101]
            link(dve.scalar_tensor_tensor(out=below, in0=lc["iota"][0:1, 1:MAX_PAIRS], scalar=2.0,
                                          in1=ends[0:1, N_EXP - 1:N_EXP].to_broadcast([1, MAX_PAIRS - 1]),
                                          op0=ALU.mult, op1=ALU.is_lt))
            link(dve.tensor_reduce(n_pairs, below, AX.X, ALU.add))
            dve.tensor_copy(tile_expert[:, 2 * MAX_PAIRS:2 * MAX_PAIRS + 1], n_pairs).then_inc(tiles_ready, 1)
            wait_full(dve, "ids")
            emptied(dve.tensor_copy(ids[:, :], bank("ids", 2 * MAX_PAIRS)))

            def empty_x():
                dve.tensor_copy(xsT[:, 4:8, :], psum[:, 4, :].rearrange("p (k t) -> p k t", k=4)
                                ).then_inc(xT_dve, 1)

            def gated(q):
                dve.tensor_tensor(he[:, q, :], sg[:, q, :], psum[:, 1, :], ALU.mult).then_inc(he_ready, 1)

            def empty_y(q):
                dve.tensor_copy(ybuf[:, q, COLS:D], psum[:, 6, :]).then_inc(y_dve, 1)

            dve.wait_ge(xT_full, 1)
            empty_x()
            dve.wait_ge(silu_done, 1)
            dve.wait_ge(up_full, 1)
            gated(0)

            def tile_step(s, q, stored):
                dve.wait_ge(xT_full, s + 1)
                empty_x()
                dve.wait_ge(silu_done, s + 1)
                dve.wait_ge(up_full, s + 1)
                if stored is not None:
                    dve.wait_ge(heT_full, s - 1)
                gated(q)
                last_row(s, 1 - q, stored)

            def last_row(s, q, stored):
                dve.wait_ge(down_full, s)
                if stored is not None:
                    dve.wait_ge(y_stored[q], stored * 16)
                empty_y(q)

            tile_step(1, 1, None)
            dve.wait_ge(heT_full, 1)
            tile_step(2, 0, None)
            tile_step(3, 1, 1)
            last_pair = load_last_pair(dve)
            with dve.Fori(2, last_pair + 1) as i:
                tile_step(i * 2, 0, i - 1)
                tile_step(i * 2 + 1, 1, i)
            last_row(last_pair * 2 + 2, 1, last_pair)

            for t in range(TT):
                a, b = pair[(2 * t) % 4], pair[(2 * t + 1) % 4]
                for n in range(2):
                    dve.wait_ge(pair_landed[(2 * t + n) % 4], 16 * (t // 2 + 1))
                link(dve.tensor_scalar(a, a, topw[:, t, 0:1], None, ALU.mult))
                link(dve.scalar_tensor_tensor(out=a, in0=b, scalar=topw[:, t, 1:2], in1=a, op0=ALU.mult, op1=ALU.add))
                link(dve.tensor_tensor(a, a, g2b[:, t // TPR, :], ALU.mult))
                dve.tensor_tensor(xbuf[:, t, :], xbuf[:, t, :], a, ALU.add).then_inc(x2_ready, 1)
            dve.wait_ge(fgain_landed, 16)
            for t in range(TT):
                dve.wait_ge(x2_root, t + 1)
                link(dve.reciprocal(small[:, 48 + t:49 + t], small[:, 52 + t:53 + t]))
                dve.scalar_tensor_tensor(out=xbuf[:, t, :], in0=xbuf[:, t, :], scalar=small[:, 48 + t:49 + t],
                                         in1=fgain, op0=ALU.mult, op1=ALU.mult).then_inc(y_ready, 1)

        @block.gpsimd
        def _(pool):
            pool.memset(og[:, 0:2, :], 0.0).then_inc(zeros_ready, 1)
            def low_part(piece):
                n = SPLITS.index(piece)
                pool.wait_ge(high_ready, n + 1)
                src = raw_piece(piece).rearrange("p (k n) -> p k n", k=KD)
                high, low = split_piece(piece, KD)
                if piece[0] == "mg":
                    src = raw_piece(piece)[:, 0:KD * 16].rearrange("p (k n) -> p k n", k=KD)
                    for g in range(4):
                        a, b = slice(QUAD * g, QUAD * g + M_HEADS), slice(M_HEADS * g, M_HEADS * (g + 1))
                        ins = pool.tensor_tensor(low[:, :, a], src[:, :, b], high[:, :, a].bitcast(F32),
                                                 ALU.subtract)
                    ins.then_inc(low_ready, 1)
                else:
                    pool.tensor_tensor(low, src, high.bitcast(F32), ALU.subtract).then_inc(low_ready, 1)

            for piece in SPLITS[:SPLITS.index(("upm", 2))]:
                low_part(piece)
                if piece == ("mq", 1):
                    pool.wait_ge(zeros_ready, 1)
                    for s in range(2 * MIN_PAIRS, 2 * MAX_PAIRS):
                        pool.dma_start(y_rows[s * P:(s + 1) * P, :], og[:, 0:2, :]).then_inc(zeros_stored, 16)
                if piece == ("upa", 1):
                    wait_full(pool, "oT3")
                    for r in range(REQS):
                        pool.dma_start(xbuf[:, 2 * r:2 * r + 2, :],
                                       x_in[r][0].rearrange("(t p) d -> p t d", p=P)).then_inc(x_again, 16)
                    pool.dma_start(late, late_consts).then_inc(late_landed, 16)
                if piece == ("upa", 3):
                    pool.wait_ge(oT_ready, 2)
                    with nc.allow_non_contiguous_dma(reason="router weights"):
                        pool.dma_start(router_w[:, :, 0:4], rg_w[0].rearrange("(k p) n -> p k n", p=P)
                                       ).then_inc(router_landed, 16)
                        pool.dma_start(router_w[:, :, 4:20], re_w[0].rearrange("(k p) n -> p k n", p=P)
                                       ).then_inc(router_landed, 16)
            rest = SPLITS[SPLITS.index(("upm", 2)):]
            for j in range(4):
                low_part(rest[j])
                for n in (2 * j, 2 * j + 1):
                    pool.wait_ge(merged_high, n + 1)
                    pool.tensor_tensor(merged[1][:, n, :], bgate[:, n, :], merged[0][:, n, :].bitcast(F32),
                                       ALU.subtract).then_inc(merged_ready, 1)
            for piece in rest[4:]:
                low_part(piece)
            for t in range(TT):
                pool.wait_ge(h2_ready, t + 1)
                pool.dma_start(h2_rows[t * P:(t + 1) * P, :], h2[:, t % 2, :]).then_inc(h2_stored[t % 2], 16)
            wait_emptied(pool, "wo3.1")
            pool.dma_start(fgain, row_bcast(final_norm_g)).then_inc(fgain_landed, 16)

            def gather(q, idx):
                pool.indirect_dma_start(xs[:, q, :], None, h2_rows,
                                        bass.IndirectOffsetOnAxis(ap=idx, axis=0)).then_inc(xs_landed[q], 16)

            for b in range(2):
                pool.wait_ge(h2_stored[b], 16 * (TT // 2))
            wait_emptied(pool, "ids")
            gather(0, ids[:, 0:1])
            gather(1, ids[:, 1:2])
            last_pair = load_last_pair(pool)
            with pool.Fori(1, last_pair + 1) as i:
                for q in range(2):
                    pool.wait_ge(xT_full, i * 2 + (q - 1))
                    pool.tensor_copy(ids_now[:, q:q + 1], ids[:, bass.ds(i * 2 + q, 1)])
                    pool.drain()
                    gather(q, ids_now[:, q:q + 1])

            pool.wait_ge(rows_stored, 1)
            for t in range(TT):
                for n in range(2):
                    if t >= 2:
                        pool.wait_ge(x2_ready, t - 1)
                    pool.indirect_dma_start(pair[(2 * t + n) % 4], None, y_rows,
                                            bass.IndirectOffsetOnAxis(ap=pos[:, t, n:n + 1], axis=0)
                                            ).then_inc(pair_landed[(2 * t + n) % 4], 16)


def shape_constants():
    f = np.float32
    i = np.arange(P)
    early = np.zeros((P, EARLY_W), f)
    late = np.zeros((P, LATE_W), f)

    def put(table, where, name, value):
        a, w = table[name]
        where[:, a:a + w] = value

    put(EARLY, early, "ident", np.eye(P, dtype=f))
    lower = np.where(i[None, :] >= i[:, None], 0.0, -BIG)
    upper = np.where(i[None, :] <= i[:, None], 0.0, -BIG)
    put(EARLY, early, "maskL", np.concatenate([lower, np.zeros((P, P))], 1))
    put(EARLY, early, "maskU", np.concatenate([np.zeros((P, P)), upper], 1))
    half = ROPE_DIM // 2
    inv = (f(1.0) / (f(ROPE_THETA) ** (np.arange(half, dtype=f) * f(2.0) / f(ROPE_DIM)))).astype(f)
    ang = (np.arange(SEQ, dtype=f)[None, :] * inv[:, None]).astype(f)
    cos, sin = np.cos(ang).astype(f), np.sin(ang).astype(f)
    ct, st, perm = np.ones((P, SEQ), f), np.zeros((P, SEQ), f), np.zeros((P, P), f)
    for base in range(0, P, A_HD):
        ct[base:base + half], ct[base + half:base + 2 * half] = cos, cos
        st[base:base + half], st[base + half:base + 2 * half] = -sin, sin
        for n in range(half):
            perm[base + half + n, base + n] = 1.0
            perm[base + n, base + half + n] = 1.0
    put(EARLY, early, "cos", ct)
    put(EARLY, early, "sin", st)
    put(EARLY, early, "perm", perm)
    pick = np.zeros((P, REQS), f)
    for r in range(REQS):
        pick[r::QUAD, r] = 1.0
    put(EARLY, early, "pick", pick)
    put(EARLY, early, "one", 1.0)
    put(LATE, late, "tri", (i[:, None] < i[None, :]).astype(f))
    put(LATE, late, "ones", 1.0)
    put(LATE, late, "iota", i[None, :].astype(f))
    put(LATE, late, "iota4", (np.arange(4) - 64.0)[None, :])
    put(LATE, late, "tokid", i[:, None] + P * np.arange(TT)[None, :])
    return {"early_consts": early, "late_consts": late}


INPUTS = ["x_prompt", "x_sample", "c_prompt", "c_sample", "ada_w", "ada_b", "norm1_g", "w_in", "conv_w",
          "m_gate_b", "attn_sink", "head_norm_g", "w_up_attn", "w_up_mlstm", "w_out", "norm2_g", "rg_w",
          "rg_b", "re_w", "re_b", "w_gate", "w_up", "w_down", "final_norm_g"]


def kernel(**inputs):
    import concourse.bacc as bacc
    from concourse.bass_utils import run_bass_kernel_spmd

    nc = bacc.Bacc("TRN2", target_bir_lowering=False, num_devices=1, dynamic_dma_scratch_size=SCRATCH)
    arrays = {name: np.ascontiguousarray(inputs[name]) for name in INPUTS}
    arrays.update(shape_constants())
    args = [nc.dram_tensor(n, a.shape, mybir.dt.from_np(a.dtype), kind="ExternalInput").ap()
            for n, a in arrays.items()]
    for name in ("y_prompt", "y_sample"):
        args.append(nc.dram_tensor(name, (1, SEQ, D), F32, kind="ExternalOutput").ap())
    hybrid_layer(nc, *args)
    r = run_bass_kernel_spmd(nc, [arrays], core_ids=[0])
    return r.results[0]["y_prompt"], r.results[0]["y_sample"]
```

```python
from contextlib import ExitStack

import numpy as np
import concourse.bass as bass
from concourse import mybir

F32 = mybir.dt.float32
F32R = mybir.dt.float32r
I32 = mybir.dt.int32
U32 = mybir.dt.uint32
ALU = mybir.AluOpType
ACT = mybir.ActivationFunctionType
AX = mybir.AxisListType

P = 128
D = 1024
KD = D // P
REQS, SEQ = 2, 256
TOK = REQS * SEQ
TT = TOK // P
TPR = SEQ // P
COLS = 512

A_HEADS, A_KV, A_HD = 8, 2, 64
PAIRS = A_HEADS // A_KV
ROPE_DIM, ROPE_THETA = 16, 500000.0
M_HEADS, M_HD = 4, 128
KM = M_HEADS
VW = M_HD + 1

OFF_AQ, OFF_AK, OFF_MQ, OFF_MK = 0, 512, 768, 1280
OFF_MV, OFF_MO, OFF_MG, OFF_BG = 1792, 2304, 2816, 2832

N_GRP, PER_GRP = 4, 4
N_EXP = N_GRP * PER_GRP
D_EXP = 512
KF = D_EXP // P
MAX_TILES = N_EXP + 2 * TOK // P - 1
MAX_PAIRS = (MAX_TILES + 1) // 2
MIN_PAIRS = N_EXP // 2
EPS = 1e-6
BIG = 1e30

RAW_SLOTS = 4
ADA_SLOTS = 4
SPLIT_SLOTS = 2
PIECE = 1024
GAINS = 88
QUAD = 32
SCRATCH = 4096

EARLY = {"ident": (0, 128), "maskL": (128, 256), "maskU": (256, 256), "cos": (512, 256),
         "sin": (768, 256), "perm": (1024, 128), "pick": (1152, 2), "one": (1154, 1)}
EARLY_W = 1155
LATE = {"tri": (0, 128), "ones": (128, 128), "iota": (256, 128), "iota4": (384, 4), "tokid": (388, 4)}
LATE_W = 392

def list_pieces():
    pieces = [(f"ada{b}", j) for b in range(4) for j in range(4)]
    pieces += [("ak", 0), ("av", 0)]
    ada = iter([(f"ada{b}", j) for b in range(4, 12) for j in range(4)])
    for name, beside in (("aq", (1, 1, 1, 1)), ("mq", (2, 1, 2, 1)), ("mk", (2, 1, 2, 1)),
                         ("mv", (2, 2, 2, 2)), ("mo", (2, 2, 2, 2))):
        pieces += [("mg", 0)] if name == "mv" else []
        for j in range(4):
            pieces.append((name, j))
            pieces += [next(ada) for _ in range(beside[j])]
    pieces += [(name, j) for name in ("bg0", "bg1", "bg2", "bg3", "upa", "upm", "wo0", "wo1")
               for j in range(4)]
    return pieces


PIECES = list_pieces()
SPLITS = [p for p in PIECES if not p[0].startswith("ada")]


ADA_PIECES = [p for p in PIECES[16:] if p[0].startswith("ada")]
FIRST_PIECES = PIECES[:16]
RAW_PIECES = [p for p in PIECES if p not in ADA_PIECES and p not in FIRST_PIECES]


def slot_of(piece):
    if piece in ADA_PIECES:
        return True, ADA_PIECES.index(piece) % ADA_SLOTS
    return False, RAW_PIECES.index(piece) % RAW_SLOTS


def before_in_ring(piece):
    later, _ = slot_of(piece)
    ring, slots = (ADA_PIECES, ADA_SLOTS) if later else (RAW_PIECES, RAW_SLOTS)
    n = ring.index(piece) - slots
    return ring[n] if n >= 0 else None


def projection_steps():
    steps, turn = [], None
    for name, j in PIECES[16:PIECES.index(("bg0", 0))]:
        steps.append(("piece", (name, j)))
        if name.startswith("ada"):
            turn = int(name[3:]) if j == 3 else turn
            continue
        if name == "aq":
            steps.append(("swap", j))
            if j == 0:
                steps.append(("values", None))
        elif (name, j) == ("mq", 0):
            steps.append(("swap", 4))
        elif (name, j) == ("mo", 1):
            steps.append(("gateT", None))
        if turn is not None:
            steps.append(("turn", turn))
            turn = None
    steps.append(("turn", turn))
    return steps


STEPS = projection_steps()


def finished_by(name, j):
    if name.startswith("ada"):
        return [(name, "v")] if j == 3 else []
    if name in ("mv", "mo"):
        return [(f"{name}{t}", "s") for t in range(TT)] if j == 3 else []
    if name in ("wo0", "wo1"):
        return [(f"wo{t}.{name[2]}", "v") for t in range(TT)] if j == 3 else []
    if name in ("upa", "upm"):
        return [(f"{name}{2 * j + n}", "v") for n in range(2)]
    if name in ("mq", "mk"):
        return [(f"conv{j + 4 * (name == 'mk')}", "v")]
    if name.startswith("bg"):
        return [(f"bg{4 * int(name[2:]) + j}", "s")]
    return [{"ak": ("raw0", "s"), "av": ("vT", "s"), "mg": ("gates", "v"), "aq": (f"raw{j + 1}", "s")}[name]]


def list_groups():
    g = [("cT", "v"), ("gainT", "v"), ("ada0", "v"), ("ada1", "v"), ("modT0", "v"), ("ada2", "v"),
         ("modT1", "v"), ("ada3", "v"), ("modT2", "v"), ("modT3", "v")]
    g += [(f"xT{k}", "s") for k in range(KD)]
    for kind, what in STEPS:
        g += {"piece": lambda: finished_by(*what), "swap": lambda: [(f"swap{what}", "v")],
              "turn": lambda: [(f"modT{what}", "v")], "gateT": lambda: [("gateT", "s")],
              "values": lambda: [("av", "s")]}[kind]()
    for b in range(TT):
        bg = [(f"bg{4 * b + n}", "s") for n in range(4)]
        g += [(f"score{b}.{j}", "v") for j in range(PAIRS)]
        g += [(f"mrow{2 * b}", "v"), (f"qk{2 * b}", "v"), bg[0], bg[1]]
        g += [(f"pT{b}.{n}", "vs"[n % 2]) for n in range(4)]
        g += [(f"num{2 * b}.0", "v"), (f"num{2 * b}.1", "v")]
        g += [(f"mrow{2 * b + 1}", "v"), (f"qk{2 * b + 1}", "v"), bg[2], (f"pv{b}", "v")]
        g += [(f"num{2 * b + 1}.0", "v"), (f"num{2 * b + 1}.1", "v"), bg[3], (f"oT{b}", "s")]
    g += [(f"spread{b}.{r}", "s") for b in range(4, 8) for r in range(REQS)]
    g += [(f"upa{j}", "v") for j in range(KD)]
    g += [(f"mT{t}", "v") for t in range(TT)]
    g += [(f"upm{j}", "v") for j in range(KD)]
    g += [(f"spread{b}.{r}", "s") for b in range(8, 10) for r in range(REQS)]
    g += [(f"wo{t}.{h}", "v") for h in range(2) for t in range(TT)]
    for t in range(TT + 1):
        g += [(f"h2T{t}.0", "s"), (f"h2T{t}.1", "s")] if t < TT else []
        g += [(f"logit{t - 1}", "v")] if t >= 1 else []
    g += [("rank", "v")] + [(f"spread{b}.{r}", "s") for b in range(10, 12) for r in range(REQS)]
    g += [("ids", "v")]
    return g


GROUPS = list_groups()
INDEX = {name: n for n, (name, _) in enumerate(GROUPS)}
BANKS = 8


def emptied_count(name):
    n = INDEX[name]
    return sum(1 for _, e in GROUPS[:n + 1] if e == GROUPS[n][1])


PARTS = [p for p in PIECES if not finished_by(*p)]
SPREADS = [name for name, _ in GROUPS if name.startswith("spread")]


def hybrid_layer(nc, x_prompt, x_sample, c_prompt, c_sample, ada_w, ada_b, norm1_g, w_in, conv_w,
                 m_gate_b, attn_sink, head_norm_g, w_up_attn, w_up_mlstm, w_out, norm2_g, rg_w,
                 rg_b, re_w, re_b, w_gate, w_up, w_down, final_norm_g, early_consts, late_consts,
                 y_prompt, y_sample):
    ctx = ExitStack()
    with ctx:
        address = {}

        def sb(name, shape, dt=F32):
            address[name] = (nc.sbuf_base + 31) // 32 * 32
            return ctx.enter_context(nc.sbuf_tensor(name, shape, dt))

        def placed_over(name, place, first, shape, dt=F32R):
            return nc.alloc_sbuf_tensor_at(name, shape, dt, offset=address[place] + 4 * first)

        def sem(name):
            return ctx.enter_context(nc.semaphore(name))

        x_in = [x_prompt, x_sample]
        y_out = [y_prompt, y_sample]

        front_ring = sb("front_ring", [P, 3, 4096])
        raw_ring = front_ring[:, 0, :].rearrange("p (s n) -> p s n", s=RAW_SLOTS)
        high_ring = placed_over("high_ring", "front_ring", 4096, [P, SPLIT_SLOTS, PIECE])
        low_ring = placed_over("low_ring", "front_ring", 4096 + SPLIT_SLOTS * PIECE, [P, SPLIT_SLOTS, PIECE])
        h_low = placed_over("h_low", "front_ring", 8192, [P, KD, TOK])
        slot3 = sb("slot3", [P, 4096])
        slots45 = sb("slots45", [P, 2, 4096])
        xbuf = sb("xbuf", [P, TT, D])
        inout = sb("inout", [P, 4096])
        h_high = placed_over("h_high", "inout", 0, [P, KD, TOK])
        g1b = sb("g1b", [P, REQS, D])
        rot_pT = sb("rot_pT", [P, 5120])
        rot_v = rot_pT[:, 0:3072]
        pTflat = rot_pT[:, 3072:5120]
        mqk = sb("mqk", [P, 8, TOK])
        mvb = sb("mvb", [P, TT, M_HEADS, VW])
        og = sb("og", [P, TT, COLS])
        pTb = pTflat.rearrange("p (a b) -> p a b", a=16)
        hm = sb("hm", [P, TT, COLS])
        oT = sb("oT", [P, KM, TOK])
        tmp = sb("tmp", [P, COLS])
        modrow = sb("modrow", [P, 2, COLS])
        early = sb("early", [P, EARLY_W])
        hng = sb("hng", [P, COLS])
        cT = sb("cT", [P, KD, QUAD])
        gainT = sb("gainT", [P, GAINS])
        modT = sb("modT", [P, 12, 4, REQS])
        scale1 = sb("scale1", [P, KD, REQS])
        small = sb("small", [P, 64])
        sink = sb("sink", [P, A_HEADS])
        nsink = sb("nsink", [P, A_HEADS])
        stat = sb("stat", [P, 2, 8, A_HEADS])
        gateT = sb("gateT", [P, 2, 2, TT, M_HEADS])
        mstat = sb("mstat", [P, 2, 2, 2])
        gbias = sb("gbias", [M_HEADS, 4])
        router_b = sb("router_b", [P, 20])
        eps = sb("eps", [P, 1])

        psum = ctx.enter_context(nc.psum_tensor("psum", [P, BANKS, COLS], F32))
        h2_rows = nc.dram_tensor("h2_rows", [TOK, D], F32, kind="Internal").ap()
        y_rows = nc.dram_tensor("y_rows", [2 * MAX_PAIRS * P, D], F32, kind="Internal").ap()

        ebuf = g1b[:, :, :].rearrange("p r d -> p (r d)")[:, 0:1536].rearrange(
            "p (b d n) -> p b d n", b=2, d=2)
        crow = hm[0:REQS, 0:2, :].rearrange("p a b -> p (a b)")
        gains = slot3[0:GAINS, 3840:3968]
        def const(name):
            a, w = EARLY[name]
            return early[:, a:a + w]

        ident, perm = const("ident"), const("perm")
        rows = slot3[0:M_HEADS, 0:2048].rearrange("p (g t) -> p g t", g=4)
        rows_x = slot3[0:M_HEADS, 2048:3072].rearrange("p (g t) -> p g t", g=2)
        ones_row = slot3[0:M_HEADS, 3072:3328]
        bgate = slots45[:, :, :].rearrange("p s (c t) -> p (s c) t", t=TOK)
        probs = xbuf[:, :, :].rearrange("p (b a) n -> p b (a n)", b=2).rearrange(
            "p b (h k) -> p b h k", h=A_HEADS)
        rot = rot_v[:, 0:2560].rearrange("p (c t) -> p c t", c=5)
        av = rot_v[:, 2560:3072].rearrange("p (t f) -> p t f", t=TT)
        o_parts = [h_high[:, 0:KM, :], h_high[:, KM:KD, :]]
        m_parts = [h_low[:, 0:KM, :], h_low[:, KM:KD, :]]
        merged = [placed_over("merged_high", "slots45", 4096, [P, KD, TOK]),
                  placed_over("merged_low", "rot_pT", 0, [P, KD, TOK])]
        ada_ring = xbuf[:, :, :]
        hbuf = [pTflat[:, n * 512:(n + 1) * 512] for n in range(4)]
        raw = [pTflat[:, n * 512:(n + 1) * 512] for n in range(2)]
        vT = pTflat[:, 1024:1536]
        acc = [pTflat[:, 1024 + n * 512:1536 + n * 512] for n in range(2)]
        mqkf = mqk[:, :, :].rearrange("p a b -> p (a b)")
        scale2 = mqkf[:, 0:2048].rearrange("p (r d) -> p r d", r=REQS)
        shift2 = mqkf[:, 2048:4096].rearrange("p (r d) -> p r d", r=REQS)
        g2b = og[:, :, :].rearrange("p a b -> p (a b)").rearrange("p (r d) -> p r d", r=REQS)
        mvf = mvb[:, :, :, :].rearrange("p a b c -> p (a b c)")
        late = mvf[:, D:D + LATE_W]
        lc = {n: late[:, a:a + w] for n, (a, w) in LATE.items()}
        route = mvf[:, D + LATE_W:D + LATE_W + 640]
        chosen_before = modrow[:, 0, 0:(TT + 1) * N_EXP]
        h2 = rot_pT[:, 0:4096].rearrange("p (t d) -> p t d", t=TT)
        hmf = hm[:, :, :].rearrange("p a b -> p (a b)")
        h2T = hmf.rearrange("p (b k t) -> p b k t", b=2, k=KD)
        hTf = inout[:, :]
        xs = hTf[:, 0:2048].rearrange("p (b d) -> p b d", b=2)
        ybuf = hTf[:, 2048:4096].rearrange("p (b d) -> p b d", b=2)
        xsT = rot_v[:, 0:1024].rearrange("p (k t) -> p k t", k=KD)
        sg = rot_v[:, 1024:2048].rearrange("p (b f) -> p b f", b=2)
        oTf = oT[:, :, :].rearrange("p a b -> p (a b)")
        he = oTf[:, 0:1024].rearrange("p (b f) -> p b f", b=2)
        heT = [placed_over("heT_high", "oT", 1024, [P, KF, P])[:, :, :],
               placed_over("heT_low", "oT", 1536, [P, KF, P])[:, :, :]]
        down_parts = [
            [placed_over("down_high0", "mqk", 0, [P, 2, D])[:, :, :],
             placed_over("down_high1", "mqk", 2048, [P, 2, D])[:, :, :]],
            [placed_over("down_low0", "rot_pT", 3072, [P, 2, D])[:, :, :],
             placed_over("down_low1", "hm", 0, [P, 2, D])[:, :, :]]]
        router_w = oTf[:, 1536:1696].rearrange("p (k n) -> p k n", k=KD)
        fgain = g1b[:, 0, :]
        junk = g1b[:, 1, :]
        sqjunk = hTf[:, 0:1024]
        pair = ([mqkf[:, n * D:(n + 1) * D] for n in range(4)]
                + [slot3[:, n * D:(n + 1) * D] for n in range(4)])
        ids = placed_over("ids", "mvb", 0, [P, 2 * MAX_PAIRS], U32)
        pos = sb("pos", [P, TT, 2], U32)
        topw = mvf[:, 32:40].rearrange("p (t n) -> p t n", n=2)
        tile_expert = sb("tile_expert", [1, 2 * MAX_PAIRS + 1], I32)

        hot_place = [pTflat[:, n * P:(n + 1) * P] for n in range(2 * TT)]
        ids_now = sb("ids_now", [P, 2], U32)
        hot_tile = [route[:, 256 + n * 24:280 + n * 24] for n in range(2 * TT)]

        moe_slot = [slot3[:, :], slots45[:, 0, :], front_ring[:, 1, :], slots45[:, 1, :],
                    front_ring[:, 2, :], front_ring[:, 0, :]]

        landed = [sem(f"landed{i}") for i in range(RAW_SLOTS)]
        first_landed = [sem(f"first_landed{i}") for i in range(4)]
        ada_landed = [sem(f"ada_landed{i}") for i in range(ADA_SLOTS)]
        part_used = sem("part_used")
        high_ready = sem("high_ready")
        low_ready = sem("low_ready")
        h_high_ready = sem("h_high_ready")
        h_ready = [sem("h_even_ready"), sem("h_odd_ready")]
        oT_high = sem("oT_high")
        oT_ready = sem("oT_ready")
        mT_high = sem("mT_high")
        merged_high = sem("merged_high")
        merged_ready = sem("merged_ready")
        diag_ready = sem("diag_ready")
        moe_landed = [sem(f"moe_landed{i}") for i in range(6)]
        x_landed = sem("x_landed")
        x_again = sem("x_again")
        c_landed = sem("c_landed")
        gains_landed = sem("gains_landed")
        small_landed = sem("small_landed")
        early_landed = sem("early_landed")
        late_landed = sem("late_landed")
        router_landed = sem("router_landed")
        fgain_landed = sem("fgain_landed")
        psum_full = sem("psum_full")
        dve_emptied = sem("dve_emptied")
        act_emptied = sem("act_emptied")
        dve_chain = sem("dve_chain")
        act_chain = sem("act_chain")
        pool_chain = sem("pool_chain")
        c_ready = sem("c_ready")
        xsq_ready = sem("xsq_ready")
        xn_ready = sem("xn_ready")
        conv_done = sem("conv_done")
        forget_abs = sem("forget_abs")
        forget_ln = sem("forget_ln")
        rows_ready = sem("rows_ready")
        ones_ready = sem("ones_ready")
        negmax_ready = sem("negmax_ready")
        probs_ready = sem("probs_ready")
        decay_ready = sem("decay_ready")
        hm_sq = sem("hm_sq")
        hm_root = sem("hm_root")
        hm_ready = sem("hm_ready")
        x1_root = sem("x1_root")
        h2_ready = sem("h2_ready")
        h2_stored = sem("h2_stored")
        gate_sum = sem("gate_sum")
        gate_exp = sem("gate_exp")
        onehots_ready = sem("onehots_ready")
        hot_slots_ready = sem("hot_slots_ready")
        tiles_ready = sem("tiles_ready")
        zeros_ready = sem("zeros_ready")
        zeros_stored = sem("zeros_stored")
        rows_stored = sem("rows_stored")
        xs_landed = [sem(f"xs_landed{i}") for i in range(2)]
        xT_full = sem("xT_full")
        xT_act = sem("xT_act")
        xT_dve = sem("xT_dve")
        gate_full = sem("gate_full")
        up_full = sem("up_full")
        silu_done = sem("silu_done")
        he_ready = sem("he_ready")
        heT_full = sem("heT_full")
        heT_high = sem("heT_high")
        heT_ready = sem("heT_ready")
        down_high = sem("down_high")
        down_low = sem("down_low")
        down_full = sem("down_full")
        y_act = sem("y_act")
        y_dve = sem("y_dve")
        y_stored = [sem(f"y_stored{i}") for i in range(2)]
        pair_landed = [sem(f"pair_landed{i}") for i in range(2 * TT)]
        first_ready = sem("first_ready")
        x2_ready = sem("x2_ready")
        x2_root = sem("x2_root")
        y_ready = sem("y_ready")
        out_stored = sem("out_stored")

        slot_count, piece_landed = {}, {}
        for piece in PIECES[16:]:
            at = slot_of(piece)
            slot_count[at] = slot_count.get(at, 0) + 16 * (2 if piece[0] == "aq" else 1)
            piece_landed[piece] = slot_count[at]

        first_blocks = [front_ring[:, 1, :], slots45[:, 0, :], slots45[:, 1, :], front_ring[:, 2, :]]

        def raw_piece(piece):
            if piece in FIRST_PIECES:
                j = piece[1]
                return first_blocks[int(piece[0][3:])][:, j * PIECE:(j + 1) * PIECE]
            later, n = slot_of(piece)
            return (ada_ring if later else raw_ring)[:, n, :]

        def landed_of(piece):
            later, n = slot_of(piece)
            return (ada_landed if later else landed)[n]

        def wait_piece(eng, piece):
            if piece in FIRST_PIECES:
                eng.wait_ge(first_landed[int(piece[0][3:])], 16)
            else:
                eng.wait_ge(landed_of(piece), piece_landed[piece])

        def split_piece(piece, k):
            n = SPLITS.index(piece) % SPLIT_SLOTS
            return [ring[:, n, :].rearrange("p (k n) -> p k n", k=k) for ring in (high_ring, low_ring)]

        def wait_used(eng, piece):
            if piece in PARTS:
                eng.wait_ge(part_used, PARTS.index(piece) + 1)
            else:
                wait_full(eng, finished_by(*piece)[-1][0])

        def bank(name, width=COLS):
            return psum[:, INDEX[name] % BANKS, 0:width]

        def wait_full(eng, name):
            eng.wait_ge(psum_full, INDEX[name] + 1)

        def wait_emptied(eng, name):
            eng.wait_ge(dve_emptied if GROUPS[INDEX[name]][1] == "v" else act_emptied,
                        emptied_count(name))

        def wait_bank(eng, name):
            if INDEX[name] >= BANKS:
                wait_emptied(eng, GROUPS[INDEX[name] - BANKS][0])

        def row_bcast(ap, n=P):
            return ap.rearrange("(a n) -> a n", a=1).to_broadcast([n, ap.shape[0]])

        def load_last_pair(eng):
            eng.wait_ge(tiles_ready, 1)
            return eng.value_load(tile_expert[0:1, 2 * MAX_PAIRS:2 * MAX_PAIRS + 1],
                                  min_val=MIN_PAIRS - 1, max_val=MAX_PAIRS - 1)

        block = ctx.enter_context(nc.Block())

        @block.sync
        def _(sp):
            for b in range(4):
                if b == 1:
                    sp.wait_ge(gains_landed, 16 * 4)
                if b == 3:
                    for r in range(REQS):
                        sp.dma_start(xbuf[:, 2 * r:2 * r + 2, :],
                                     x_in[r][0].rearrange("(t p) d -> p t d", p=P)).then_inc(x_landed, 16)
                sp.dma_start(first_blocks[b].rearrange("p (k n) -> p k n", k=KD),
                             ada_w[0, :, b * COLS:(b + 1) * COLS].rearrange("(k p) n -> p k n", p=P)
                             ).then_inc(first_landed[b], 16)

            def load_piece(piece):
                name, j = piece
                slot, done = raw_piece(piece), landed_of(piece)
                deep = slot.rearrange("p (k n) -> p k n", k=2)
                if name.startswith("ada"):
                    src = ada_w[0, :, int(name[3:]) * COLS:(int(name[3:]) + 1) * COLS]
                elif name in ("wo0", "wo1"):
                    src = w_out[0, :, int(name[2]) * COLS:(int(name[2]) + 1) * COLS]
                elif name in ("mv", "mo"):
                    a = OFF_MV if name == "mv" else OFF_MO
                    src = w_in[0, :, a:a + COLS]
                elif name in ("upa", "upm"):
                    src = (w_up_attn if name == "upa" else w_up_mlstm)[0, :, j * 256:(j + 1) * 256]
                    sp.dma_start(slot.rearrange("p (k n) -> p k n", k=KM),
                                 src.rearrange("(k p) n -> p k n", p=P)).then_inc(done, 16)
                    return
                else:
                    wide = slot.rearrange("p (k n) -> p k n", k=KD)
                    if name == "aq":
                        for n, h in enumerate((j, j + PAIRS)):
                            sp.dma_start(wide[:, :, n * A_HD:(n + 1) * A_HD],
                                         w_in[0, :, OFF_AQ + h * A_HD:OFF_AQ + (h + 1) * A_HD]
                                         .rearrange("(k p) n -> p k n", p=P)).then_inc(done, 16)
                        return
                    if name == "mg":
                        a, wide = OFF_MG, slot[:, 0:KD * 16].rearrange("p (k n) -> p k n", k=KD)
                    elif name.startswith("bg"):
                        a = OFF_BG + (4 * int(name[2:]) + j) * P
                    else:
                        a = {"ak": OFF_AK, "av": OFF_AK + P, "mq": OFF_MQ, "mk": OFF_MK}[name] + j * P
                    sp.dma_start(wide, w_in[0, :, a:a + (16 if name == "mg" else P)]
                                 .rearrange("(k p) n -> p k n", p=P)).then_inc(done, 16)
                    return
                sp.dma_start(deep, src[j * 256:(j + 1) * 256, :].rearrange("(k p) n -> p k n", p=P)
                             ).then_inc(done, 16)

            for piece in PIECES[16:]:
                old = before_in_ring(piece)
                if old in SPLITS:
                    sp.wait_ge(low_ready, SPLITS.index(old) + 1)
                elif old is not None:
                    wait_used(sp, old)
                elif piece in ADA_PIECES:
                    wait_full(sp, f"xT{KD - 1}")
                load_piece(piece)
                if piece == ("aq", 3):
                    sp.wait_ge(zeros_ready, 1)
                    sp.dma_start(y_rows[2 * MIN_PAIRS * P:2 * MAX_PAIRS * P, :]
                                 .rearrange("(s p) d -> p s d", p=P),
                                 og[:, 0:2, :].rearrange("p a b -> p (a b)").rearrange("p (s d) -> p s d", s=1)
                                 .to_broadcast([P, 2 * (MAX_PAIRS - MIN_PAIRS), D])).then_inc(zeros_stored, 16)

            def expert(s):
                return sp.value_load(tile_expert[0:1, bass.ds(s, 1)], min_val=0, max_val=N_EXP - 1)

            def load_in(e, q, which):
                w = (w_gate, w_up)[which]
                sp.dma_start(moe_slot[3 * q + which],
                             w[0, bass.ds(e, 1)].rearrange("e (p k) n -> (e p) (k n)", k=KD)
                             ).then_inc(moe_landed[3 * q + which], 16)

            def load_down(e, q):
                sp.dma_start(moe_slot[3 * q + 2],
                             w_down[0, bass.ds(e, 1)].rearrange("e (p k) n -> (e p) (k n)", k=KF)
                             ).then_inc(moe_landed[3 * q + 2], 16)

            wait_full(sp, "wo3.1")
            load_in(0, 0, 0)
            load_in(0, 0, 1)
            load_in(1, 1, 0)
            load_in(1, 1, 1)
            load_down(0, 1)

            def tile_loads(s, q, e, before):
                sp.wait_ge(gate_full, s - 1)
                load_in(e, q, 0)
                sp.wait_ge(up_full, s - 1)
                load_in(e, q, 1)
                sp.wait_ge(xT_full, s)
                load_down(before, q)

            last_pair = load_last_pair(sp)
            with sp.Fori(1, last_pair + 1) as i:
                for q in range(2):
                    s = i * 2 + q
                    tile_loads(s, q, expert(s), expert(i * 2 + (q - 1)))
            e = expert(last_pair * 2 + 1)
            sp.wait_ge(down_full, last_pair * 2)
            load_down(e, 0)

        @block.tensor
        def _(pe):
            def product(name, out, lhs, rhs, count):
                for k in range(count):
                    mm = pe.matmul(out, lhs(k), rhs(k), start=(k == 0), stop=(k == count - 1))
                mm.then_inc(psum_full, 1)

            def split_product(out, lhs, rhs, count, start=True, stop=True):
                for k in range(count):
                    for a, b in ((1, 0), (0, 1), (0, 0)):
                        mm = pe.matmul(out, lhs(a, k), rhs(b, k), start=(start and k == 0 and a == 1),
                                       stop=(stop and k == count - 1 and (a, b) == (0, 0)))
                return mm

            h_parts = [h_high, h_low]

            def wait_split(piece):
                pe.wait_ge(low_ready, SPLITS.index(piece) + 1)

            def columns_out(piece):
                name = finished_by(*piece)[0][0]
                wait_bank(pe, name)
                wait_split(piece)
                w = split_piece(piece, KD)
                for k in range(KD):
                    if piece == ("ak", 0):
                        pe.wait_ge(h_ready[k % 2], k // 2 + 1)
                    mm = split_product(bank(name), lambda a, i: w[a][:, k, :], lambda b, i: h_parts[b][:, k, :], 1,
                                       start=(k == 0), stop=(k == KD - 1))
                mm.then_inc(psum_full, 1)

            def tokens_out(piece, names, parts):
                j = piece[1]
                if j == 0:
                    for name in names:
                        wait_bank(pe, name)
                wait_split(piece)
                w = split_piece(piece, 2)
                for t, name in enumerate(names):
                    mm = split_product(bank(name), lambda a, k: parts[a][:, 2 * j + k, t * P:(t + 1) * P],
                                       lambda b, k: w[b][:, k, :], 2, start=(j == 0), stop=(j == 3))
                    if j == 3:
                        mm.then_inc(psum_full, 1)
                if j < 3:
                    mm.then_inc(part_used, 1)

            def widen(piece, parts):
                wait_split(piece)
                w = split_piece(piece, KM)
                for n, (name, _) in enumerate(finished_by(*piece)):
                    wait_bank(pe, name)
                    split_product(bank(name), lambda a, k: w[a][:, k, n * P:(n + 1) * P],
                                  lambda b, k: parts[b][:, k, :], KM).then_inc(psum_full, 1)

            def transposes(name, srcs, idn=None):
                wait_bank(pe, name)
                out = bank(name).rearrange("p (n t) -> p n t", t=P)
                for n, s in enumerate(srcs):
                    mm = pe.transpose(out[:, n, :], s, ident)
                mm.then_inc(psum_full, 1)

            def ada(piece):
                name, j = piece
                if j == 0:
                    wait_bank(pe, name)
                wait_piece(pe, piece)
                w = raw_piece(piece).rearrange("p (k n) -> p k n", k=2)
                half = COLS // 2
                for n in range(2):
                    for c in range(2):
                        g = 2 * n + (c + j) % 2
                        own = slice(c * half, (c + 1) * half)
                        mm = pe.matmul(bank(name)[g * QUAD:(g + 1) * QUAD, own], cT[:, 2 * j + n, :],
                                       w[:, n, own], start=(j == 0), stop=(j == 3))
                mm.then_inc(psum_full if j == 3 else part_used, 1)

            def mod_turn(b):
                name = f"modT{b}"
                wait_bank(pe, name)
                wait_emptied(pe, f"ada{b}")
                for c in range(4):
                    mm = pe.matmul(bank(name)[:, c * REQS:(c + 1) * REQS],
                                   modrow[:, b % 2, c * P:(c + 1) * P], const("pick"), start=True, stop=True)
                mm.then_inc(psum_full, 1)

            def spread(first, last):
                for b in range(first, last):
                    for r in range(REQS):
                        name = f"spread{b}.{r}"
                        n = SPREADS.index(name)
                        wait_bank(pe, name)
                        pe.wait_ge(diag_ready, n + 1)
                        pe.matmul(bank(name), const("one").to_broadcast([P, P]), modrow[:, n % 2, :],
                                  start=True, stop=True).then_inc(psum_full, 1)

            pe.wait_ge(early_landed, 16)
            pe.wait_ge(c_ready, 1)
            for k in range(KD):
                mm = pe.transpose(bank("cT")[:, k * REQS:(k + 1) * REQS], crow[:, k * P:(k + 1) * P],
                                  ident[0:REQS, 0:REQS])
            mm.then_inc(psum_full, 1)
            pe.wait_ge(gains_landed, 16 * 4)
            pe.transpose(bank("gainT", GAINS), gains, ident[0:GAINS, 0:GAINS]).then_inc(psum_full, 1)
            wait_emptied(pe, "cT")
            for b in range(4):
                for j in range(4):
                    ada((f"ada{b}", j))
                if b >= 1:
                    mod_turn(b - 1)
            mod_turn(3)
            pe.wait_ge(xn_ready, TT)
            for k in range(KD):
                transposes(f"xT{k}", [xbuf[:, t, k * P:(k + 1) * P] for t in range(TT)])

            def swap(n):
                wait_bank(pe, f"swap{n}")
                wait_emptied(pe, f"raw{n}")
                pe.matmul(bank(f"swap{n}"), perm, raw[n % 2], start=True, stop=True).then_inc(psum_full, 1)

            def turn_gates():
                pe.wait_ge(rows_ready, 1)
                wait_bank(pe, "gateT")
                for kind in range(2):
                    for d in range(2):
                        for t in range(TT):
                            c = ((kind * 2 + d) * TT + t) * M_HEADS
                            src = rows if kind == 0 else rows_x
                            mm = pe.transpose(bank("gateT")[:, c:c + M_HEADS], src[:, d, t * P:(t + 1) * P],
                                              ident[0:M_HEADS, 0:M_HEADS])
                mm.then_inc(psum_full, 1)

            for kind, what in STEPS:
                if kind == "swap":
                    swap(what)
                elif kind == "turn":
                    mod_turn(what)
                elif kind == "gateT":
                    turn_gates()
                elif kind == "values":
                    wait_emptied(pe, "vT")
                    transposes("av", [vT[:, t * P:(t + 1) * P] for t in range(TT)])
                elif what[0].startswith("ada"):
                    ada(what)
                elif what[0] in ("mv", "mo"):
                    tokens_out(what, [f"{what[0]}{t}" for t in range(TT)], h_parts)
                else:
                    columns_out(what)

            def branch_gate(c):
                columns_out((f"bg{c // 4}", c % 4))

            def scores(b):
                r = b // TPR
                if b == 0:
                    wait_emptied(pe, "swap4")
                for n in range(A_HEADS // 2):
                    name = f"score{b}.{n}"
                    wait_bank(pe, name)
                    for h in (2 * n, 2 * n + 1):
                        at, j = h // PAIRS * A_HD, h % PAIRS
                        mm = pe.matmul(bank(name)[:, (h % 2) * SEQ:(h % 2 + 1) * SEQ],
                                       rot[at:at + A_HD, 1 + j, b * P:(b + 1) * P],
                                       rot[at:at + A_HD, 0, r * SEQ:(r + 1) * SEQ],
                                       start=True, stop=True)
                    mm.then_inc(psum_full, 1)

            def mlstm_scores(u):
                r, h = u // M_HEADS, u % M_HEADS
                name = f"mrow{u}"
                wait_bank(pe, name)
                for d in range(2):
                    mm = pe.matmul(bank(name)[:, d * SEQ:(d + 1) * SEQ],
                                   ident[0:M_HEADS, h:h + 1].to_broadcast([M_HEADS, P]),
                                   rows[:, 2 + d, r * SEQ:(r + 1) * SEQ], start=True, stop=True)
                mm.then_inc(psum_full, 1)
                if u == 0:
                    pe.wait_ge(conv_done, 8)
                name = f"qk{u}"
                wait_bank(pe, name)
                for s in range(TPR):
                    mm = pe.matmul(bank(name)[:, s * SEQ:(s + 1) * SEQ],
                                   mqk[:, 4 + h, r * SEQ + s * P:r * SEQ + (s + 1) * P],
                                   mqk[:, h, r * SEQ:(r + 1) * SEQ], start=True, stop=True)
                mm.then_inc(psum_full, 1)

            def mlstm_values(u):
                r, h = u // M_HEADS, u % M_HEADS
                wait_emptied(pe, f"qk{u}")
                if u == 0:
                    wait_emptied(pe, "mv3")
                    pe.wait_ge(ones_ready, 1)
                e = ebuf[:, u % 2]
                v = [mvb[:, r * TPR + s, h, :] for s in range(TPR)]
                plan = [[(0, [(0, 0)]), (1, [(128, 0), (256, 1)])],
                        [(0, [(0, 1), (256, 0)]), (1, [(128, 1)])]]
                for d in range(2):
                    name = f"num{u}.{d}"
                    wait_bank(pe, name)
                    for t, parts in plan[d]:
                        for n, (col, s) in enumerate(parts):
                            mm = pe.matmul(bank(name)[:, t * VW:(t + 1) * VW], e[:, d, col:col + P],
                                           v[s], start=(n == 0), stop=(n == len(parts) - 1))
                    mm.then_inc(psum_full, 1)

            def turn_probs(b):
                pe.wait_ge(probs_ready, b + 1)
                for n in range(4):
                    transposes(f"pT{b}.{n}", [probs[:, b % 2, 2 * n + i // 2, (i % 2) * P:(i % 2 + 1) * P]
                                              for i in range(4)])

            def attend(b):
                r = b // TPR
                wait_emptied(pe, f"pT{b}.2")
                wait_emptied(pe, f"pT{b}.3")
                if b == 0:
                    wait_emptied(pe, "av")
                wait_bank(pe, f"pv{b}")
                for h in range(A_HEADS):
                    for s in range(TPR):
                        kv = h // PAIRS
                        mm = pe.matmul(bank(f"pv{b}")[:, h * 64:(h + 1) * 64], pTb[:, 2 * h + s, :],
                                       av[:, r * TPR + s, kv * 64:(kv + 1) * 64],
                                       start=(s == 0), stop=(s == 1))
                mm.then_inc(psum_full, 1)

            for b in range(TT):
                scores(b)
                mlstm_scores(2 * b)
                branch_gate(4 * b)
                branch_gate(4 * b + 1)
                turn_probs(b)
                mlstm_values(2 * b)
                mlstm_scores(2 * b + 1)
                branch_gate(4 * b + 2)
                attend(b)
                mlstm_values(2 * b + 1)
                branch_gate(4 * b + 3)
                wait_emptied(pe, f"pv{b}")
                o = probs[:, b % 2].rearrange("p h k -> p (h k)")
                transposes(f"oT{b}", [o[:, k * P:(k + 1) * P] for k in range(KM)])

            spread(4, 8)
            pe.wait_ge(oT_ready, 2)
            for j in range(4):
                widen(("upa", j), o_parts)
            for t in range(TT):
                pe.wait_ge(hm_ready, t + 1)
                transposes(f"mT{t}", [hm[:, t, k * P:(k + 1) * P] for k in range(KM)])
            wait_emptied(pe, "mT3")
            for j in range(4):
                widen(("upm", j), m_parts)
            spread(8, 10)
            for h in range(2):
                for j in range(4):
                    if h == 0:
                        pe.wait_ge(merged_ready, 2 * j + 2)
                    tokens_out((f"wo{h}", j), [f"wo{t}.{h}" for t in range(TT)], merged)
            pe.wait_ge(router_landed, 16 * 2)
            for t in range(TT + 1):
                if t < TT:
                    pe.wait_ge(h2_ready, t + 1)
                    for h in range(2):
                        transposes(f"h2T{t}.{h}", [h2[:, t, (4 * h + n) * P:(4 * h + n + 1) * P]
                                                   for n in range(4)])
                if t >= 1:
                    name = f"logit{t - 1}"
                    wait_bank(pe, name)
                    wait_emptied(pe, f"h2T{t - 1}.1")
                    product(name, bank(name, 20), lambda k: h2T[:, (t - 1) % 2, k, :],
                            lambda k: router_w[:, k, :], KD)

            pe.wait_ge(onehots_ready, 1)
            pe.wait_ge(late_landed, 16)
            name = "rank"
            wait_bank(pe, name)
            pe.matmul(bank(name, 80), lc["ones"], chosen_before, start=True, stop=False)
            mm = pe.matmul(bank(name, 64), lc["tri"], route[:, 128:192], start=False, stop=True)
            mm.then_inc(psum_full, 1)
            spread(10, 12)
            name = "ids"
            wait_bank(pe, name)
            for n in range(2 * TT):
                pe.wait_ge(hot_slots_ready, 2 * n + 2)
                mm = pe.matmul(bank(name, 2 * MAX_PAIRS), hot_place[n], hot_tile[n], start=(n == 0),
                               stop=(n == 2 * TT - 1))
            mm.then_inc(psum_full, 1)

            bank_gate, bank_up, bank_heT = psum[:, 0, :], psum[:, 1, :], psum[:, 2, :]
            wait_emptied(pe, "ids")
            wait_emptied(pe, "rank")
            wait_emptied(pe, "spread11.1")

            def weights(q, part, k):
                return moe_slot[3 * q + part].rearrange("p (k n) -> p k n", k=k)

            def turn_x(s, q, nth):
                pe.wait_ge(xs_landed[q], 16 * nth)
                v = xs[:, q, :].rearrange("t (p k) -> t k p", k=KD)
                for k in range(KD):
                    mm = pe.transpose(psum[:, 3 + k // 4, (k % 4) * P:(k % 4 + 1) * P], v[:, k, :], ident)
                mm.then_inc(xT_full, 1)

            def expand(s, q, nth, part):
                w = weights(q, part, KD)
                out, done = (bank_gate, gate_full) if part == 0 else (bank_up, up_full)
                pe.wait_ge(moe_landed[3 * q + part], 16 * nth)
                for k in range(KD):
                    mm = pe.matmul(out, xsT[:, k, :], w[:, k, :], start=(k == 0), stop=(k == KD - 1))
                mm.then_inc(done, 1)

            def turn_he(q):
                v = he[:, q, :].rearrange("t (p k) -> t k p", k=KF)
                for k in range(KF):
                    mm = pe.transpose(bank_heT[:, k * P:(k + 1) * P], v[:, k, :], ident)
                mm.then_inc(heT_full, 1)

            def contract(s):
                for j in range(2):
                    pe.wait_ge(down_low, s * 2 + (j - 1))
                    for h in range(2):
                        mm = split_product(psum[:, 5 + h, :], lambda a, k: heT[a][:, 2 * j + k, :],
                                           lambda b, k: down_parts[b][j][:, k, h * COLS:(h + 1) * COLS], 2,
                                           start=(j == 0), stop=(j == 1))
                mm.then_inc(down_full, 1)

            turn_x(0, 0, 1)
            pe.wait_ge(xT_act, 1)
            pe.wait_ge(xT_dve, 1)
            expand(0, 0, 1, 0)
            expand(0, 0, 1, 1)

            def tile_step(s, q, fills, first=False):
                turn_x(s, q, fills)
                pe.wait_ge(he_ready, s)
                turn_he(1 - q)
                pe.wait_ge(xT_act, s + 1)
                pe.wait_ge(xT_dve, s + 1)
                pe.wait_ge(silu_done, s)
                expand(s, q, fills, 0)
                expand(s, q, fills, 1)
                pe.wait_ge(heT_ready, s)
                if not first:
                    pe.wait_ge(y_act, s - 1)
                    pe.wait_ge(y_dve, s - 1)
                contract(s)

            tile_step(1, 1, 1, first=True)
            last_pair = load_last_pair(pe)
            with pe.Fori(1, last_pair + 1) as i:
                tile_step(i * 2, 0, i + 1)
                tile_step(i * 2 + 1, 1, i + 1)
            pe.wait_ge(he_ready, last_pair * 2 + 2)
            turn_he(1)
            pe.wait_ge(heT_high, last_pair * 2 + 2)
            pe.wait_ge(moe_landed[2], last_pair * 16 + 16)
            pe.wait_ge(y_act, last_pair * 2 + 1)
            pe.wait_ge(y_dve, last_pair * 2 + 1)
            w = weights(0, 2, KF)
            for h in range(2):
                for k in range(KF):
                    mm = pe.matmul(psum[:, 5 + h, :], xsT[:, k, :], w[:, k, h * COLS:(h + 1) * COLS],
                                   start=(k == 0), stop=(k == KF - 1))
            mm.then_inc(down_full, 1)

        @block.scalar
        def _(act):
            steps = [0]

            def link(ins):
                steps[0] += 1
                ins.then_inc(act_chain, 1)
                act.wait_ge(act_chain, steps[0])

            act.dma_start(crow[0:1, :], c_prompt).then_inc(c_landed, 16)
            act.dma_start(crow[1:2, :], c_sample).then_inc(c_landed, 16)
            act.dma_start(early[:, :], early_consts).then_inc(early_landed, 16)
            act.dma_start(gains[0:KD, :], norm1_g.rearrange("a (k p) -> (a k) p", p=P)).then_inc(gains_landed, 16)
            act.dma_start(gains[KD:32, :], conv_w[0].rearrange("w (k p) -> (w k) p", p=P)).then_inc(gains_landed, 16)
            act.dma_start(gains[32:40, :], norm2_g.rearrange("a (k p) -> (a k) p", p=P)).then_inc(gains_landed, 16)
            act.dma_start(gains[40:GAINS, :], ada_b.rearrange("a (k p) -> (a k) p", p=P)).then_inc(gains_landed, 16)
            act.dma_start(sink[:, :], row_bcast(attn_sink[0])).then_inc(small_landed, 16)
            act.dma_start(hng[:, :], row_bcast(head_norm_g[0])).then_inc(small_landed, 16)
            act.dma_start(router_b[:, 0:4], row_bcast(rg_b[0])).then_inc(small_landed, 16)
            act.dma_start(router_b[:, 4:20], row_bcast(re_b[0])).then_inc(small_landed, 16)
            with nc.allow_non_contiguous_dma(reason="16 gate biases"):
                act.dma_start(gbias[:, :], m_gate_b[0].rearrange("(g h) -> h g", h=M_HEADS)).then_inc(small_landed, 16)
            act.wait_ge(c_landed, 16 * REQS)
            act.activation(crow, crow, ACT.Silu).then_inc(c_ready, 1)
            act.wait_ge(x_landed, 16 * REQS)
            act.wait_ge(ones_ready, 1)
            for t in range(TT):
                link(act.activation(sqjunk, xbuf[:, t, :], ACT.Square, accum_out=small[:, t:t + 1]))
            act.activation(small[:, 4:8], small[:, 0:4], ACT.Sqrt, scale=1.0 / D, bias=eps[:, 0:1]
                           ).then_inc(xsq_ready, 1)

            def split_high(n):
                if n >= len(SPLITS):
                    return
                piece = SPLITS[n]
                wait_piece(act, piece)
                src, dst = raw_piece(piece), split_piece(piece, KD)[0]
                if piece[0] == "mg":
                    src = src[:, 0:KD * 16].rearrange("p (k n) -> p k n", k=KD)
                    for g in range(4):
                        ins = act.activation(dst[:, :, QUAD * g:QUAD * g + M_HEADS],
                                             src[:, :, M_HEADS * g:M_HEADS * (g + 1)], ACT.Copy)
                    ins.then_inc(high_ready, 1)
                else:
                    act.activation(dst, src.rearrange("p (k n) -> p k n", k=KD), ACT.Copy
                                   ).then_inc(high_ready, 1)

            def next_high(piece):
                wait_used(act, piece)
                split_high(SPLITS.index(piece) + SPLIT_SLOTS)

            wait_full(act, "ada0")
            for n in range(SPLIT_SLOTS):
                split_high(n)
            for k in range(KD):
                name = f"xT{k}"
                wait_full(act, name)
                if k == 0:
                    act.wait_ge(dve_emptied, emptied_count("modT3"))
                    act.wait_ge(xn_ready, TT + 1)
                if k >= 4:
                    act.wait_ge(h_ready[k % 2], k // 2 - 1)
                for r in range(REQS):
                    ins = act.activation(hbuf[k % 4][:, r * SEQ:(r + 1) * SEQ], bank(name)[:, r * SEQ:(r + 1) * SEQ],
                                         ACT.Identity, scale=scale1[:, k, r:r + 1],
                                         bias=modT[:, k // 4, k % 4, r:r + 1])
                ins.then_inc(act_emptied, 1)

            def copy_raw(n):
                wait_full(act, f"raw{n}")
                if n >= 2:
                    wait_emptied(act, f"swap{n - 2}")
                act.activation(raw[n % 2], bank(f"raw{n}"), ACT.Copy).then_inc(act_emptied, 1)

            for kind, what in STEPS:
                if kind == "gateT":
                    wait_full(act, "gateT")
                    act.activation(gateT[:, 0], bank("gateT", 32).rearrange("p (d t h) -> p d t h", d=2, t=TT),
                                   ACT.Copy)
                    act.activation(gateT[:, 1], bank("gateT", 64)[:, 32:64].rearrange(
                        "p (d t h) -> p d t h", d=2, t=TT), ACT.Exp).then_inc(act_emptied, 1)
                if kind == "values":
                    wait_full(act, "av")
                    act.activation(rot_v[:, 2560:3072], bank("av"), ACT.Copy).then_inc(act_emptied, 1)
                if kind != "piece" or what not in SPLITS:
                    continue
                name, j = what
                next_high(what)
                if name == "ak":
                    copy_raw(0)
                elif name == "av":
                    act.activation(vT, bank("vT"), ACT.Copy).then_inc(act_emptied, 1)
                elif what == ("mv", 0):
                    act.wait_ge(forget_abs, 1)
                    link(act.activation(rows_x, rows_x, ACT.Exp))
                    act.activation(rows_x, rows_x, ACT.Ln, bias=1.0).then_inc(forget_ln, 1)
                elif name == "aq":
                    copy_raw(j + 1)
                elif name in ("mq", "mk"):
                    c = j + 4 * (name == "mk")
                    wait_emptied(act, f"conv{c}")
                    act.activation(mqk[:, c, :], acc[c % 2], ACT.Silu).then_inc(conv_done, 1)
                elif j == 3 and name == "mv":
                    for t in range(TT):
                        wait_full(act, f"mv{t}")
                        act.activation(mvb[:, t, :, 0:M_HD],
                                       bank(f"mv{t}").rearrange("p (h e) -> p h e", h=M_HEADS),
                                       ACT.Copy).then_inc(act_emptied, 1)
                elif j == 3 and name == "mo":
                    act.wait_ge(zeros_stored, 16)
                    for t in range(TT):
                        wait_full(act, f"mo{t}")
                        act.activation(og[:, t, :], bank(f"mo{t}"), ACT.Tanh, scale=0.5).then_inc(act_emptied, 1)

            def branch_gate(c):
                next_high((f"bg{c // 4}", c % 4))
                act.activation(bgate[:, c, :], bank(f"bg{c}"), ACT.Tanh, scale=0.5).then_inc(act_emptied, 1)

            def softmax_exp(b):
                act.wait_ge(negmax_ready, b + 1)
                st = stat[:, b % 2]
                for h in range(A_HEADS):
                    act.activation(probs[:, b % 2, h, :], probs[:, b % 2, h, :], ACT.Exp,
                                   bias=st[:, 1, h:h + 1], accum_out=st[:, 3, h:h + 1])
                act.activation(st[:, 4, :], st[:, 2, :], ACT.Exp).then_inc(probs_ready, 1)

            def decay_exp(u):
                wait_emptied(act, f"mrow{u}")
                act.activation(ebuf[:, u % 2], ebuf[:, u % 2], ACT.Exp).then_inc(decay_ready, 1)

            for b in range(TT):
                softmax_exp(b)
                decay_exp(2 * b)
                branch_gate(4 * b)
                branch_gate(4 * b + 1)
                for n in (1, 3):
                    wait_full(act, f"pT{b}.{n}")
                    if b >= 1:
                        wait_full(act, f"pv{b - 1}")
                    act.activation(pTb[:, 4 * n:4 * n + 4, :], bank(f"pT{b}.{n}").rearrange("p (n t) -> p n t", t=P),
                                   ACT.Copy).then_inc(act_emptied, 1)
                decay_exp(2 * b + 1)
                branch_gate(4 * b + 2)
                branch_gate(4 * b + 3)
                wait_full(act, f"oT{b}")
                act.activation(oT[:, :, b * P:(b + 1) * P], bank(f"oT{b}").rearrange("p (k t) -> p k t", k=KM),
                               ACT.Copy).then_inc(act_emptied, 1)

            wait_emptied(act, "oT3")
            for n in range(2):
                act.activation(o_parts[0][:, 2 * n:2 * n + 2, :], oT[:, 2 * n:2 * n + 2, :], ACT.Copy
                               ).then_inc(oT_high, 1)

            def spread(b, dst):
                for n in range(2):
                    for r in range(REQS):
                        name = f"spread{b + n}.{r}"
                        wait_full(act, name)
                        act.activation(dst[:, r, n * COLS:(n + 1) * COLS], bank(name), ACT.Copy
                                       ).then_inc(act_emptied, 1)

            spread(4, g1b)
            spread(6, shift2)
            act.wait_ge(hm_sq, 1)
            act.activation(small[:, 24:40], small[:, 8:24], ACT.Sqrt, scale=1.0 / M_HD, bias=eps[:, 0:1]
                           ).then_inc(hm_root, 1)
            for j in range(4):
                next_high(("upa", j))
            for t in range(TT):
                wait_full(act, f"mT{t}")
                act.activation(m_parts[0][:, :, t * P:(t + 1) * P],
                               bank(f"mT{t}").rearrange("p (k t) -> p k t", k=KM), ACT.Copy).then_inc(mT_high, 1)
            for j in range(4):
                next_high(("upm", j))
                for n in (2 * j, 2 * j + 1):
                    wait_emptied(act, f"upm{n}")
                    act.activation(merged[0][:, n, :], bgate[:, n, :], ACT.Copy).then_inc(merged_high, 1)
            spread(8, scale2)
            for h in range(2):
                for j in range(4):
                    if (h, j) < (1, 2):
                        next_high((f"wo{h}", j))
            for t in range(TT):
                wait_emptied(act, f"wo{t}.1")
                link(act.activation(sqjunk, xbuf[:, t, :], ACT.Square, accum_out=small[:, 40 + t:41 + t]))
                act.activation(small[:, 44 + t:45 + t], small[:, 40 + t:41 + t], ACT.Sqrt, scale=1.0 / D,
                               bias=eps[:, 0:1]).then_inc(x1_root, 1)
            for t in range(TT):
                for h in range(2):
                    wait_full(act, f"h2T{t}.{h}")
                    if t >= 2:
                        wait_full(act, f"logit{t - 2}")
                    act.activation(h2T[:, t % 2, 4 * h:4 * h + 4, :],
                                   bank(f"h2T{t}.{h}").rearrange("p (k t) -> p k t", t=P),
                                   ACT.Copy).then_inc(act_emptied, 1)
            act.wait_ge(gate_sum, 1)
            act.activation(route[:, 80:100], route[:, 80:100], ACT.Exp).then_inc(gate_exp, 1)
            spread(10, g2b)

            def empty_x():
                act.activation(xsT[:, 0:4, :], psum[:, 3, :].rearrange("p (k t) -> p k t", k=4), ACT.Copy
                               ).then_inc(xT_act, 1)

            def silu(q):
                act.activation(sg[:, q, :], psum[:, 0, :], ACT.Silu).then_inc(silu_done, 1)

            def empty_he():
                act.activation(heT[0], psum[:, 2, :].rearrange("p (k t) -> p k t", k=KF), ACT.Copy
                               ).then_inc(heT_high, 1)

            def split_down(q, nth):
                act.wait_ge(moe_landed[3 * q + 2], nth * 16)
                w = moe_slot[3 * q + 2].rearrange("p (k n) -> p k n", k=KF)
                for j in range(2):
                    act.activation(down_parts[0][j], w[:, 2 * j:2 * j + 2, :], ACT.Copy).then_inc(down_high, 1)

            def empty_y(q):
                act.activation(ybuf[:, q, 0:COLS], psum[:, 5, :], ACT.Copy).then_inc(y_act, 1)

            act.wait_ge(xT_full, 1)
            empty_x()
            act.wait_ge(gate_full, 1)
            silu(0)

            def tile_step(s, q, stored, fills_down):
                act.wait_ge(xT_full, s + 1)
                empty_x()
                act.wait_ge(heT_full, s)
                empty_he()
                split_down(q, fills_down)
                act.wait_ge(gate_full, s + 1)
                if stored is not None:
                    act.wait_ge(he_ready, s - 1)
                silu(q)
                last_row(s, 1 - q, stored)

            def last_row(s, q, stored):
                act.wait_ge(down_full, s)
                if stored is not None:
                    act.wait_ge(y_stored[q], stored * 16)
                empty_y(q)
                act.wait_ge(y_act, s)
                act.wait_ge(y_dve, s)
                act.dma_start(y_rows[bass.ds((s - 1) * P, P), :], ybuf[:, q, :]).then_inc(y_stored[q], 16)

            tile_step(1, 1, None, 1)
            act.wait_ge(he_ready, 1)
            tile_step(2, 0, None, 1)
            tile_step(3, 1, 1, 2)
            last_pair = load_last_pair(act)
            with act.Fori(2, last_pair + 1) as i:
                tile_step(i * 2, 0, i - 1, i)
                tile_step(i * 2 + 1, 1, i, i + 1)
            act.wait_ge(heT_full, last_pair * 2 + 2)
            act.activation(xsT[:, 0:KF, :], psum[:, 2, :].rearrange("p (k t) -> p k t", k=KF), ACT.Copy
                           ).then_inc(heT_high, 1)
            last_row(last_pair * 2 + 2, 1, last_pair)
            act.wait_ge(y_stored[0], last_pair * 16 + 16)
            act.wait_ge(y_stored[1], last_pair * 16 + 16)
            act.activation(small[:, 56:57], eps[:, :], ACT.Copy).then_inc(rows_stored, 1)

            def weight_first(t):
                act.wait_ge(pair_landed[2 * t], 16)
                act.activation(pair[2 * t], pair[2 * t], ACT.Copy, scale=topw[:, t, 0:1]).then_inc(first_ready, 1)

            weight_first(0)
            weight_first(1)
            for t in range(TT):
                act.wait_ge(x2_ready, t + 1)
                link(act.activation(junk, xbuf[:, t, :], ACT.Square, accum_out=small[:, 48 + t:49 + t]))
                act.activation(small[:, 52 + t:53 + t], small[:, 48 + t:49 + t], ACT.Sqrt, scale=1.0 / D,
                               bias=eps[:, 0:1]).then_inc(x2_root, 1)
                if t + 2 < TT:
                    weight_first(t + 2)
            for t in range(TT):
                act.wait_ge(y_ready, t + 1)
                r, tt = t // TPR, t % TPR
                act.dma_start(y_out[r][0, tt * P:(tt + 1) * P, :], xbuf[:, t, :]).then_inc(out_stored, 16)
            act.wait_ge(out_stored, 16 * TT)

        @block.vector
        def _(dve):
            steps = [0]

            def link(ins):
                steps[0] += 1
                ins.then_inc(dve_chain, 1)
                dve.wait_ge(dve_chain, steps[0])

            def emptied(ins):
                ins.then_inc(dve_emptied, 1)

            link(dve.memset(mvb[:, :, :, M_HD:VW], 1.0))
            link(dve.memset(ones_row, 1.0))
            link(dve.memset(cT[:, :, :], 0.0))
            dve.memset(eps[:, :], EPS).then_inc(ones_ready, 1)
            wait_full(dve, "cT")
            emptied(dve.tensor_copy(cT[:, :, 0:REQS], bank("cT")[:, 0:KD * REQS].rearrange("p (k r) -> p k r", k=KD)))
            wait_full(dve, "gainT")
            emptied(dve.tensor_copy(gainT[:, :], bank("gainT", GAINS)))

            def empty_ada(b):
                name = f"ada{b}"
                wait_full(dve, name)
                if b >= 2:
                    wait_full(dve, f"modT{b - 2}")
                emptied(dve.tensor_copy(modrow[:, b % 2, :], bank(name)))

            def mod_turned(b):
                wait_full(dve, f"modT{b}")
                over_r = lambda a: gainT[:, a:a + 4].rearrange("p (c r) -> p c r", r=1).to_broadcast([P, 4, REQS])
                m = modT[:, b]
                ins = dve.tensor_tensor(m, bank(f"modT{b}", 8).rearrange("p (c r) -> p c r", c=4),
                                        over_r(40 + 4 * b), ALU.add)
                if b in (4, 5):
                    link(ins)
                    ins = dve.tensor_scalar(m, m, 0.5, None, ALU.mult)
                elif b in (8, 9):
                    link(ins)
                    ins = dve.scalar_tensor_tensor(out=m, in0=m, scalar=1.0, in1=over_r(32 + 4 * (b - 8)),
                                                   op0=ALU.add, op1=ALU.mult)
                emptied(ins)

            def diagonals(first, last):
                for b in range(first, last):
                    for r in range(REQS):
                        n = SPREADS.index(f"spread{b}.{r}")
                        if n >= 2:
                            wait_full(dve, SPREADS[n - 2])
                        dve.tensor_tensor(modrow[:, n % 2, :].rearrange("p (c n) -> p c n", c=4),
                                          ident.rearrange("p (c n) -> p c n", c=1).to_broadcast([P, 4, P]),
                                          modT[:, b, :, r:r + 1].to_broadcast([P, 4, P]), ALU.mult
                                          ).then_inc(diag_ready, 1)

            empty_ada(0)
            empty_ada(1)
            mod_turned(0)
            empty_ada(2)
            mod_turned(1)
            dve.wait_ge(xsq_ready, 1)
            link(dve.reciprocal(small[:, 0:4], small[:, 4:8]))
            for t in range(TT):
                dve.tensor_scalar(xbuf[:, t, :], xbuf[:, t, :], small[:, t:t + 1], None, ALU.mult
                                  ).then_inc(xn_ready, 1)
            empty_ada(3)
            mod_turned(2)
            mod_turned(3)
            dve.wait_ge(dve_emptied, emptied_count("modT3"))
            for r in range(REQS):
                ins = dve.scalar_tensor_tensor(out=scale1[:, :, r],
                                               in0=modT[:, 2:4, :, r].rearrange("p b c -> p (b c)"),
                                               scalar=1.0, in1=gainT[:, 0:KD], op0=ALU.add, op1=ALU.mult)
                if r == 0:
                    link(ins)
                else:
                    ins.then_inc(xn_ready, 1)
            dve.wait_ge(xn_ready, TT + 1)
            for k in range(KD):
                wait_emptied(dve, f"xT{k}")
                dve.tensor_copy(h_high[:, k, :], hbuf[k % 4]).then_inc(h_high_ready, 1)
                if k % 2 == 1:
                    dve.wait_ge(h_high_ready, k)
                    dve.tensor_tensor(h_low[:, k - 1, :], hbuf[(k - 1) % 4], h_high[:, k - 1, :].bitcast(F32),
                                      ALU.subtract).then_inc(h_ready[0], 1)

            def gate_rows():
                wait_full(dve, "gates")
                for g, slot in ((0, 0), (2, 1), (1, 2), (3, 3)):
                    ins = dve.tensor_copy(rows[:, slot, :], bank("gates")[32 * g:32 * g + M_HEADS, :])
                emptied(ins)
                wait_emptied(dve, "gates")
                for g, slot in ((0, 0), (2, 1), (1, 2), (3, 3)):
                    link(dve.tensor_scalar(rows[:, slot, :], rows[:, slot, :], gbias[:, g:g + 1], None, ALU.add))
                dve.scalar_tensor_tensor(out=rows_x, in0=rows[:, 2:4, :], scalar=-1.0, in1=rows[:, 2:4, :],
                                         op0=ALU.mult, op1=ALU.min).then_inc(forget_abs, 1)

            def gate_scans():
                dve.wait_ge(forget_ln, 1)
                link(dve.scalar_tensor_tensor(out=rows[:, 2:4, :], in0=rows[:, 2:4, :], scalar=0.0, in1=rows_x,
                                              op0=ALU.min, op1=ALU.subtract))

                def scans(dst, src, first, first_op, second_op):
                    for d in range(2):
                        for r in range(REQS):
                            o, i = dst[:, d, r * SEQ:(r + 1) * SEQ], src[:, d, r * SEQ:(r + 1) * SEQ]
                            a = i if first is None else first
                            if d == 1:
                                o, i, a = o[:, ::-1], i[:, ::-1], a[:, ::-1]
                            link(dve.tensor_tensor_scan(o, a, i, 0.0, first_op, second_op))

                log_f, cum, inp, run = rows[:, 2:4, :], rows_x, rows[:, 0:2, :], rows[:, 2:4, :]
                scans(cum, log_f, ones_row, ALU.mult, ALU.add)
                link(dve.tensor_tensor(inp, inp, cum, ALU.subtract))
                scans(run, inp, None, ALU.max, ALU.max)
                link(dve.scalar_tensor_tensor(out=cum, in0=cum, scalar=-1.0, in1=run, op0=ALU.mult, op1=ALU.subtract))
                dve.tensor_scalar(run, run, -1.0, None, ALU.mult).then_inc(rows_ready, 1)

            def rotate(n):
                wait_emptied(dve, f"raw{n}")
                two = lambda ap: ap.rearrange("p (r t) -> p r t", r=REQS)
                table = lambda c: const(c).rearrange("p (a t) -> p a t", a=1).to_broadcast([P, REQS, SEQ])
                link(dve.tensor_tensor(two(rot[:, n, :]), two(raw[n % 2]), table("cos"), ALU.mult))
                wait_full(dve, f"swap{n}")
                link(dve.tensor_tensor(two(tmp[:, :]), two(bank(f"swap{n}")), table("sin"), ALU.mult))
                emptied(dve.tensor_tensor(rot[:, n, :], rot[:, n, :], tmp[:, :], ALU.add))
                wait_emptied(dve, f"swap{n}")

            def conv(c):
                wait_full(dve, f"conv{c}")
                if c >= 2:
                    dve.wait_ge(conv_done, c - 1)
                a = acc[c % 2].rearrange("p (r t) -> p r t", r=REQS)
                u = bank(f"conv{c}").rearrange("p (r t) -> p r t", r=REQS)
                w = [gainT[:, 8 + 8 * j + c:9 + 8 * j + c] for j in range(3)]
                link(dve.tensor_scalar(a, u, w[1], None, ALU.mult))
                link(dve.scalar_tensor_tensor(out=a[:, :, 1:SEQ], in0=u[:, :, 0:SEQ - 1], scalar=w[0],
                                              in1=a[:, :, 1:SEQ], op0=ALU.mult, op1=ALU.add))
                emptied(dve.scalar_tensor_tensor(out=a[:, :, 0:SEQ - 1], in0=u[:, :, 1:SEQ], scalar=w[2],
                                                 in1=a[:, :, 0:SEQ - 1], op0=ALU.mult, op1=ALU.add))

            dve.wait_ge(small_landed, 16 * 5)
            link(dve.tensor_scalar(nsink[:, :], sink[:, :], -1.0, None, ALU.mult))

            for kind, what in STEPS:
                if kind == "swap":
                    rotate(what)
                elif kind == "turn":
                    mod_turned(what)
                    if what == 8:
                        gate_scans()
                elif kind == "piece":
                    name, j = what
                    if name == "mg":
                        gate_rows()
                    elif name in ("mq", "mk"):
                        conv(j + 4 * (name == "mk"))
                    elif name.startswith("ada") and j == 3:
                        empty_ada(int(name[3:]))

            def softmax_rows(b):
                st = stat[:, b % 2]
                if b >= 2:
                    wait_full(dve, f"oT{b - 2}")
                m = const("maskU" if b % TPR == 0 else "maskL")
                m = m.rearrange("p (a k) -> p a k", a=1).to_broadcast([P, 2, SEQ])
                for n in range(A_HEADS // 2):
                    name = f"score{b}.{n}"
                    wait_full(dve, name)
                    emptied(dve.scalar_tensor_tensor(
                        out=probs[:, b % 2, 2 * n:2 * n + 2, :],
                        in0=bank(name).rearrange("p (g k) -> p g k", g=2), scalar=A_HD ** -0.5, in1=m,
                        op0=ALU.mult, op1=ALU.add))
                wait_emptied(dve, f"score{b}.3")
                link(dve.tensor_reduce(st[:, 0, :], probs[:, b % 2], AX.X, ALU.max))
                link(dve.scalar_tensor_tensor(out=st[:, 1, :], in0=st[:, 0, :], scalar=-1.0, in1=nsink[:, :],
                                              op0=ALU.mult, op1=ALU.min))
                dve.tensor_tensor(st[:, 2, :], st[:, 1, :], sink[:, :], ALU.add).then_inc(negmax_ready, 1)

            def decays(u):
                r, h = u // M_HEADS, u % M_HEADS
                if u >= 2:
                    wait_full(dve, f"num{u - 2}.1")
                if u == 0:
                    wait_emptied(dve, "gateT")
                name = f"mrow{u}"
                wait_full(dve, name)
                e = ebuf[:, u % 2]
                L, U = const("maskL"), const("maskU")
                for d in range(2):
                    m = bank(name)[:, d * SEQ:(d + 1) * SEQ]
                    for s in range(TPR):
                        wide = s == d
                        col = gateT[:, 0, d, r * TPR + s, h:h + 1]
                        own = slice(s * P, (s + 1) * P)
                        mask = L if d == 0 else U
                        if not wide:
                            mask = L[:, 0:P] if d == 0 else U[:, P:2 * P]
                        ins = dve.scalar_tensor_tensor(
                            out=e[:, d, 0:SEQ] if wide else e[:, d, SEQ:SEQ + P],
                            in0=m if wide else m[:, own], scalar=col, in1=mask, op0=ALU.add, op1=ALU.add)
                emptied(ins)

            def weigh(u):
                dve.wait_ge(decay_ready, u + 1)
                name = f"qk{u}"
                wait_full(dve, name)
                e = ebuf[:, u % 2]
                for d in range(2):
                    for s in range(TPR):
                        wide = s == d
                        a = bank(name)[:, s * SEQ:(s + 1) * SEQ]
                        o = e[:, d, 0:SEQ] if wide else e[:, d, SEQ:SEQ + P]
                        ins = dve.scalar_tensor_tensor(out=o, in0=a if wide else a[:, s * P:(s + 1) * P],
                                                       scalar=M_HD ** -0.5, in1=o, op0=ALU.mult, op1=ALU.mult)
                emptied(ins)

            def normalise(u):
                r, h = u // M_HEADS, u % M_HEADS
                for d in range(2):
                    name = f"num{u}.{d}"
                    wait_full(dve, name)
                    v = bank(name)[:, 0:TPR * VW].rearrange("p (t e) -> p t e", t=TPR)
                    link(dve.tensor_tensor(mstat[:, d, 0, :], v[:, :, M_HD],
                                           gateT[:, 1, d, r * TPR:(r + 1) * TPR, h], ALU.max))
                    link(dve.scalar_tensor_tensor(out=mstat[:, d, 0, :], in0=v[:, :, M_HD], scalar=-1.0,
                                                  in1=mstat[:, d, 0, :], op0=ALU.mult, op1=ALU.max))
                    link(dve.reciprocal(mstat[:, d, 1, :], mstat[:, d, 0, :]))
                    for t in range(TPR):
                        o = hm[:, r * TPR + t, h * M_HD:(h + 1) * M_HD]
                        rec = mstat[:, d, 1, t:t + 1]
                        if d == 0:
                            ins = dve.tensor_scalar(o, v[:, t, 0:M_HD], rec, None, ALU.mult)
                        else:
                            ins = dve.scalar_tensor_tensor(out=o, in0=v[:, t, 0:M_HD], scalar=rec, in1=o,
                                                           op0=ALU.mult, op1=ALU.add)
                    emptied(ins)
                    wait_emptied(dve, name)

            for b in range(TT):
                softmax_rows(b)
                decays(2 * b)
                weigh(2 * b)
                for n in (0, 2):
                    wait_full(dve, f"pT{b}.{n}")
                    if b >= 1:
                        wait_full(dve, f"pv{b - 1}")
                    emptied(dve.tensor_copy(pTb[:, 4 * n:4 * n + 4, :],
                                            bank(f"pT{b}.{n}").rearrange("p (n t) -> p n t", t=P)))
                st = stat[:, b % 2]
                link(dve.tensor_tensor(st[:, 5, :], st[:, 3, :], st[:, 4, :], ALU.add))
                link(dve.reciprocal(st[:, 6, :], st[:, 5, :]))
                normalise(2 * b)
                decays(2 * b + 1)
                weigh(2 * b + 1)
                wait_full(dve, f"pv{b}")
                o = probs[:, b % 2].rearrange("p h k -> p (h k)")[:, 0:COLS].rearrange("p (h d) -> p h d", h=A_HEADS)
                emptied(dve.tensor_tensor(o, bank(f"pv{b}").rearrange("p (h d) -> p h d", h=A_HEADS),
                                          st[:, 6, :].rearrange("p (h a) -> p h a", a=1).to_broadcast([P, A_HEADS, A_HD]),
                                          ALU.mult))
                normalise(2 * b + 1)

            wait_emptied(dve, "modT11")
            for n in range(2):
                diagonals(4 + n, 5 + n)
                dve.wait_ge(oT_high, n + 1)
                dve.tensor_tensor(o_parts[1][:, 2 * n:2 * n + 2, :], oT[:, 2 * n:2 * n + 2, :],
                                  o_parts[0][:, 2 * n:2 * n + 2, :].bitcast(F32), ALU.subtract
                                  ).then_inc(oT_ready, 1)
            diagonals(6, 8)
            for t in range(TT):
                link(dve.tensor_tensor(tmp[:, :], hm[:, t, :], hm[:, t, :], ALU.mult))
                ins = dve.tensor_reduce(small[:, 8 + 4 * t:12 + 4 * t], tmp[:, :].rearrange("p (h e) -> p h e", h=M_HEADS),
                                        AX.X, ALU.add)
                if t < TT - 1:
                    link(ins)
            ins.then_inc(hm_sq, 1)
            dve.wait_ge(hm_root, 1)
            link(dve.reciprocal(small[:, 8:24], small[:, 24:40]))
            link(dve.tensor_scalar(small[:, 8:24], small[:, 8:24], 0.5, None, ALU.mult))
            wait_emptied(dve, "mo3")
            for t in range(TT):
                v = hm[:, t, :].rearrange("p (h e) -> p h e", h=M_HEADS)
                link(dve.tensor_tensor(v, v, small[:, 8 + 4 * t:12 + 4 * t].rearrange("p (h a) -> p h a", a=1)
                                       .to_broadcast([P, M_HEADS, M_HD]), ALU.mult))
                link(dve.tensor_tensor(hm[:, t, :], hm[:, t, :], hng[:, :], ALU.mult))
                dve.scalar_tensor_tensor(out=hm[:, t, :], in0=og[:, t, :], scalar=1.0, in1=hm[:, t, :],
                                         op0=ALU.add, op1=ALU.mult).then_inc(hm_ready, 1)

            wait_emptied(dve, "bg15")
            for j in range(KD):
                wait_full(dve, f"upa{j}")
                emptied(dve.scalar_tensor_tensor(out=bgate[:, j, :], in0=bgate[:, j, :], scalar=1.0,
                                                 in1=bank(f"upa{j}"), op0=ALU.add, op1=ALU.mult))
            for t in range(TT):
                dve.wait_ge(mT_high, t + 1)
                own = slice(t * P, (t + 1) * P)
                emptied(dve.tensor_tensor(m_parts[1][:, :, own],
                                          bank(f"mT{t}").rearrange("p (k t) -> p k t", k=KM),
                                          m_parts[0][:, :, own].bitcast(F32), ALU.subtract))
            for j in range(KD):
                wait_full(dve, f"upm{j}")
                link(dve.scalar_tensor_tensor(out=bgate[:, KD + j, :], in0=bgate[:, KD + j, :], scalar=1.0,
                                              in1=bank(f"upm{j}"), op0=ALU.add, op1=ALU.mult))
                emptied(dve.tensor_tensor(bgate[:, j, :], bgate[:, j, :], bgate[:, KD + j, :], ALU.add))
            diagonals(8, 10)

            dve.wait_ge(x_again, 16 * REQS)
            wait_emptied(dve, "spread5.1")
            for h in range(2):
                for t in range(TT):
                    name = f"wo{t}.{h}"
                    wait_full(dve, name)
                    xs_ = xbuf[:, t, h * COLS:(h + 1) * COLS]
                    link(dve.tensor_tensor(tmp[:, :], bank(name), g1b[:, t // TPR, h * COLS:(h + 1) * COLS], ALU.mult))
                    emptied(dve.tensor_tensor(xs_, xs_, tmp[:, :], ALU.add))
                    wait_emptied(dve, name)
            wait_emptied(dve, "spread9.1")
            wait_full(dve, "wo3.1")
            for t in range(TT):
                r = t // TPR
                dve.wait_ge(x1_root, t + 1)
                link(dve.reciprocal(small[:, 40 + t:41 + t], small[:, 44 + t:45 + t]))
                link(dve.scalar_tensor_tensor(out=h2[:, t, :], in0=xbuf[:, t, :], scalar=small[:, 40 + t:41 + t],
                                              in1=scale2[:, r, :], op0=ALU.mult, op1=ALU.mult))
                dve.tensor_tensor(h2[:, t, :], h2[:, t, :], shift2[:, r, :], ALU.add).then_inc(h2_ready, 1)
            logits = route[:, 0:80].rearrange("p (t n) -> p t n", t=TT)
            for t in range(TT):
                wait_full(dve, f"logit{t}")
                emptied(dve.tensor_tensor(logits[:, t, :], bank(f"logit{t}", 20), router_b[:, :], ALU.add))
            wait_emptied(dve, "logit3")
            dve.wait_ge(late_landed, 16)

            def three(a, w, n=4):
                return route[:, a:a + w].rearrange("p (t n) -> p t n", n=n)

            def over(ap, n=4):
                return ap.rearrange("p (t a) -> p t a", a=1).to_broadcast([P, TT, n])

            best = small[:, 0:4]
            second = small[:, 4:8]
            grp_p = small[:, 8:12]
            t4 = small[:, 12:16]
            lo = small[:, 16:20]
            iota4 = lc["iota4"].rearrange("p (a n) -> p a n", a=1).to_broadcast([P, TT, 4])
            grp_hot, e_in, hot1, hot2, scr = (three(448, 16), three(464, 16), three(480, 16),
                                              three(496, 16), three(512, 16))

            def first_hot(out, vals, top):
                link(dve.tensor_tensor(out, vals, over(top), ALU.is_equal))
                link(dve.tensor_tensor(out, out, iota4, ALU.mult))
                link(dve.tensor_reduce(lo, out, AX.X, ALU.min))
                link(dve.tensor_tensor(out, iota4, over(lo), ALU.is_equal))

            g_log, e_log = logits[:, :, 0:N_GRP], logits[:, :, N_GRP:20]
            link(dve.tensor_reduce(best, g_log, AX.X, ALU.max))
            first_hot(grp_hot, g_log, best)
            gdiff = three(80, 16)
            link(dve.tensor_tensor(gdiff, g_log, over(best), ALU.subtract))
            prod = route[:, 192:256]
            p4 = prod.rearrange("p (t g k) -> p t g k", t=TT, g=N_GRP)
            by_group = lambda a: a.rearrange("p t (g k) -> p t g k", k=1).to_broadcast([P, TT, N_GRP, PER_GRP])
            link(dve.tensor_tensor(p4, e_log.rearrange("p t (g k) -> p t g k", g=N_GRP), by_group(grp_hot), ALU.mult))
            link(dve.tensor_reduce(e_in, p4.rearrange("p t g k -> p t k g"), AX.X, ALU.add))
            link(dve.tensor_reduce(best, e_in, AX.X, ALU.max))
            first_hot(hot1, e_in, best)
            link(dve.scalar_tensor_tensor(out=scr, in0=hot1, scalar=-BIG, in1=e_in, op0=ALU.mult, op1=ALU.add))
            link(dve.tensor_reduce(second, scr, AX.X, ALU.max))
            first_hot(hot2, scr, second)
            dve.tensor_tensor(route[:, 96:100], second, best, ALU.subtract).then_inc(gate_sum, 1)
            c12 = [hmf[:, n * 64:(n + 1) * 64].rearrange("p (t e) -> p t e", t=TT) for n in range(2)]
            chosen = route[:, 128:192].rearrange("p (t e) -> p t e", t=TT)
            for n, hot in enumerate((hot1, hot2)):
                link(dve.tensor_tensor(c12[n].rearrange("p t (g k) -> p t g k", g=N_GRP), by_group(grp_hot),
                                       hot.rearrange("p t (g k) -> p t g k", g=1)
                                       .to_broadcast([P, TT, N_GRP, PER_GRP]), ALU.mult))
            link(dve.tensor_tensor(chosen, c12[0], c12[1], ALU.add))
            before = chosen_before.rearrange("p (t e) -> p t e", e=N_EXP)
            link(dve.memset(before[:, 0, :], 0.0))
            for t in range(TT):
                ins = dve.tensor_tensor(before[:, t + 1, :], before[:, t, :], chosen[:, t, :], ALU.add)
                if t < TT - 1:
                    link(ins)
            ins.then_inc(onehots_ready, 1)
            dve.wait_ge(gate_exp, 1)
            link(dve.tensor_reduce(t4, gdiff, AX.X, ALU.add))
            link(dve.reciprocal(grp_p, t4))
            link(dve.tensor_scalar(t4, route[:, 96:100], 1.0, None, ALU.add))
            link(dve.reciprocal(lo, t4))
            link(dve.tensor_tensor(topw[:, :, 0], lo, grp_p, ALU.mult))
            link(dve.tensor_tensor(topw[:, :, 1], topw[:, :, 0], route[:, 96:100], ALU.mult))
            wait_full(dve, "rank")
            diagonals(10, 11)

            wait_full(dve, "rank")
            f = hmf[:, 128:]
            rank = f[:, 0:64]
            cnt = f[:, 64:80]
            tiles = f[:, 80:96]
            ends = f[:, 96:112]
            starts = f[:, 112:128]
            div = f[:, 128:192]
            mod = f[:, 192:256]
            link(dve.tensor_copy(rank, bank("rank", 64)))
            emptied(dve.tensor_copy(cnt, bank("rank", 80)[:, 64:80]))
            wait_emptied(dve, "rank")
            link(dve.tensor_scalar(tiles, cnt, float(P), None, ALU.is_gt))
            for j in range(2, TT):
                link(dve.scalar_tensor_tensor(out=tiles, in0=cnt, scalar=float(j * P), in1=tiles,
                                              op0=ALU.is_gt, op1=ALU.add))
            link(dve.tensor_tensor_scan(ends, lc["ones"][:, 0:N_EXP], tiles, 0.0, ALU.mult, ALU.add))
            link(dve.tensor_tensor(starts, ends, tiles, ALU.subtract))
            link(dve.tensor_scalar(ends, ends, float(N_EXP), None, ALU.add))
            more = 2 * MAX_PAIRS - N_EXP
            te = hmf[0:1, 512:512 + more * N_EXP].rearrange("p (s e) -> p s e", e=N_EXP)
            tf = hmf[0:1, 1024:1024 + more]
            link(dve.tensor_tensor(te, ends[0:1, :].rearrange("p (a e) -> p a e", a=1).to_broadcast([1, more, N_EXP]),
                                   lc["iota"][0:1, N_EXP:2 * MAX_PAIRS].rearrange("p (s a) -> p s a", a=1)
                                   .to_broadcast([1, more, N_EXP]), ALU.is_le))
            link(dve.tensor_reduce(tf, te, AX.X, ALU.add))
            link(dve.tensor_copy(tile_expert[:, 0:N_EXP], lc["iota"][0:1, 0:N_EXP]))
            link(dve.tensor_scalar(tile_expert[:, N_EXP:2 * MAX_PAIRS], tf, float(N_EXP - 1), None, ALU.min))
            below = hmf[0:1, 1024:1024 + MAX_PAIRS - 1]
            n_pairs = hmf[0:1, 1100:1101]
            link(dve.scalar_tensor_tensor(out=below, in0=lc["iota"][0:1, 1:MAX_PAIRS], scalar=2.0,
                                          in1=ends[0:1, N_EXP - 1:N_EXP].to_broadcast([1, MAX_PAIRS - 1]),
                                          op0=ALU.mult, op1=ALU.is_lt))
            link(dve.tensor_reduce(n_pairs, below, AX.X, ALU.add))
            dve.tensor_copy(tile_expert[:, 2 * MAX_PAIRS:2 * MAX_PAIRS + 1], n_pairs).then_inc(tiles_ready, 1)
            diagonals(11, 12)
            link(dve.scalar_tensor_tensor(out=starts, in0=starts, scalar=float(N_EXP - 1),
                                          in1=lc["iota"][:, 0:N_EXP], op0=ALU.add, op1=ALU.subtract))
            link(dve.tensor_scalar(div, rank, float(P), None, ALU.is_ge))
            for j in range(2, TT):
                link(dve.scalar_tensor_tensor(out=div, in0=rank, scalar=float(j * P), in1=div,
                                              op0=ALU.is_ge, op1=ALU.add))
            link(dve.scalar_tensor_tensor(out=mod, in0=div, scalar=-float(P), in1=rank, op0=ALU.mult, op1=ALU.add))
            d3 = div.rearrange("p (t e) -> p t e", t=TT)
            m3 = mod.rearrange("p (t e) -> p t e", t=TT)
            over_t = lambda a: a.rearrange("p (a e) -> p a e", a=1).to_broadcast([P, TT, N_EXP])
            beyond = f[:, 336:400].rearrange("p (t e) -> p t e", t=TT)
            link(dve.tensor_scalar(beyond, d3, 1.0, None, ALU.min))
            link(dve.tensor_tensor(d3, d3, over_t(starts), ALU.add))
            link(dve.tensor_tensor(d3, d3, beyond, ALU.mult))
            link(dve.tensor_tensor(d3, d3, over_t(lc["iota"][:, 0:N_EXP]), ALU.add))
            tile_of = f[:, 256:264].rearrange("p (t n) -> p t n", t=TT)
            place_of = f[:, 264:272].rearrange("p (t n) -> p t n", t=TT)
            scratch = f[:, 272:336].rearrange("p (t e) -> p t e", t=TT)
            for n in range(2):
                link(dve.tensor_tensor(scratch, d3, c12[n], ALU.mult))
                link(dve.tensor_reduce(tile_of[:, :, n], scratch, AX.X, ALU.add))
                link(dve.tensor_tensor(scratch, m3, c12[n], ALU.mult))
                link(dve.tensor_reduce(place_of[:, :, n], scratch, AX.X, ALU.add))
            link(dve.scalar_tensor_tensor(out=pos[:, :, :], in0=tile_of, scalar=float(P), in1=place_of,
                                          op0=ALU.mult, op1=ALU.add))
            dve.wait_ge(h2_stored, 16 * TT)
            for t in range(TT):
                for n in range(2):
                    dve.tensor_scalar(hot_place[2 * t + n], lc["iota"], place_of[:, t, n:n + 1], None,
                                      ALU.is_equal).then_inc(hot_slots_ready, 1)
                    dve.tensor_scalar(hot_tile[2 * t + n], lc["iota"][:, 0:2 * MAX_PAIRS], tile_of[:, t, n:n + 1],
                                      lc["tokid"][:, t:t + 1], ALU.is_equal, ALU.mult
                                      ).then_inc(hot_slots_ready, 1)
            wait_full(dve, "ids")
            emptied(dve.tensor_copy(ids[:, :], bank("ids", 2 * MAX_PAIRS)))

            def empty_x():
                dve.tensor_copy(xsT[:, 4:8, :], psum[:, 4, :].rearrange("p (k t) -> p k t", k=4)
                                ).then_inc(xT_dve, 1)

            def split_low(s, q):
                dve.wait_ge(heT_high, s)
                dve.tensor_tensor(heT[1], psum[:, 2, :].rearrange("p (k t) -> p k t", k=KF),
                                  heT[0].bitcast(F32), ALU.subtract).then_inc(heT_ready, 1)
                w = moe_slot[3 * q + 2].rearrange("p (k n) -> p k n", k=KF)
                for j in range(2):
                    dve.wait_ge(down_high, s * 2 + (j - 1))
                    dve.tensor_tensor(down_parts[1][j], w[:, 2 * j:2 * j + 2, :],
                                      down_parts[0][j].bitcast(F32), ALU.subtract).then_inc(down_low, 1)

            def gated(q):
                dve.tensor_tensor(he[:, q, :], sg[:, q, :], psum[:, 1, :], ALU.mult).then_inc(he_ready, 1)

            def empty_y(q):
                dve.tensor_copy(ybuf[:, q, COLS:D], psum[:, 6, :]).then_inc(y_dve, 1)

            dve.wait_ge(xT_full, 1)
            empty_x()
            dve.wait_ge(silu_done, 1)
            dve.wait_ge(up_full, 1)
            gated(0)

            def tile_step(s, q, stored):
                dve.wait_ge(xT_full, s + 1)
                empty_x()
                split_low(s, q)
                dve.wait_ge(silu_done, s + 1)
                dve.wait_ge(up_full, s + 1)
                if stored is not None:
                    dve.wait_ge(heT_full, s - 1)
                gated(q)
                last_row(s, 1 - q, stored)

            def last_row(s, q, stored):
                dve.wait_ge(down_full, s)
                if stored is not None:
                    dve.wait_ge(y_stored[q], stored * 16)
                empty_y(q)

            tile_step(1, 1, None)
            dve.wait_ge(heT_full, 1)
            tile_step(2, 0, None)
            tile_step(3, 1, 1)
            last_pair = load_last_pair(dve)
            with dve.Fori(2, last_pair + 1) as i:
                tile_step(i * 2, 0, i - 1)
                tile_step(i * 2 + 1, 1, i)
            last_row(last_pair * 2 + 2, 1, last_pair)

            def normalise_row(t):
                dve.wait_ge(x2_root, t + 1)
                link(dve.reciprocal(small[:, 48 + t:49 + t], small[:, 52 + t:53 + t]))
                dve.scalar_tensor_tensor(out=xbuf[:, t, :], in0=xbuf[:, t, :], scalar=small[:, 48 + t:49 + t],
                                         in1=fgain, op0=ALU.mult, op1=ALU.mult).then_inc(y_ready, 1)

            dve.wait_ge(fgain_landed, 16)
            for t in range(TT):
                a, b = pair[2 * t], pair[2 * t + 1]
                dve.wait_ge(first_ready, t + 1)
                dve.wait_ge(pair_landed[2 * t + 1], 16)
                link(dve.scalar_tensor_tensor(out=a, in0=b, scalar=topw[:, t, 1:2], in1=a, op0=ALU.mult, op1=ALU.add))
                link(dve.tensor_tensor(a, a, g2b[:, t // TPR, :], ALU.mult))
                dve.tensor_tensor(xbuf[:, t, :], xbuf[:, t, :], a, ALU.add).then_inc(x2_ready, 1)
                if t >= 1:
                    normalise_row(t - 1)
            normalise_row(TT - 1)

        @block.gpsimd
        def _(pool):
            pool.memset(og[:, 0:2, :], 0.0).then_inc(zeros_ready, 1)
            def low_part(piece):
                n = SPLITS.index(piece)
                pool.wait_ge(high_ready, n + 1)
                src = raw_piece(piece).rearrange("p (k n) -> p k n", k=KD)
                high, low = split_piece(piece, KD)
                if piece[0] == "mg":
                    src = raw_piece(piece)[:, 0:KD * 16].rearrange("p (k n) -> p k n", k=KD)
                    for g in range(4):
                        a, b = slice(QUAD * g, QUAD * g + M_HEADS), slice(M_HEADS * g, M_HEADS * (g + 1))
                        ins = pool.tensor_tensor(low[:, :, a], src[:, :, b], high[:, :, a].bitcast(F32),
                                                 ALU.subtract)
                    ins.then_inc(low_ready, 1)
                else:
                    pool.tensor_tensor(low, src, high.bitcast(F32), ALU.subtract).then_inc(low_ready, 1)

            for piece in SPLITS[:SPLITS.index(("upm", 2))]:
                low_part(piece)
                if piece == SPLITS[1]:
                    for k in range(1, KD, 2):
                        pool.wait_ge(h_high_ready, k + 1)
                        pool.tensor_tensor(h_low[:, k, :], hbuf[k % 4], h_high[:, k, :].bitcast(F32),
                                           ALU.subtract).then_inc(h_ready[1], 1)
                if piece == ("upa", 1):
                    wait_full(pool, "oT3")
                    for r in range(REQS):
                        pool.dma_start(xbuf[:, 2 * r:2 * r + 2, :],
                                       x_in[r][0].rearrange("(t p) d -> p t d", p=P)).then_inc(x_again, 16)
                    pool.dma_start(late, late_consts).then_inc(late_landed, 16)
                if piece == ("upa", 3):
                    pool.wait_ge(oT_ready, 2)
                    with nc.allow_non_contiguous_dma(reason="router weights"):
                        pool.dma_start(router_w[:, :, 0:4], rg_w[0].rearrange("(k p) n -> p k n", p=P)
                                       ).then_inc(router_landed, 16)
                        pool.dma_start(router_w[:, :, 4:20], re_w[0].rearrange("(k p) n -> p k n", p=P)
                                       ).then_inc(router_landed, 16)
            rest = SPLITS[SPLITS.index(("upm", 2)):]
            for j in range(4):
                low_part(rest[j])
                for n in (2 * j, 2 * j + 1):
                    pool.wait_ge(merged_high, n + 1)
                    pool.tensor_tensor(merged[1][:, n, :], bgate[:, n, :], merged[0][:, n, :].bitcast(F32),
                                       ALU.subtract).then_inc(merged_ready, 1)
            for piece in rest[4:]:
                low_part(piece)
            for t in range(TT):
                pool.wait_ge(h2_ready, t + 1)
                pool.dma_start(h2_rows[t * P:(t + 1) * P, :], h2[:, t, :]).then_inc(h2_stored, 16)
            wait_emptied(pool, "wo3.1")
            pool.dma_start(fgain, row_bcast(final_norm_g)).then_inc(fgain_landed, 16)

            def gather(q, idx):
                pool.indirect_dma_start(xs[:, q, :], None, h2_rows,
                                        bass.IndirectOffsetOnAxis(ap=idx, axis=0)).then_inc(xs_landed[q], 16)

            pool.wait_ge(h2_stored, 16 * TT)
            wait_emptied(pool, "ids")
            gather(0, ids[:, 0:1])
            gather(1, ids[:, 1:2])
            last_pair = load_last_pair(pool)
            with pool.Fori(1, last_pair + 1) as i:
                for q in range(2):
                    pool.wait_ge(xT_full, i * 2 + (q - 1))
                    pool.tensor_copy(ids_now[:, q:q + 1], ids[:, bass.ds(i * 2 + q, 1)])
                    pool.drain()
                    gather(q, ids_now[:, q:q + 1])

            pool.wait_ge(rows_stored, 1)
            for t in range(TT):
                for n in range(2):
                    pool.indirect_dma_start(pair[2 * t + n], None, y_rows,
                                            bass.IndirectOffsetOnAxis(ap=pos[:, t, n:n + 1], axis=0)
                                            ).then_inc(pair_landed[2 * t + n], 16)


def shape_constants():
    f = np.float32
    i = np.arange(P)
    early = np.zeros((P, EARLY_W), f)
    late = np.zeros((P, LATE_W), f)

    def put(table, where, name, value):
        a, w = table[name]
        where[:, a:a + w] = value

    put(EARLY, early, "ident", np.eye(P, dtype=f))
    lower = np.where(i[None, :] >= i[:, None], 0.0, -BIG)
    upper = np.where(i[None, :] <= i[:, None], 0.0, -BIG)
    put(EARLY, early, "maskL", np.concatenate([lower, np.zeros((P, P))], 1))
    put(EARLY, early, "maskU", np.concatenate([np.zeros((P, P)), upper], 1))
    half = ROPE_DIM // 2
    inv = (f(1.0) / (f(ROPE_THETA) ** (np.arange(half, dtype=f) * f(2.0) / f(ROPE_DIM)))).astype(f)
    ang = (np.arange(SEQ, dtype=f)[None, :] * inv[:, None]).astype(f)
    cos, sin = np.cos(ang).astype(f), np.sin(ang).astype(f)
    ct, st, perm = np.ones((P, SEQ), f), np.zeros((P, SEQ), f), np.zeros((P, P), f)
    for base in range(0, P, A_HD):
        ct[base:base + half], ct[base + half:base + 2 * half] = cos, cos
        st[base:base + half], st[base + half:base + 2 * half] = -sin, sin
        for n in range(half):
            perm[base + half + n, base + n] = 1.0
            perm[base + n, base + half + n] = 1.0
    put(EARLY, early, "cos", ct)
    put(EARLY, early, "sin", st)
    put(EARLY, early, "perm", perm)
    pick = np.zeros((P, REQS), f)
    for r in range(REQS):
        pick[r::QUAD, r] = 1.0
    put(EARLY, early, "pick", pick)
    put(EARLY, early, "one", 1.0)
    put(LATE, late, "tri", (i[:, None] < i[None, :]).astype(f))
    put(LATE, late, "ones", 1.0)
    put(LATE, late, "iota", i[None, :].astype(f))
    put(LATE, late, "iota4", (np.arange(4) - 64.0)[None, :])
    put(LATE, late, "tokid", i[:, None] + P * np.arange(TT)[None, :])
    return {"early_consts": early, "late_consts": late}


INPUTS = ["x_prompt", "x_sample", "c_prompt", "c_sample", "ada_w", "ada_b", "norm1_g", "w_in", "conv_w",
          "m_gate_b", "attn_sink", "head_norm_g", "w_up_attn", "w_up_mlstm", "w_out", "norm2_g", "rg_w",
          "rg_b", "re_w", "re_b", "w_gate", "w_up", "w_down", "final_norm_g"]


def kernel(**inputs):
    import concourse.bacc as bacc
    from concourse.bass_utils import run_bass_kernel_spmd

    nc = bacc.Bacc("TRN2", target_bir_lowering=False, num_devices=1, dynamic_dma_scratch_size=SCRATCH)
    arrays = {name: np.ascontiguousarray(inputs[name]) for name in INPUTS}
    arrays.update(shape_constants())
    args = [nc.dram_tensor(n, a.shape, mybir.dt.from_np(a.dtype), kind="ExternalInput").ap()
            for n, a in arrays.items()]
    for name in ("y_prompt", "y_sample"):
        args.append(nc.dram_tensor(name, (1, SEQ, D), F32, kind="ExternalOutput").ap())
    hybrid_layer(nc, *args)
    r = run_bass_kernel_spmd(nc, [arrays], core_ids=[0])
    return r.results[0]["y_prompt"], r.results[0]["y_sample"]
```
